# Optimizing a Trainium2 kernel written in Bass

```python
import jax, jax.numpy as jnp
from jax import lax
import numpy as np

D_MODEL = 1024
BATCH = 1
SEQ = 1024
DEPTH = 2

GRID_W = 64
CTX_LEN = 256
EPS = 1e-6

F_GROUPS = 4
F_GDIM = 64
F_WIDTH = F_GROUPS * F_GDIM
NA_HEADS = 8
HEAD_DIM = 64
NA_WIDTH = NA_HEADS * HEAD_DIM
NA_WIN_R = 8
NA_WIN_C = 16
ATTN_SCALE = HEAD_DIM ** -0.5
ROPE_BASE = 10000.0
ROPE_HALF = HEAD_DIM // 2
ROPE_PER_AXIS = HEAD_DIM // 4
CONV_WIDTH = 256
CONV_K = 3
N_BRANCH = 3
COL_F = 0
COL_Q = COL_F + F_WIDTH
COL_K = COL_Q + NA_WIDTH
COL_V = COL_K + NA_WIDTH
COL_CX = COL_V + NA_WIDTH
COL_CB = COL_CX + CONV_WIDTH
COL_CC = COL_CB + CONV_WIDTH
COL_G = COL_CC + CONV_WIDTH
IN_WIDTH = COL_G + N_BRANCH * D_MODEL
N_EXPERTS = 16
N_GROUPS = 4
EXPERTS_PER_GROUP = N_EXPERTS // N_GROUPS
TOPK_GROUPS = 1
TOP_K = 2
D_EXPERT = 512
MOE_BLOCK = 128

kernel_name = 'hybrid_fourier_na_conv_grouped_moe_dit'

def rmsnorm(x, g):
    xf = x.astype(jnp.float32)
    y = xf * lax.rsqrt(jnp.mean(xf * xf, axis=-1, keepdims=True) + EPS)
    return (y * g.astype(jnp.float32)).astype(x.dtype)

def modulate(h, shift, scale):
    return h * (1.0 + scale) + shift

def axial_rope_tables(L, dtype):
    t = jnp.arange(L)
    row = (t // GRID_W).astype(jnp.float32)
    col = (t % GRID_W).astype(jnp.float32)
    inv = jnp.power(ROPE_BASE, -jnp.arange(ROPE_PER_AXIS, dtype=jnp.float32) / ROPE_PER_AXIS)
    ang = jnp.concatenate([row[:, None] * inv, col[:, None] * inv], axis=-1)
    return jnp.cos(ang)[:, None, :].astype(dtype), jnp.sin(ang)[:, None, :].astype(dtype)

def apply_rope(x, cos, sin):
    x1, x2 = x[..., :ROPE_HALF], x[..., ROPE_HALF:]
    return jnp.concatenate([x1 * cos - x2 * sin, x2 * cos + x1 * sin], axis=-1)

def q_heads(pq, qn_g):
    bsz, L, _ = pq.shape
    return rmsnorm(pq.reshape(bsz, L, NA_HEADS, HEAD_DIM), qn_g)

def kv_heads(pkv, kn_g):
    bsz, L, _ = pkv.shape
    k = rmsnorm(pkv[..., :NA_WIDTH].reshape(bsz, L, NA_HEADS, HEAD_DIM), kn_g)
    v = pkv[..., NA_WIDTH:].reshape(bsz, L, NA_HEADS, HEAD_DIM)
    return k, v

def fourier_mix(u):
    bsz, L, _ = u.shape
    ug = u.reshape(bsz, L, F_GROUPS, F_GDIM).astype(jnp.float32)
    f = jnp.fft.fft2(ug, axes=(1, 3), norm='ortho').real
    return f.reshape(bsz, L, F_WIDTH).astype(u.dtype)

def short_conv(xc, bg, cg, conv_w):
    u = cg * xc
    up = jnp.pad(u, ((0, 0), (1, 1), (0, 0)))
    y = conv_w[0] * up[:, :-2] + conv_w[1] * up[:, 1:-1] + conv_w[2] * up[:, 2:]
    return bg * y

def context_attention(q, k, v):
    bsz, L = q.shape[:2]
    s = jnp.einsum('bqhd,bkhd->bhqk', q, k).astype(jnp.float32) * ATTN_SCALE
    p = jax.nn.softmax(s, axis=-1).astype(v.dtype)
    return jnp.einsum('bhqk,bkhd->bqhd', p, v).reshape(bsz, L, NA_WIDTH)

def neighbourhood_attention(q, k, v, k_ctx, v_ctx, rpb):
    bsz, L, H, Dh = q.shape
    rows = L // GRID_W
    wr = min(NA_WIN_R, rows)
    qg = q.reshape(bsz, rows, GRID_W, H, Dh)
    kg = k.reshape(bsz, rows, GRID_W, H, Dh)
    vg = v.reshape(bsz, rows, GRID_W, H, Dh)
    r = jnp.arange(rows)
    row_start = jnp.clip(r - wr // 2, 0, rows - wr)
    row_idx = row_start[:, None] + jnp.arange(wr)[None, :]
    kb = kg[:, row_idx]
    vb = vg[:, row_idx]
    col = jnp.arange(GRID_W)
    col_start = jnp.clip(col - NA_WIN_C // 2, 0, GRID_W - NA_WIN_C)
    col_mask = (col[None, :] >= col_start[:, None]) & (col[None, :] < col_start[:, None] + NA_WIN_C)
    dr = row_idx - r[:, None] + (NA_WIN_R - 1)
    dc = jnp.clip(col[None, :] - col[:, None] + (NA_WIN_C - 1), 0, 2 * NA_WIN_C - 2)
    bias = rpb[:, dr][:, :, :, dc].transpose(1, 3, 0, 2, 4)
    s_loc = jnp.einsum('brqhd,brkwhd->brqhkw', qg, kb).astype(jnp.float32) * ATTN_SCALE
    s_loc = s_loc + bias.astype(jnp.float32)
    s_loc = jnp.where(col_mask[:, None, None, :], s_loc, -jnp.inf)
    s_ctx = jnp.einsum('brqhd,bkhd->brqhk', qg, k_ctx).astype(jnp.float32) * ATTN_SCALE
    n_loc = wr * GRID_W
    s = jnp.concatenate([s_loc.reshape(bsz, rows, GRID_W, H, n_loc), s_ctx], axis=-1)
    p = jax.nn.softmax(s, axis=-1).astype(v.dtype)
    p_loc = p[..., :n_loc].reshape(bsz, rows, GRID_W, H, wr, GRID_W)
    p_ctx = p[..., n_loc:]
    out = (jnp.einsum('brqhkw,brkwhd->brqhd', p_loc, vb)
           + jnp.einsum('brqhk,bkhd->brqhd', p_ctx, v_ctx))
    return out.reshape(bsz, L, NA_WIDTH)

def merge_branches(P, attn, w_f, w_na, w_cv, conv_w, w_o):
    f = fourier_mix(P[..., COL_F:COL_Q])
    y_cv = short_conv(P[..., COL_CX:COL_CB], P[..., COL_CB:COL_CC], P[..., COL_CC:COL_G], conv_w)
    g = jax.nn.sigmoid(P[..., COL_G:])
    g_f = g[..., :D_MODEL]
    g_na = g[..., D_MODEL:2 * D_MODEL]
    g_cv = g[..., 2 * D_MODEL:]
    merged = g_f * (f @ w_f) + g_na * (attn @ w_na) + g_cv * (y_cv @ w_cv)
    return merged @ w_o

def route(h, router_w, router_b):
    n = h.shape[0]
    s = jax.nn.sigmoid((h @ router_w).astype(jnp.float32))
    sb = s + router_b.astype(jnp.float32)
    gscore = lax.top_k(sb.reshape(n, N_GROUPS, EXPERTS_PER_GROUP), 2)[0].sum(-1)
    _, gidx = lax.top_k(gscore, TOPK_GROUPS)
    gmask = jnp.any(gidx[..., None] == jnp.arange(N_GROUPS), axis=1)
    emask = jnp.repeat(gmask, EXPERTS_PER_GROUP, axis=-1)
    _, eidx = lax.top_k(jnp.where(emask, sb, -jnp.inf), TOP_K)
    w = jnp.take_along_axis(s, eidx, axis=-1)
    w = w / jnp.sum(w, axis=-1, keepdims=True)
    return eidx, w

def moe_ffn(h, router_w, router_b, w1, w3, w2):
    n, d = h.shape
    eidx, wts = route(h, router_w, router_b)
    a = n * TOP_K
    flat_e = eidx.reshape(a)
    flat_t = jnp.repeat(jnp.arange(n, dtype=jnp.int32), TOP_K)
    flat_w = wts.reshape(a)
    order = jnp.argsort(flat_e)
    e_s, t_s, w_s = flat_e[order], flat_t[order], flat_w[order]
    counts = jnp.bincount(flat_e, length=N_EXPERTS)
    starts = jnp.cumsum(counts) - counts
    padded = (counts + MOE_BLOCK - 1) // MOE_BLOCK * MOE_BLOCK
    pends = jnp.cumsum(padded)
    pstarts = pends - padded
    dest = pstarts[e_s] + (jnp.arange(a) - starts[e_s])
    n_blk = (a + N_EXPERTS * (MOE_BLOCK - 1) + MOE_BLOCK - 1) // MOE_BLOCK
    p_len = n_blk * MOE_BLOCK
    tok_buf = jnp.full((p_len,), n, dtype=jnp.int32).at[dest].set(t_s)
    w_buf = jnp.zeros((p_len,), h.dtype).at[dest].set(w_s.astype(h.dtype))
    blk_e = jnp.minimum(jnp.searchsorted(pends, jnp.arange(n_blk) * MOE_BLOCK, side='right'), N_EXPERTS - 1)
    h_pad = jnp.concatenate([h, jnp.zeros((1, d), h.dtype)], axis=0)
    xb = h_pad[tok_buf].reshape(n_blk, MOE_BLOCK, d)

    def expert_block(args):
        xblk, e = args
        return (jax.nn.silu(xblk @ w1[e]) * (xblk @ w3[e])) @ w2[e]

    yb = lax.map(expert_block, (xb, blk_e)).reshape(p_len, d)
    out = jnp.zeros((n + 1, d), h.dtype).at[tok_buf].add(yb * w_buf[:, None])
    return out[:n]

def setup_inputs(seed: int = 0) -> dict:
    key = jax.random.key(seed)
    ks = jax.random.split(key, 24)
    D = D_MODEL

    def nrm(k, shape, scale):
        return jax.random.normal(k, shape, jnp.float32) * scale

    return {
        'x': nrm(ks[0], (BATCH, SEQ, D), 1.0),
        'c': nrm(ks[1], (BATCH, D), 1.0),
        'ctx': nrm(ks[2], (BATCH, CTX_LEN, D), 1.0),
        'c_ctx': nrm(ks[3], (D,), 1.0),
        'ada_w': nrm(ks[4], (DEPTH, D, 6 * D), 0.5 * D ** -0.5),
        'ada_b': nrm(ks[5], (DEPTH, 6 * D), 0.02),
        'norm1_g': 1.0 + nrm(ks[6], (DEPTH, D), 0.05),
        'w_in': nrm(ks[7], (DEPTH, D, IN_WIDTH), D ** -0.5),
        'qn_g': 1.0 + nrm(ks[8], (DEPTH, HEAD_DIM), 0.05),
        'kn_g': 1.0 + nrm(ks[9], (DEPTH, HEAD_DIM), 0.05),
        'rpb': nrm(ks[10], (DEPTH, NA_HEADS, 2 * NA_WIN_R - 1, 2 * NA_WIN_C - 1), 0.2),
        'conv_w': nrm(ks[11], (DEPTH, CONV_K, CONV_WIDTH), CONV_K ** -0.5),
        'w_f': nrm(ks[12], (DEPTH, F_WIDTH, D), F_WIDTH ** -0.5),
        'w_na': nrm(ks[13], (DEPTH, NA_WIDTH, D), NA_WIDTH ** -0.5),
        'w_cv': nrm(ks[14], (DEPTH, CONV_WIDTH, D), CONV_WIDTH ** -0.5),
        'w_o': nrm(ks[15], (DEPTH, D, D), D ** -0.5),
        'norm2_g': 1.0 + nrm(ks[16], (DEPTH, D), 0.05),
        'router_w': nrm(ks[17], (D, N_EXPERTS), D ** -0.5),
        'router_b': nrm(ks[18], (N_EXPERTS,), 0.01),
        'w1': nrm(ks[19], (DEPTH, N_EXPERTS, D, D_EXPERT), D ** -0.5),
        'w3': nrm(ks[20], (DEPTH, N_EXPERTS, D, D_EXPERT), D ** -0.5),
        'w2': nrm(ks[21], (DEPTH, N_EXPERTS, D_EXPERT, D), D_EXPERT ** -0.5),
    }

def reference(x, c, ctx, c_ctx, ada_w, ada_b, norm1_g, w_in, qn_g, kn_g, rpb, conv_w, w_f, w_na, w_cv, w_o,
              norm2_g, router_w, router_b, w1, w3, w2):
    bsz, L, d = x.shape
    cos, sin = axial_rope_tables(L, x.dtype)
    sc = jax.nn.silu(c)
    scc = jax.nn.silu(c_ctx)
    for l in range(DEPTH):
        last = l == DEPTH - 1
        mod = (sc @ ada_w[l] + ada_b[l])[:, None, :]
        mod_c = scc @ ada_w[l] + ada_b[l]
        sh1, sc1, g1, sh2, sc2, g2 = jnp.split(mod, 6, axis=-1)
        csh1, csc1, cg1, csh2, csc2, cg2 = jnp.split(mod_c, 6, axis=-1)

        hc = modulate(rmsnorm(ctx, norm1_g[l]), csh1, csc1)
        if last:
            k_c, v_c = kv_heads(hc @ w_in[l][:, COL_K:COL_CX], kn_g[l])
        else:
            Pc = hc @ w_in[l]
            q_c = q_heads(Pc[..., COL_Q:COL_K], qn_g[l])
            k_c, v_c = kv_heads(Pc[..., COL_K:COL_CX], kn_g[l])
            attn_c = context_attention(q_c, k_c, v_c)
            ctx_new = ctx + cg1 * merge_branches(Pc, attn_c, w_f[l], w_na[l], w_cv[l], conv_w[l], w_o[l])

        h = modulate(rmsnorm(x, norm1_g[l]), sh1, sc1)
        P = h @ w_in[l]
        q = apply_rope(q_heads(P[..., COL_Q:COL_K], qn_g[l]), cos, sin)
        k, v = kv_heads(P[..., COL_K:COL_CX], kn_g[l])
        k = apply_rope(k, cos, sin)
        attn = neighbourhood_attention(q, k, v, k_c, v_c, rpb[l])
        x = x + g1 * merge_branches(P, attn, w_f[l], w_na[l], w_cv[l], conv_w[l], w_o[l])

        h2 = modulate(rmsnorm(x, norm2_g[l]), sh2, sc2).reshape(bsz * L, d)
        if last:
            y = moe_ffn(h2, router_w, router_b, w1[l], w3[l], w2[l])
            x = x + g2 * y.reshape(bsz, L, d)
        else:
            h2c = modulate(rmsnorm(ctx_new, norm2_g[l]), csh2, csc2).reshape(bsz * CTX_LEN, d)
            y = moe_ffn(jnp.concatenate([h2, h2c], axis=0), router_w, router_b, w1[l], w3[l], w2[l])
            x = x + g2 * y[:bsz * L].reshape(bsz, L, d)
            ctx = ctx_new + cg2 * y[bsz * L:].reshape(bsz, CTX_LEN, d)
    return x


_drawn_inputs = setup_inputs


def setup_inputs(seed=0):
    import zlib

    import numpy as np

    out = dict(_drawn_inputs(seed))
    spreads = {}
    factors = {'qn_g': 5.909, 'kn_g': 5.512, 'rpb': 6.499}
    for name, (base, spread) in spreads.items():
        noise = np.random.default_rng([zlib.crc32(name.encode()), seed]).standard_normal(out[name].shape)
        drawn = base * np.exp(spread * noise) if base else spread * noise
        out[name] = __import__('jax').numpy.asarray(drawn.astype(out[name].dtype))
    for name, factor in factors.items():
        out[name] = (out[name] * factor).astype(out[name].dtype)
    return out
```

```python
import concourse.bass as bass
from concourse import mybir
from contextlib import ExitStack
import numpy as np

F32 = mybir.dt.float32
I32 = mybir.dt.int32
ALU = mybir.AluOpType
ACT = mybir.ActivationFunctionType
AX = mybir.AxisListType

P = 128
D = 1024
DEPTH = 2
SEQ = 1024
CTX = 256
GRID_W = 64
ROWS = SEQ // GRID_W
EPS = 1e-6
KD = D // P
NTX = SEQ // P
NT = (SEQ + CTX) // P
TOK = SEQ + CTX
F_WIDTH = 256
HEADS = 8
HD = 64
NAW = HEADS * HD
PAIRS = HEADS // 2
WIN_R = 8
WIN_C = 16
RPB_R = 2 * WIN_R - 1
RPB_PAD = 128
CONV = 256
KS = (0, 256, 768, 1280, 1792, 2560)
EXP = 16
GROUPS = 4
DE = 512
NEG = -1e30

V_C = 0
V_ADAB = V_C + 2 * KD
V_N1 = V_ADAB + DEPTH * 48
V_CONV = V_N1 + DEPTH * KD
V_QG = V_CONV + DEPTH * 6
V_RB = V_QG + DEPTH * 4 * HD
V_TOTAL = V_RB + EXP
C_ID = 0
C_TRI = C_ID + P
C_MASK = C_TRI + P
C_DFT = C_MASK + GRID_W
C_DCTX = C_DFT + 4 * P
C_THR = C_DCTX + 4 * CTX
C_BLK = C_THR + NT
C_DESC = C_BLK + 48
C_TOTAL = C_DESC + EXP

A_X = 0
A_H = A_X + NT * D
A_ATT = A_H + NT * D
A_FT = A_ATT + 4 * TOK
A_YC = A_FT + 2 * TOK
A_R = A_YC + 2 * TOK
ARENA = 51200


class Count:

    def __init__(self, sem, base=0):
        self.sem, self.base, self.n = sem, base, 0

    def up(self, instruction, by=1):
        instruction.then_inc(self.sem, by)
        self.n += by
        return instruction

    def now(self):
        return self.base + self.n


def hybrid_backbone(nc, a, out):
    with ExitStack() as es:
        def sb(name, shape, dt=F32):
            return es.enter_context(nc.sbuf_tensor(name, shape, dt))

        banks = [es.enter_context(nc.psum_tensor(f"bank{i}", [P, 512], F32)) for i in range(8)]
        arena = sb("arena", [P, ARENA])
        vec = sb("vec", [P, V_TOTAL])
        mod = sb("mod", [P, DEPTH, 48, 2])
        scale1 = sb("scale1", [P, KD, 2])
        eps_col = sb("eps_col", [P, 1])
        ident = sb("ident", [P, P])
        state = dict(
            nc=nc, a=a, out=out, banks=banks, arena=arena, vec=vec, mod=mod, scale1=scale1, ident=ident, eps=eps_col,
            slots=nc.dram_tensor("slots", [MAX_SLOTS, D], F32).ap(),
            q_rows=nc.dram_tensor("q_rows", [TOK, NAW], F32).ap(),
            k_rows=nc.dram_tensor("k_rows", [TOK, NAW], F32).ap(),
            v_rows=nc.dram_tensor("v_rows", [TOK, NAW], F32).ap(),
            dest=sb("dest", [P, 2, NT], I32), wts=sb("wts", [P, 2, NT]),
            block_expert=sb("block_expert", [1, 64], I32),
        )

        first_sem = min(nc.free_semaphores)
        sets = [range(first_sem + i * STAGE_SEMS, first_sem + (i + 1) * STAGE_SEMS) for i in range(2)]
        names = {"stage": 0, "used": 0, "pool": 0}

        def sem(name):
            n = names["used"]
            names["used"] += 1
            assert n < STAGE_SEMS
            return stage_semaphores.enter_context(
                nc.semaphore(f"{name}_{names['stage']}", num=sets[names["stage"] % 2][n]))

        def pool_dma_sem(name):
            names["pool"] += 1
            return es.enter_context(nc.semaphore(f"{name}_{names['stage']}", num=sets[1][-1] + names["pool"]))

        def clear_last(sp):
            if names["stage"]:
                sp.sem_clear(sets[(names["stage"] + 1) % 2])

        def place(at, *dims):
            n = int(np.prod(dims))
            assert at + n <= ARENA
            flat = arena[:, at:at + n]
            if len(dims) == 1:
                return flat
            if len(dims) == 2:
                return flat.rearrange("p (a b) -> p a b", b=dims[1])
            return flat.rearrange("p (a b c) -> p a b c", b=dims[1], c=dims[2])

        state["sem"], state["place"], state["clear_last"] = sem, place, clear_last
        state["pool_dma_sem"] = pool_dma_sem
        stages = [(load_and_modulations, ())]
        for layer in range(DEPTH):
            last = layer == DEPTH - 1
            stages += [(norm_for_mixers, (layer,))]
            stages += [(f, (layer, last)) for f in (project_rows, conv_branch, fourier_branch, attention,
                                                    gates_and_merge, mixer_output, norm_and_route, experts, combine)]
        for n, (stage, args) in enumerate(stages[:STAGES]):
            names.update(stage=n, used=0)
            with ExitStack() as stage_semaphores:
                stage(state, *args)


STAGE_SEMS = 32
STAGES = 99
MAX_SLOTS = 36 * P


def apart(eng, passed):
    eng.sem_inc(passed, 1)


def load_and_modulations(s):
    nc, sem, place, vec, mod, banks = s["nc"], s["sem"], s["place"], s["vec"], s["mod"], s["banks"]
    X = place(A_X, NT, D)
    CH = 12
    wbuf = [place(A_H + i * 4096, KD, 512) for i in range(2)]
    silu = place(A_R, KD, 2)
    zeros = place(A_R + 64, D)
    ada = s["a"]["ada_w"]
    s_small, s_x, s_silu = sem("small_loaded"), sem("x_loaded"), sem("silu_done")
    s_w = [sem("ada_w_loaded_even"), sem("ada_w_loaded_odd")]
    s_ps, s_psfree, s_out = sem("mod_product"), sem("mod_bank_free"), sem("mod_done")
    s_zero, s_fill = sem("zeros"), sem("slots_filled")
    with nc.Block() as block:
        @block.sync
        def _(sp):
            s["clear_last"](sp)
            sp.dma_start(vec[:], s["a"]["vectors"]).then_inc(s_small, 16)
            sp.dma_start(s["ident"][:], s["a"]["consts"][:, C_ID:C_ID + P]).then_inc(s_small, 16)
            for layer in range(DEPTH):
                with sp.Fori(0, CH - 1, 2) as i:
                    for b in range(2):
                        sp.wait_ge(s_ps, i + layer * CH + b + 1)
                        sp.dma_start(wbuf[b], ada[layer, bass.ds(i + b, 1)]
                                     .rearrange("o p k n -> p (o k) n")).then_inc(s_w[b], 16)

        @block.scalar
        def _(act):
            act.dma_start(X[:, 0:NTX], s["a"]["x"][0].rearrange("(t p) d -> p t d", p=P)).then_inc(s_x, 16)
            act.dma_start(X[:, NTX:NT], s["a"]["ctx"][0].rearrange("(t p) d -> p t d", p=P)).then_inc(s_x, 16)
            act.wait_ge(s_small, 32)
            act.activation(silu, vec[:, V_C:V_C + 2 * KD].rearrange("p (k w) -> p k w", w=2),
                           ACT.Silu).then_inc(s_silu, 1)
            act.wait_ge(s_zero, 1)
            n = MAX_SLOTS // P
            for r in range(n):
                act.dma_start(s["slots"][r * P:(r + 1) * P], zeros).then_inc(s_fill, 16)
            act.wait_ge(s_fill, 16 * n)
            act.wait_ge(s_x, 32)

        @block.gpsimd
        def _(pool):
            pool.memset(zeros, 0.0).then_inc(s_zero, 1)

        @block.tensor
        def _(pe):
            pe.sem_inc(s_ps, 2)
            pe.wait_ge(s_silu, 1)
            for layer in range(DEPTH):
                with pe.Fori(0, CH - 1, 2) as i:
                    for b in range(2):
                        pe.wait_ge(s_w[b], i * 8 + layer * CH * 8 + 16)
                        pe.wait_ge(s_psfree, i + layer * CH + b + 1)
                        for t in range(4):
                            for k in range(KD):
                                mm = pe.matmul(banks[b][:, 2 * t:2 * t + 2], wbuf[b][:, k, t * P:(t + 1) * P],
                                               silu[:, k, :], start=k == 0, stop=k == KD - 1)
                        mm.then_inc(s_ps, 1)

        @block.vector
        def _(dve):
            dve.memset(s["eps"][:], EPS).then_inc(s_out, 1)
            dve.sem_inc(s_psfree, 2)
            dve.wait_ge(s_small, 32)
            for layer in range(DEPTH):
                bias = vec[:, V_ADAB + layer * 48:V_ADAB + (layer + 1) * 48]
                with dve.Fori(0, CH - 1, 2) as i:
                    for b in range(2):
                        dve.wait_ge(s_ps, i + layer * CH + b + 3)
                        dve.tensor_copy(mod[:, layer, bass.ds(i * 4 + b * 4, 4), :],
                                        banks[b][:, 0:8].rearrange("p (t w) -> p t w", w=2)).then_inc(s_psfree, 1)
                dve.wait_ge(s_psfree, 2 + CH * (layer + 1))
                dve.tensor_tensor(mod[:, layer], mod[:, layer],
                                  bias.unsqueeze(2).broadcast_to([P, 48, 2]), ALU.add).then_inc(s_out, 1)
            dve.wait_ge(s_out, 1 + DEPTH)


def norm_for_mixers(s, layer):
    nc, sem, place, vec, mod, banks = s["nc"], s["sem"], s["place"], s["vec"], s["mod"], s["banks"]
    X, HT = place(A_X, NT, D), place(A_H, KD, TOK)
    xn = [place(A_R + i * 4 * D, 4, D) for i in range(2)]
    junk = place(A_R + 8 * D, D)
    sq = place(A_R + 9 * D, NT)
    root = place(A_R + 9 * D + 16, NT)
    rstd = place(A_R + 9 * D + 32, NT)
    scale1 = s["scale1"]
    groups = [(0, 4, 0), (4, 8, 0), (8, 10, 1)]
    s_sq, s_root, s_rstd, s_sc = sem("squares"), sem("root"), sem("rstd"), sem("scale1_done")
    s_xn, s_turn, s_evac = sem("rows_scaled"), sem("turned"), sem("turned_copied")
    with nc.Block() as block:
        @block.sync
        def _(sp):
            s["clear_last"](sp)

        @block.scalar
        def _(act):
            for t in range(NT):
                if t:
                    act.wait_ge(s_sq, t)
                act.activation(junk, X[:, t], ACT.Square, accum_out=sq[:, t:t + 1]).then_inc(s_sq, 1)
            act.wait_ge(s_sq, NT)
            act.activation(root, sq, ACT.Sqrt, bias=s["eps"][:, 0:1], scale=1.0 / D).then_inc(s_root, 1)
            act.wait_ge(s_sc, 2)
            n = 0
            for g, (t0, t1, w) in enumerate(groups):
                for k in range(KD):
                    n += 1
                    if k % 2:
                        act.wait_ge(s_turn, n)
                        act.activation(HT[:, k, t0 * P:t1 * P], banks[(n - 1) % 8][:, 0:(t1 - t0) * P], ACT.Identity,
                                       bias=mod[:, layer, k, w:w + 1],
                                       scale=scale1[:, k, w:w + 1]).then_inc(s_evac, 1)
            act.wait_ge(s_evac, 12)

        @block.vector
        def _(dve):
            gain = vec[:, V_N1 + layer * KD:V_N1 + (layer + 1) * KD]
            dve.tensor_scalar(scale1[:], mod[:, layer, KD:2 * KD, :], 1.0, None, ALU.add).then_inc(s_sc, 1)
            dve.wait_ge(s_sc, 1)
            dve.tensor_tensor(scale1[:], scale1[:], gain.unsqueeze(2).broadcast_to([P, KD, 2]),
                              ALU.mult).then_inc(s_sc, 1)
            dve.wait_ge(s_root, 1)
            dve.reciprocal(rstd, root).then_inc(s_rstd, 1)
            dve.wait_ge(s_rstd, 1)
            dve.wait_ge(s_sc, 2)
            for t in range(4):
                dve.tensor_scalar(xn[0][:, t], X[:, t], rstd[:, t:t + 1], None, ALU.mult).then_inc(s_xn, 1)
            n = 0
            for g, (t0, t1, w) in enumerate(groups):
                if g + 1 < len(groups):
                    if g >= 1:
                        dve.wait_ge(s_turn, 8 * g)
                    for t in range(groups[g + 1][0], groups[g + 1][1]):
                        dve.tensor_scalar(xn[(g + 1) % 2][:, t % 4], X[:, t], rstd[:, t:t + 1], None,
                                          ALU.mult).then_inc(s_xn, 1)
                for k in range(KD):
                    n += 1
                    if k % 2 == 0:
                        dve.wait_ge(s_turn, n)
                        dve.tensor_scalar(HT[:, k, t0 * P:t1 * P], banks[(n - 1) % 8][:, 0:(t1 - t0) * P],
                                          scale1[:, k, w:w + 1], mod[:, layer, k, w:w + 1],
                                          ALU.mult, ALU.add).then_inc(s_sc, 1)
            dve.wait_ge(s_sc, 14)

        @block.tensor
        def _(pe):
            for g, (t0, t1, w) in enumerate(groups):
                pe.wait_ge(s_xn, t1)
                for k in range(KD):
                    if g:
                        if k % 2:
                            pe.wait_ge(s_evac, 4 * (g - 1) + k // 2 + 1)
                        else:
                            pe.wait_ge(s_sc, 2 + 4 * (g - 1) + k // 2 + 1)
                    for t in range(t0, t1):
                        mm = pe.transpose(banks[k][:, (t - t0) * P:(t - t0 + 1) * P],
                                          xn[g % 2][:, t % 4, k * P:(k + 1) * P], s["ident"][:])
                    mm.then_inc(s_turn, 1)


def project_rows(s, layer, last):
    nc, sem, place, vec, banks = s["nc"], s["sem"], s["place"], s["vec"], s["banks"]
    HT, U = place(A_H, KD, TOK), place(A_R, NT, F_WIDTH)
    at = A_R + NT * F_WIDTH
    wb = [place(at + i * 4096, KD, 512) for i in range(2)]
    at += 8192
    trig = place(at, 2, NTX, HD)
    tabs = place(at + 1024, 4, NTX, HD)
    gq = place(at + 3072, HD)
    at += 3136
    sqb = [place(at + i * 512, 512) for i in range(2)]
    xr = [place(at + 1024 + i * 512, 512) for i in range(2)]
    rot = [place(at + 2048 + i * 512, 512) for i in range(2)]
    res = [place(at + 3072 + i * 512, 512) for i in range(4)]
    ssum = place(at + 5120, 2, HEADS)
    root = place(at + 5136, 2, HEADS)
    rinv = place(at + 5152, 2, HEADS)
    chunks = []
    for c in range(4):
        chunks.append((c, list(range(NTX if last and c < 2 else NT))))
    work = [(c, t) for c, ts in chunks for t in ts]
    normed = [n for n, (c, t) in enumerate(work) if c in (1, 2)]
    s_w = [sem(f"w_in_{'FQKV'[c]}_loaded") for c in range(4)]
    s_trig, s_tab, s_mm = sem("trig_loaded"), sem("tables"), sem("row_product")
    s_free = sem("row_bank_free")
    s_sq, s_ss, s_rt, s_ri, s_xr = sem("q_squared"), sem("q_sums"), sem("q_root"), sem("q_rinv"), sem("q_scaled")
    s_rot, s_res, s_vc = sem("q_rot"), sem("qk_rows"), sem("v_rows")
    s_st = [sem(f"stored_{i}") for i in range(4)]
    s_sin = sem("q_sin")
    vwork = [n for n, (c, t) in enumerate(work) if c == 3]
    RQ = V_QG + layer * 4 * HD

    with nc.Block() as block:
        @block.sync
        def _(sp):
            s["clear_last"](sp)
            w = s["a"]["w_rows"]
            sp.dma_start(trig, s["a"]["trig"]).then_inc(s_trig, 16)

            def load(c):
                if c >= 2:
                    sp.wait_ge(s_mm, sum(len(ts) for _, ts in chunks[:c - 1]))
                n = 256 if c == 0 else 512
                sp.dma_start(wb[c % 2][:, :, 0:n],
                             w[layer, :, KS[c] * KD:KS[c] * KD + n * KD].rearrange("p (k n) -> p k n", k=KD)).then_inc(s_w[c], 16)

            for c in range(3):
                load(c)
            for m, n in enumerate(normed):
                if n == sum(len(ts) for _, ts in chunks[:2]):
                    load(3)
                sp.wait_ge(s_res, m + 1)
                c, t = work[n]
                sp.dma_start(s["q_rows" if c == 1 else "k_rows"][t * P:(t + 1) * P], res[m % 4])\
                    .then_inc(s_st[m % 4], 16)
            for m, n in enumerate(vwork):
                sp.wait_ge(s_vc, m + 1)
                sp.dma_start(s["v_rows"][work[n][1] * P:(work[n][1] + 1) * P], res[m % 4]).then_inc(s_st[m % 4], 16)
            for q in range(4):
                sp.wait_ge(s_st[q], 16 * (len(range(q, len(normed), 4)) + len(range(q, len(vwork), 4))))

        @block.tensor
        def _(pe):
            for n, (c, t) in enumerate(work):
                if t == 0:
                    pe.wait_ge(s_w[c], 16)
                if n >= 6:
                    was = work[n - 6][0]
                    done = sum(1 for k, _ in work[:n - 5] if k == was or {k, was} == {1, 2})
                    pe.wait_ge({0: s_free, 1: s_xr, 2: s_xr, 3: s_vc}[was], done)
                w = 256 if c == 0 else 512
                for k in range(KD):
                    mm = pe.matmul(banks[n % 6][:, 0:w], HT[:, k, t * P:(t + 1) * P], wb[c % 2][:, k, 0:w],
                                   start=k == 0, stop=k == KD - 1)
                mm.then_inc(s_mm, 1)

        @block.scalar
        def _(act):
            nq = nv = 0
            for n, (c, t) in enumerate(work):
                act.wait_ge(s_mm, n + 1)
                if c == 0:
                    act.activation(U[:, t], banks[n % 6][:, 0:256], ACT.Copy).then_inc(s_free, 1)
                elif c == 3:
                    m = nv
                    act.wait_ge(s_st[m % 4], 16 * (len(range(m % 4, len(normed), 4)) + m // 4))
                    act.activation(res[m % 4], banks[n % 6][:], ACT.Copy).then_inc(s_vc, 1)
                    nv += 1
                else:
                    if nq >= 2:
                        act.wait_ge(s_ss, nq - 1)
                    act.activation(sqb[nq % 2], banks[n % 6][:], ACT.Square).then_inc(s_sq, 1)
                    act.wait_ge(s_ss, nq + 1)
                    act.activation(root[:, nq % 2], ssum[:, nq % 2], ACT.Sqrt, bias=s["eps"][:, 0:1],
                                   scale=1.0 / HD).then_inc(s_rt, 1)
                    nq += 1

        @block.vector
        def _(dve):
            dve.wait_ge(s_trig, 16)
            dve.tensor_scalar(gq, vec[:, RQ:RQ + HD], HD ** -0.5, None, ALU.mult).then_inc(s_tab, 1)
            for j in range(4):
                g = vec[:, RQ + j * HD:RQ + (j + 1) * HD].unsqueeze(1).broadcast_to([P, NTX, HD])
                if j < 2:
                    dve.tensor_scalar(tabs[:, j], trig[:, j % 2], HD ** -0.5, None, ALU.mult).then_inc(s_tab, 1)
                    dve.wait_ge(s_tab, 2 + 2 * j)
                    dve.tensor_tensor(tabs[:, j], tabs[:, j], g, ALU.mult).then_inc(s_tab, 1)
                else:
                    dve.tensor_tensor(tabs[:, j], trig[:, j % 2], g, ALU.mult).then_inc(s_tab, 1)
            dve.wait_ge(s_tab, 7)
            for m, n in enumerate(normed):
                c, t = work[n]
                b = m % 2
                dve.wait_ge(s_sq, m + 1)
                if m >= 2:
                    dve.wait_ge(s_rt, m - 1)
                dve.tensor_reduce(ssum[:, b], sqb[b].rearrange("p (h d) -> p h d", d=HD), AX.X,
                                  ALU.add).then_inc(s_ss, 1)
                dve.wait_ge(s_rt, m + 1)
                dve.reciprocal(rinv[:, b], root[:, b]).then_inc(s_ri, 1)
                dve.wait_ge(s_ri, m + 1)
                if m >= 2:
                    dve.wait_ge(s_res, m - 1)
                dve.tensor_tensor(xr[b].rearrange("p (h d) -> p h d", d=HD),
                                  banks[n % 6][:].rearrange("p (h d) -> p h d", d=HD),
                                  rinv[:, b].unsqueeze(2).broadcast_to([P, HEADS, HD]), ALU.mult).then_inc(s_xr, 1)
                dve.wait_ge(s_xr, m + 1)
                if t < NTX:
                    sn = tabs[:, 2 * c - 1, t]
                    v = xr[b].rearrange("p (h f d) -> p h f d", h=HEADS, f=2)
                    o = rot[b].rearrange("p (h f d) -> p h f d", h=HEADS, f=2)
                    for f in range(2):
                        dve.tensor_tensor(o[:, :, f], v[:, :, 1 - f],
                                          sn[:, f * 32:(f + 1) * 32].unsqueeze(1).broadcast_to([P, HEADS, 32]),
                                          ALU.mult).then_inc(s_rot, 1)

        @block.gpsimd
        def _(pool):
            pool.wait_ge(s_tab, 7)
            pool.wait_ge(s_trig, 16)
            rots = 0
            for m, n in enumerate(normed):
                c, t = work[n]
                b = m % 2
                pool.wait_ge(s_xr, m + 1)
                if m >= 4:
                    pool.wait_ge(s_st[m % 4], 16 * (m // 4))
                if t < NTX:
                    g = tabs[:, 2 * c - 2, t]
                else:
                    g = gq if c == 1 else vec[:, RQ + 2 * HD:RQ + 3 * HD]
                gb = g.unsqueeze(1).broadcast_to([P, HEADS, HD])
                o = res[m % 4].rearrange("p (h d) -> p h d", d=HD)
                pool.tensor_tensor(o, xr[b].rearrange("p (h d) -> p h d", d=HD), gb, ALU.mult)\
                    .then_inc(s_sin, 1)
                pool.wait_ge(s_sin, m + 1)
                if t < NTX:
                    rots += 2
                    pool.wait_ge(s_rot, rots)
                    pool.tensor_tensor(res[m % 4], res[m % 4], rot[b], ALU.add).then_inc(s_res, 1)
                else:
                    pool.sem_inc(s_res, 1)


def conv_branch(s, layer, last):
    nc, sem, place, vec, banks = s["nc"], s["sem"], s["place"], s["vec"], s["banks"]
    HT, YC = place(A_H, KD, TOK), place(A_YC, 2, TOK)
    at = A_R + NT * F_WIDTH
    wb = place(at, KD, 3 * CONV)
    at += 3 * CONV * KD
    UW = TOK + 4
    u = place(at, 2, UW)
    gate = place(at + 2 * UW, 2, TOK)
    xc = [place(at + 2 * UW + 2 * TOK + i * 512, 512) for i in range(2)]
    y = place(at + 2 * UW + 2 * TOK + 1024, 2, TOK)
    spans = [(0, 512, 1), (512, 512, 1)] + ([] if last else [(1024, 256, 3)])
    work = [(j, sp) for j in range(2) for sp in spans]
    segs = [(0, SEQ, 0)] + ([] if last else [(SEQ, CTX, SEQ + 2)])
    s_w, s_mm, s_zero = sem("w_conv_loaded"), sem("conv_product"), sem("conv_zeros")
    s_x, s_g, s_u, s_y = sem("conv_x"), sem("conv_gate"), sem("conv_u"), sem("conv_y")
    with nc.Block() as block:
        @block.sync
        def _(sp):
            s["clear_last"](sp)
            sp.dma_start(wb, s["a"]["w_rows"][layer, :, KS[4] * KD:KS[5] * KD]
                         .rearrange("p (k n) -> p k n", k=KD)).then_inc(s_w, 16)

        @block.tensor
        def _(pe):
            pe.wait_ge(s_w, 16)
            for n, (j, (t0, tn, _)) in enumerate(work):
                if n >= 2:
                    pe.wait_ge(s_g, n - 1)
                    pe.wait_ge(s_u, n - 1)
                for q in range(3):
                    for k in range(KD):
                        mm = pe.matmul(banks[3 * (n % 2) + q][:, 0:tn],
                                       wb[:, k, q * CONV + j * P:q * CONV + (j + 1) * P],
                                       HT[:, k, t0:t0 + tn], start=k == 0, stop=k == KD - 1)
                    mm.then_inc(s_mm, 1)

        @block.scalar
        def _(act):
            for n, (j, (t0, tn, _)) in enumerate(work):
                act.wait_ge(s_mm, 3 * n + 1)
                if n >= 2:
                    act.wait_ge(s_u, n - 1)
                act.activation(xc[n % 2][:, 0:tn], banks[3 * (n % 2)][:, 0:tn], ACT.Copy).then_inc(s_x, 1)
                act.wait_ge(s_mm, 3 * n + 2)
                act.activation(gate[:, j, t0:t0 + tn], banks[3 * (n % 2) + 1][:, 0:tn], ACT.Copy).then_inc(s_g, 1)
            act.wait_ge(s_g, len(work))

        @block.vector
        def _(dve):
            dve.memset(u, 0.0).then_inc(s_zero, 1)
            dve.wait_ge(s_zero, 1)
            for n, (j, (t0, tn, off)) in enumerate(work):
                dve.wait_ge(s_x, n + 1)
                dve.wait_ge(s_mm, 3 * n + 3)
                dve.tensor_tensor(u[:, j, off + t0:off + t0 + tn], banks[3 * (n % 2) + 2][:, 0:tn],
                                  xc[n % 2][:, 0:tn], ALU.mult).then_inc(s_u, 1)
            dve.wait_ge(s_u, len(work))
            done = Count(s_y)
            for j in range(2):
                for t0, tn, off in segs:
                    w = [vec[:, V_CONV + layer * 6 + j * 3 + i:V_CONV + layer * 6 + j * 3 + i + 1] for i in range(3)]
                    yy = y[:, j, t0:t0 + tn]
                    done.up(dve.tensor_scalar(yy, u[:, j, off:off + tn], w[0], None, ALU.mult))
                    for i in (1, 2):
                        dve.wait_ge(s_y, done.now())
                        done.up(dve.scalar_tensor_tensor(yy, u[:, j, off + i:off + i + tn], w[i], yy,
                                                         ALU.mult, ALU.add))
                    dve.wait_ge(s_y, done.now())
                    dve.wait_ge(s_g, len(work))
                    done.up(dve.tensor_tensor(YC[:, j, t0:t0 + tn], yy, gate[:, j, t0:t0 + tn], ALU.mult))
            dve.wait_ge(s_y, done.now())


def fourier_branch(s, layer, last):
    nc, sem, place, banks = s["nc"], s["sem"], s["place"], s["banks"]
    U, FT = place(A_R, NT, F_WIDTH), place(A_FT, 2, TOK)
    at = A_R + NT * F_WIDTH
    cb = [place(at + i * 4096, NTX, 512) for i in range(2)]
    at += 8192
    small = place(at, 4, P)
    dctx = place(at + 512, 2, 2, CTX)
    ab = place(at + 1536, 4, 512)
    s_c = [sem("dft_loaded_even"), sem("dft_loaded_odd")]
    s_small, s_mm, s_ab, s_fm, s_f = sem("dft_small_loaded"), sem("dft_product"), sem("dft_copied"), \
        sem("dft_channels"), sem("ft_copied")
    spans = [(0, 0, 512), (1, 512, 512)] + ([] if last else [(2, 1024, 256)])
    with nc.Block() as block:
        @block.sync
        def _(sp):
            s["clear_last"](sp)
            sp.dma_start(small, s["a"]["consts"][:, C_DFT:C_DFT + 4 * P].rearrange("p (a b) -> p a b", b=P))\
                .then_inc(s_small, 16)
            sp.dma_start(dctx, s["a"]["consts"][:, C_DCTX:C_DCTX + 4 * CTX]
                         .rearrange("p (a b c) -> p a b c", b=2, c=CTX)).then_inc(s_small, 16)
            for n in range(4):
                if n >= 2:
                    sp.wait_ge(s_mm, 2 * (n - 1))
                sp.dma_start(cb[n % 2], s["a"]["dft"][n]).then_inc(s_c[n % 2], 16)

        @block.tensor
        def _(pe):
            pe.wait_ge(s_small, 32)
            for g, t0, tn in spans:
                if g:
                    pe.wait_ge(s_ab, 4 * g)
                for w in range(2):
                    n = 2 * g + w
                    if g < 2:
                        pe.wait_ge(s_c[n % 2], 16 * (n // 2 + 1))
                    tiles = range(NTX) if g < 2 else range(2)
                    for ct in range(2):
                        for t in tiles:
                            rhs = cb[n % 2][:, t, :] if g < 2 else dctx[:, t, w, :]
                            mm = pe.matmul(banks[2 * w + ct][:, 0:tn],
                                           U[:, t + (NTX if g == 2 else 0), ct * P:(ct + 1) * P], rhs,
                                           start=t == 0, stop=t == len(tiles) - 1)
                        mm.then_inc(s_mm, 1)
                pe.wait_ge(s_ab, 4 * g + 4)
                if g:
                    pe.wait_ge(s_f, 2 * g)
                for ct in range(2):
                    for w in range(2):
                        mm = pe.matmul(banks[4 + ct][:, 0:tn], small[:, (2 if g == 2 else 0) + w, :],
                                       ab[:, 2 * w + ct, 0:tn], start=w == 0, stop=w == 1)
                    mm.then_inc(s_fm, 1)

        @block.scalar
        def _(act):
            for g, t0, tn in spans:
                if g:
                    act.wait_ge(s_fm, 2 * g)
                for i in range(4):
                    act.wait_ge(s_mm, 4 * g + i + 1)
                    act.activation(ab[:, i, 0:tn], banks[i][:, 0:tn], ACT.Copy).then_inc(s_ab, 1)
            act.wait_ge(s_ab, 4 * len(spans))

        @block.vector
        def _(dve):
            for g, t0, tn in spans:
                for ct in range(2):
                    dve.wait_ge(s_fm, 2 * g + ct + 1)
                    dve.tensor_copy(FT[:, ct, t0:t0 + tn], banks[4 + ct][:, 0:tn]).then_inc(s_f, 1)
            dve.wait_ge(s_f, 2 * len(spans))


def attention(s, layer, last):
    nc, sem, place, vec, banks = s["nc"], s["sem"], s["place"], s["vec"], s["banks"]
    ATT = place(A_ATT, PAIRS, TOK)
    at = A_R
    V = place(at, NT, NAW)
    VS = place(at + NT * NAW, NTX - 1, NAW)
    at += (2 * NT - 3) * NAW
    raw, tbl = place(at, RPB_R, GRID_W), place(at + 960, RPB_R, GRID_W)
    at += 1920
    QT, KT = place(at, TOK), place(at + TOK, TOK)
    qs, ks = place(at + 2 * TOK, NT, P), place(at + 3 * TOK, NT, P)
    at += 4 * TOK
    sc = [place(at + i * 512, 512) for i in range(2)]
    pr = [place(at + 1024 + i * 768, 768) for i in range(2)]
    pt = [place(at + 2560 + i * 768, 6, P) for i in range(2)]
    ao = [place(at + 4096 + i * HD, HD) for i in range(2)]
    at += 4096 + 2 * HD
    mask = place(at, GRID_W)
    st = place(at + GRID_W, 4, 8)
    ident = s["ident"]
    NQ = NTX if last else NT
    NI = ROWS + (0 if last else CTX // GRID_W)
    groups = [(qs, QT, t, min(t + 4, NQ)) for t in range(0, NQ, 4)] + [(ks, KT, t, min(t + 4, NT)) for t in range(0, NT, 4)]
    G4, G5 = (len(groups) + 1) // 2, len(groups) // 2
    U4, U5 = G4 + ROWS, G5 + NI
    start = [min(max(r - WIN_R // 2, 0), ROWS - WIN_R) for r in range(ROWS)]
    s_v, s_qk, s_raw, s_mask = sem("v_loaded"), sem("qk_loaded"), sem("bias_loaded"), sem("mask_loaded")
    s_tbl, s_pe, s_dve = sem("bias_ready"), sem("tensor_passed"), sem("vector_passed")
    s_sc, s_mid, s_m, s_e, s_el = sem("scores"), sem("local_max"), sem("neg_max"), sem("probs"), sem("probs_local")
    s_t4, s_t5, s_b4, s_b5 = sem("bank4_filled"), sem("bank5_filled"), sem("bank4_copied"), sem("bank5_copied")
    s_pv, s_o, s_tt, s_at, s_l = sem("weighted"), sem("normalised"), sem("out_turned"), sem("out_copied"), sem("inv")

    def v_tiles(n, pair):
        cols = bass.ds(pair * P, P)
        local = []
        if n < ROWS:
            src, t0 = (V, start[n] // 2) if start[n] % 2 == 0 else (VS, (start[n] - 1) // 2)
            local = [(j, src[:, t0 + j, cols]) for j in range(4)]
        return local + [(4 + j, V[:, NTX + j, cols]) for j in range(2)]

    with nc.Block() as block:
        @block.sync
        def _(sp):
            s["clear_last"](sp)
            sp.dma_start(mask, s["a"]["consts"][:, C_MASK:C_MASK + GRID_W]).then_inc(s_mask, 16)

            def load(pair):
                sp.dma_start(qs[:, 0:NQ], s["q_rows"][0:NQ * P, bass.ds(pair * P, P)]
                             .rearrange("(t p) d -> p t d", p=P)).then_inc(s_qk, 16)
                sp.dma_start(ks, s["k_rows"][:, bass.ds(pair * P, P)]
                             .rearrange("(t p) d -> p t d", p=P)).then_inc(s_qk, 16)

            def load_biases(pair):
                for h in range(2):
                    sp.dma_start(raw[h * 64:(h + 1) * 64],
                                 bass.AP(s["a"]["rpb"].tensor,
                                         pair * (2 * RPB_R * RPB_PAD) + (layer * HEADS + h) * RPB_R * RPB_PAD,
                                         [[1, GRID_W], [RPB_PAD, RPB_R], [1, GRID_W]])).then_inc(s_raw, 16)

            load(0)
            load_biases(0)
            sp.dma_start(V, s["v_rows"].rearrange("(t p) d -> p t d", p=P)).then_inc(s_v, 16)
            sp.dma_start(VS, s["v_rows"][GRID_W:SEQ - GRID_W].rearrange("(t p) d -> p t d", p=P)).then_inc(s_v, 16)
            with sp.Fori(0, PAIRS - 1) as i:
                sp.wait_ge(s_b4, i * U4 + (G4 + 1))
                sp.wait_ge(s_b5, i * U5 + (G5 + 1))
                load(i + 1)
                sp.wait_ge(s_tbl, i + 1)
                load_biases(i + 1)

        @block.gpsimd
        def _(pool):
            pool.wait_ge(s_mask, 16)
            with pool.Fori(0, PAIRS) as i:
                pool.wait_ge(s_raw, i * 32 + 32)
                pool.wait_ge(s_m, i * NI + 1)
                pool.tensor_tensor(tbl, raw[:, :, ::-1], mask.unsqueeze(1).broadcast_to([P, RPB_R, GRID_W]),
                                   ALU.add).then_inc(s_tbl, 1)
            pool.wait_ge(s_tbl, PAIRS)

        @block.tensor
        def _(pe):
            pe.sem_inc(s_pv, 2)
            pe.sem_inc(s_tt, 2)
            with pe.Fori(0, PAIRS) as i:
                pe.wait_ge(s_qk, i * 32 + 32)
                for g, (src, dst, t0, t1) in enumerate(groups):
                    filled, copied, u = (s_t5, s_b5, i * U5 + g // 2) if g % 2 else (s_t4, s_b4, i * U4 + g // 2)
                    pe.wait_ge(copied, u + 1)
                    for t in range(t0, t1):
                        mm = pe.transpose(banks[4 + g % 2][:, (t - t0) * P:(t - t0 + 1) * P], src[:, t, :], ident[:])
                    mm.then_inc(filled, 1)
                pe.wait_ge(s_b4, i * U4 + (G4 + 1))
                pe.wait_ge(s_b5, i * U5 + (G5 + 1))
                for j in range(NI + 3):
                    if j < NI:
                        n = j
                        pe.wait_ge(s_e, i * NI + (n + 1))
                        q0 = n * GRID_W
                        apart(pe, s_pe)
                        for h in (0, 64):
                            if n < ROWS:
                                k0 = start[n] * GRID_W
                                pe.matmul(banks[n % 2][h:h + 64, :], QT[h:h + 64, q0:q0 + 64],
                                          KT[h:h + 64, k0:k0 + 512], start=True, stop=True)
                            mm = pe.matmul(banks[2 + n % 2][h:h + 64, 0:CTX], QT[h:h + 64, q0:q0 + 64],
                                           KT[h:h + 64, SEQ:TOK], start=True, stop=True)
                        mm.then_inc(s_sc, 1)
                    if 1 <= j <= NI:
                        n = j - 1
                        pe.wait_ge(s_e, i * NI + (n + 3))
                        if n < ROWS:
                            pe.wait_ge(s_b4, i * U4 + (G4 + n + 1))
                            for k in range(4):
                                mm = pe.transpose(banks[4][:, k * P:(k + 1) * P], pr[n % 2][:, k * P:(k + 1) * P],
                                                  ident[:])
                            mm.then_inc(s_t4, 1)
                        pe.wait_ge(s_b5, i * U5 + (G5 + n + 1))
                        for k in range(2):
                            mm = pe.transpose(banks[5][:, k * P:(k + 1) * P], pr[n % 2][:, (4 + k) * P:(5 + k) * P],
                                              ident[:])
                        mm.then_inc(s_t5, 1)
                    if 2 <= j <= NI + 1:
                        n = j - 2
                        if n == 0:
                            pe.wait_ge(s_v, 32)
                        if n < ROWS:
                            pe.wait_ge(s_b4, i * U4 + (G4 + n + 2))
                        pe.wait_ge(s_b5, i * U5 + (G5 + n + 2))
                        pe.wait_ge(s_o, i * NI + (n + 1))
                        tiles = v_tiles(n, i)
                        for m, (k, v) in enumerate(tiles):
                            mm = pe.matmul(banks[6][:, 0:P], pt[n % 2][:, k, :], v, start=m == 0,
                                           stop=m == len(tiles) - 1)
                        mm.then_inc(s_pv, 1)
                    if j >= 3:
                        n = j - 3
                        pe.wait_ge(s_o, i * NI + (n + 2))
                        pe.wait_ge(s_at, i * NI + (n + 1))
                        apart(pe, s_pe)
                        pe.transpose(banks[7][0:HD, 0:P], ao[n % 2], ident[:]).then_inc(s_tt, 1)

        @block.vector
        def _(dve):
            dve.sem_inc(s_m, 1)
            dve.sem_inc(s_b5, 1)
            dve.sem_inc(s_o, 1)
            with dve.Fori(0, PAIRS) as i:
                for g, (src, dst, t0, t1) in enumerate(groups):
                    if g % 2:
                        dve.wait_ge(s_t5, i * U5 + (g // 2 + 1))
                        dve.tensor_copy(dst[:, t0 * P:t1 * P], banks[5][:, 0:(t1 - t0) * P]).then_inc(s_b5, 1)
                dve.wait_ge(s_b5, i * U5 + (G5 + 1))
                for j in range(NI + 2):
                    if j < NI:
                        n = j
                        x = st[:, n % 4]
                        dve.wait_ge(s_sc, i * NI + (n + 1))
                        dve.wait_ge(s_e, i * NI + (n + 1))
                        if n < ROWS:
                            if n == 0:
                                dve.wait_ge(s_tbl, i + 1)
                            d0 = start[n] - n + WIN_R - 1
                            apart(dve, s_dve)
                            dve.tensor_tensor_reduce(
                                out=sc[n % 2], in0=banks[n % 2][:],
                                in1=tbl[:, d0:d0 + WIN_R, :].rearrange("p a b -> p (a b)"), scale=1.0,
                                scalar=-3e38, op0=ALU.add, op1=ALU.max, accum_out=x[:, 0:1]).then_inc(s_mid, 1)
                        dve.tensor_reduce(x[:, 1:2], banks[2 + n % 2][:, 0:CTX], AX.X, ALU.max).then_inc(s_mid, 1)
                        dve.wait_ge(s_mid, i * (ROWS + NI) + (min(n + 1, ROWS) + n + 1))
                        if n < ROWS:
                            dve.tensor_scalar(x[:, 2:3], x[:, 1:2], x[:, 0:1], -1.0, ALU.max,
                                              ALU.mult).then_inc(s_m, 1)
                        else:
                            dve.tensor_scalar(x[:, 2:3], x[:, 1:2], -1.0, None, ALU.mult).then_inc(s_m, 1)
                    if 1 <= j <= NI:
                        n = j - 1
                        dve.wait_ge(s_t5, i * U5 + (G5 + n + 1))
                        dve.wait_ge(s_pv, i * NI + (n + 1))
                        dve.tensor_copy(pt[n % 2][:, 4:6, :].rearrange("p a b -> p (a b)"),
                                        banks[5][:, 0:CTX]).then_inc(s_b5, 1)
                    if j >= 2:
                        n = j - 2
                        x = st[:, n % 4]
                        if n < ROWS:
                            dve.tensor_tensor(x[:, 5:6], x[:, 3:4], x[:, 4:5], ALU.add).then_inc(s_l, 1)
                        else:
                            dve.tensor_copy(x[:, 5:6], x[:, 4:5]).then_inc(s_l, 1)
                        dve.wait_ge(s_l, i * (2 * NI) + (2 * n + 1))
                        dve.reciprocal(x[:, 6:7], x[:, 5:6]).then_inc(s_l, 1)
                        dve.wait_ge(s_l, i * (2 * NI) + (2 * n + 2))
                        dve.wait_ge(s_pv, i * NI + (n + 3))
                        dve.wait_ge(s_tt, i * NI + (n + 1))
                        dve.tensor_scalar(ao[n % 2][0:64], banks[6][0:64, 0:HD], x[0:64, 6:7], None, ALU.mult)
                        dve.tensor_scalar(ao[n % 2][64:128], banks[6][64:128, HD:2 * HD], x[64:128, 6:7], None,
                                          ALU.mult).then_inc(s_o, 1)

        @block.scalar
        def _(act):
            act.sem_inc(s_e, 2)
            act.sem_inc(s_b4, 1)
            act.sem_inc(s_at, 1)
            with act.Fori(0, PAIRS) as i:
                for g, (src, dst, t0, t1) in enumerate(groups):
                    if g % 2 == 0:
                        act.wait_ge(s_t4, i * U4 + (g // 2 + 1))
                        act.activation(dst[:, t0 * P:t1 * P], banks[4][:, 0:(t1 - t0) * P], ACT.Copy).then_inc(s_b4, 1)
                for j in range(NI + 3):
                    if j < NI:
                        n = j
                        x = st[:, n % 4]
                        act.wait_ge(s_m, i * NI + (n + 2))
                        if n >= 2:
                            act.wait_ge(s_t5, i * U5 + (G5 + n - 1))
                        if n < ROWS:
                            act.activation(pr[n % 2][:, 0:512], sc[n % 2], ACT.Exp, bias=x[:, 2:3],
                                           accum_out=x[:, 3:4]).then_inc(s_el, 1)
                            act.wait_ge(s_el, i * ROWS + (n + 1))
                        act.activation(pr[n % 2][:, 512:768], banks[2 + n % 2][:, 0:CTX], ACT.Exp, bias=x[:, 2:3],
                                       accum_out=x[:, 4:5]).then_inc(s_e, 1)
                    if 1 <= j <= ROWS:
                        n = j - 1
                        act.wait_ge(s_t4, i * U4 + (G4 + n + 1))
                        act.wait_ge(s_pv, i * NI + (n + 1))
                        act.activation(pt[n % 2][:, 0:4, :].rearrange("p a b -> p (a b)"), banks[4][:],
                                       ACT.Copy).then_inc(s_b4, 1)
                    if j >= 3:
                        n = j - 3
                        act.wait_ge(s_tt, i * NI + (n + 3))
                        for h in range(2):
                            cp = act.activation(ATT[h * 64:(h + 1) * 64, bass.ds(i, 1), n * 64:(n + 1) * 64],
                                                banks[7][0:HD, h * 64:(h + 1) * 64].unsqueeze(1), ACT.Copy)
                        cp.then_inc(s_at, 1)
            act.wait_ge(s_at, PAIRS * NI + 1)


def gates_and_merge(s, layer, last):
    nc, sem, place, banks = s["nc"], s["sem"], s["place"], s["banks"]
    HT, ATT, FT, YC = place(A_H, KD, TOK), place(A_ATT, PAIRS, TOK), place(A_FT, 2, TOK), place(A_YC, 2, TOK)
    MERGED = place(A_R, KD, TOK)
    wb = [place(A_R + KD * TOK + i * 4096, 32, P) for i in range(2)]
    at = A_R + KD * TOK + 8192
    sg = [place(at + i * 512, 512) for i in range(2)]
    prod = [place(at + 1024 + i * 512, 512) for i in range(2)]
    spans = [(0, 512), (512, 512)] + ([] if last else [(1024, 256)])
    NS = len(spans)
    branches = [(FT, 24, 2), (ATT, 26, 4), (YC, 30, 2)]
    s_w = [sem("gate_w_loaded_even"), sem("gate_w_loaded_odd")]
    s_gm, s_bm, s_sg, s_pr, s_mg = sem("gate_product"), sem("branch_product"), sem("gate_ready"), sem("gated"), sem("merged")
    s_pool = sem("gpsimd_passed")
    U = 3 * NS
    with nc.Block() as block:
        @block.sync
        def _(sp):
            s["clear_last"](sp)
            with sp.Fori(0, KD - 1, 2) as i:
                for b in range(2):
                    sp.wait_ge(s_bm, i * U + (b * U + 1))
                    sp.dma_start(wb[b], s["a"]["w_gates"][layer, bass.ds(i + b, 1)]
                                 .rearrange("o p k n -> p (o k) n")).then_inc(s_w[b], 16)

        @block.tensor
        def _(pe):
            pe.sem_inc(s_bm, U + 1)
            with pe.Fori(0, KD - 1, 2) as i:
                for b in range(2):
                    pe.wait_ge(s_w[b], i * 8 + 16)
                    for n in range(U):
                        (t0, tn), q = spans[n // 3], n % 3
                        src, w0, ks = branches[q]
                        pe.wait_ge(s_pr, i * U + (b * U + n + 1))
                        for k in range(KD):
                            mm = pe.matmul(banks[2 * q][:, 0:tn], wb[b][:, q * KD + k, :], HT[:, k, t0:t0 + tn],
                                           start=k == 0, stop=k == KD - 1)
                        mm.then_inc(s_gm, 1)
                        for k in range(ks):
                            mm = pe.matmul(banks[2 * q + 1][:, 0:tn], wb[b][:, w0 + k, :], src[:, k, t0:t0 + tn],
                                           start=k == 0, stop=k == ks - 1)
                        mm.then_inc(s_bm, 1)

        @block.scalar
        def _(act):
            with act.Fori(0, KD - 1, 2) as i:
                for m in range(2 * U):
                    tn, q = spans[m % U // 3][1], m % 3
                    act.wait_ge(s_gm, i * U + (m + 1))
                    act.wait_ge(s_pr, i * U + (m + 2))
                    act.activation(sg[m % 2][:, 0:tn], banks[2 * q][:, 0:tn], ACT.Sigmoid).then_inc(s_sg, 1)

        @block.vector
        def _(dve):
            dve.sem_inc(s_pr, 3)
            with dve.Fori(0, KD - 1, 2) as i:
                for m in range(2 * U):
                    b, (t0, tn), q = m // U, spans[m % U // 3], m % 3
                    dve.wait_ge(s_sg, i * U + (m + 1))
                    dve.wait_ge(s_bm, i * U + (m + U + 2))
                    if q == 0:
                        to = MERGED[:, bass.ds(i + b, 1), t0:t0 + tn].rearrange("p o n -> p (o n)")
                    else:
                        to = prod[q - 1][:, 0:tn]
                        dve.wait_ge(s_mg, i * (2 * NS) + (m // 3 * 2 + q))
                    dve.tensor_tensor(to, banks[2 * q + 1][:, 0:tn], sg[m % 2][:, 0:tn], ALU.mult).then_inc(s_pr, 1)

        @block.gpsimd
        def _(pool):
            pool.sem_inc(s_mg, 2)
            with pool.Fori(0, KD - 1, 2) as i:
                for m in range(2 * U):
                    b, (t0, tn), q = m // U, spans[m % U // 3], m % 3
                    if q == 0:
                        continue
                    pool.wait_ge(s_pr, i * U + (m + 4))
                    pool.wait_ge(s_mg, i * (2 * NS) + (m // 3 * 2 + q + 1))
                    to = MERGED[:, bass.ds(i + b, 1), t0:t0 + tn].rearrange("p o n -> p (o n)")
                    apart(pool, s_pool)
                    pool.tensor_tensor(to, to, prod[q - 1][:, 0:tn], ALU.add).then_inc(s_mg, 1)
            pool.wait_ge(s_mg, 2 + KD * NS * 2)


def broadcast_columns(s, pe, columns, bank):
    for j, col in enumerate(columns):
        mm = pe.matmul(bank[:, j * P:(j + 1) * P], col.broadcast_to([P, P]), s["ident"][:], start=True, stop=True)
    return mm


def mixer_output(s, layer, last):
    nc, sem, place, mod, banks = s["nc"], s["sem"], s["place"], s["mod"], s["banks"]
    X, MERGED = place(A_X, NT, D), place(A_R, KD, TOK)
    wo = place(A_H, 2, KD, 512)
    g1 = place(A_H + 8192, 2, D)
    tmp = [place(A_R + KD * TOK + i * 512, 512) for i in range(2)]
    NQ = NTX if last else NT
    work = [(h, t) for h in range(2) for t in range(NQ)]
    s_w = [sem("w_o_first_loaded"), sem("w_o_second_loaded")]
    s_b, s_g, s_mm, s_t, s_x = sem("g1_rows"), sem("g1_copied"), sem("out_product"), sem("gated_out"), sem("x_updated")
    with nc.Block() as block:
        @block.sync
        def _(sp):
            s["clear_last"](sp)
            for h in range(2):
                sp.dma_start(wo[:, h], s["a"]["w_o"][layer, h]).then_inc(s_w[h], 16)

        @block.tensor
        def _(pe):
            for w in range(2):
                for h in range(2):
                    cols = [mod[:, layer, 2 * KD + 4 * h + j, w:w + 1] for j in range(4)]
                    broadcast_columns(s, pe, cols, banks[4 + 2 * w + h]).then_inc(s_b, 1)
            for n, (h, t) in enumerate(work):
                if t == 0:
                    pe.wait_ge(s_w[h], 16)
                if n >= 4:
                    pe.wait_ge(s_t, n - 3)
                for k in range(KD):
                    mm = pe.matmul(banks[n % 4][:], MERGED[:, k, t * P:(t + 1) * P], wo[:, h, k, :],
                                   start=k == 0, stop=k == KD - 1)
                mm.then_inc(s_mm, 1)

        @block.scalar
        def _(act):
            for w in range(2):
                for h in range(2):
                    act.wait_ge(s_b, 2 * w + h + 1)
                    act.activation(g1[:, w, h * 512:(h + 1) * 512], banks[4 + 2 * w + h][:], ACT.Copy)\
                        .then_inc(s_g, 1)

        @block.vector
        def _(dve):
            dve.wait_ge(s_g, 4)
            for n, (h, t) in enumerate(work):
                dve.wait_ge(s_mm, n + 1)
                if n >= 2:
                    dve.wait_ge(s_x, n - 1)
                dve.tensor_tensor(tmp[n % 2], banks[n % 4][:], g1[:, t // NTX, h * 512:(h + 1) * 512],
                                  ALU.mult).then_inc(s_t, 1)

        @block.gpsimd
        def _(pool):
            for n, (h, t) in enumerate(work):
                pool.wait_ge(s_t, n + 1)
                xs = X[:, t, h * 512:(h + 1) * 512]
                pool.tensor_tensor(xs, xs, tmp[n % 2], ALU.add).then_inc(s_x, 1)
            pool.wait_ge(s_x, len(work))


def norm_and_route(s, layer, last):
    nc, sem, place, vec, mod, banks = s["nc"], s["sem"], s["place"], s["vec"], s["mod"], s["banks"]
    X, H2 = place(A_X, NT, D), place(A_H, NT, D)
    NQ = NTX if last else NT
    at = A_R - 5 * TOK
    mul, add = place(at, 2, D), place(at + 2 * D, 2, D)
    n2 = place(at + 4 * D, D)
    rw = place(at + 5 * D, KD, EXP)
    at += 5 * D + KD * EXP
    junk = place(at, D)
    HT2 = [place(at + D + i * D, KD, P) for i in range(2)]
    at += 3 * D
    sq, root, rstd = place(at, NT), place(at + 16, NT), place(at + 32, NT)
    at += 48
    W = NQ * EXP
    big = [place(at + i * NT * EXP, NQ, EXP) for i in range(10)]
    S, SB, MSK, OH1, OH2, M, T1, RANK, TOT, T2 = big
    at += 10 * NT * EXP
    sm = [place(at + i * 48, NQ * 4) for i in range(10)]
    at += 480
    tri = place(at, P)
    ones = place(at + P, P)
    thr = place(at + 2 * P, NT)
    blk = place(at + 2 * P + NT, 48)
    desc = place(at + 2 * P + NT + 48, EXP)
    at += 2 * P + NT + 48 + EXP
    cnt, nb, cum, cum2, base = (place(at + i * EXP, EXP) for i in range(5))
    cmp = place(at + 5 * EXP, EXP, NT)
    cmpb = place(at + 5 * EXP + EXP * NT, 48, EXP)
    be = place(at + 5 * EXP + EXP * NT + 48 * EXP, 64)
    fd = place(at + 5 * EXP + EXP * NT + 48 * EXP + 64, NQ)
    s_ld, s_sq, s_root, s_r, s_bc, s_bcc = sem("router_loaded"), sem("squares2"), sem("root2"), sem("rstd2"), \
        sem("mod2_rows"), sem("mod2_copied")
    s_a, s_h, s_tn, s_tc, s_lg, s_s = sem("rows_scaled2"), sem("h2_ready"), sem("h2_turned"), sem("h2_turned_copied"), \
        sem("logits"), sem("router_scores")
    s_c, s_pp, s_pc, s_idx, s_sent = sem("routing_step"), sem("ranks"), sem("ones_ready"), sem("slots_known"), \
        s["pool_dma_sem"]("rows_sent")
    s_sh = sem("mod2_scale")
    CM, CB = 4 * KD, 3 * KD
    sc2 = place(at + 5 * EXP + EXP * NT + 48 * EXP + 64 + NT, KD, 2)
    with nc.Block() as block:
        @block.sync
        def _(sp):
            s["clear_last"](sp)
            sp.dma_start(n2, s["a"]["norm2_rows"][layer]).then_inc(s_ld, 16)
            sp.dma_start(rw, s["a"]["router_w"]).then_inc(s_ld, 16)
            c = s["a"]["consts"]
            sp.dma_start(tri, c[:, C_TRI:C_TRI + P]).then_inc(s_ld, 16)
            sp.dma_start(thr, c[:, C_THR:C_THR + NT]).then_inc(s_ld, 16)
            sp.dma_start(blk, c[:, C_BLK:C_BLK + 48]).then_inc(s_ld, 16)
            sp.dma_start(desc, c[:, C_DESC:C_DESC + EXP]).then_inc(s_ld, 16)

        @block.scalar
        def _(act):
            for t in range(NQ):
                if t:
                    act.wait_ge(s_sq, t)
                act.activation(junk, X[:, t], ACT.Square, accum_out=sq[:, t:t + 1]).then_inc(s_sq, 1)
            act.wait_ge(s_sq, NQ)
            act.activation(root[:, 0:NQ], sq[:, 0:NQ], ACT.Sqrt, bias=s["eps"][:, 0:1], scale=1.0 / D)\
                .then_inc(s_root, 1)
            for n in range(8):
                v, w, h = n // 4, n // 2 % 2, n % 2
                act.wait_ge(s_bc, n + 1)
                act.activation((mul, add)[v][:, w, h * 512:(h + 1) * 512], banks[n][:], ACT.Copy).then_inc(s_bcc, 1)
            for t in range(NQ):
                for h in range(2):
                    act.wait_ge(s_tn, 2 * t + h + 1)
                    if t >= 2:
                        act.wait_ge(s_lg, t - 1)
                    act.activation(HT2[t % 2][:, 4 * h:4 * h + 4].rearrange("p a b -> p (a b)"),
                                   banks[2 * (t % 2) + h][:], ACT.Copy).then_inc(s_tc, 1)
                if t >= 1:
                    act.wait_ge(s_lg, t)
                    act.activation(S[:, t - 1], banks[4 + (t - 1) % 2][:, 0:EXP], ACT.Sigmoid).then_inc(s_s, 1)
            act.wait_ge(s_lg, NQ)
            act.activation(S[:, NQ - 1], banks[4 + (NQ - 1) % 2][:, 0:EXP], ACT.Sigmoid).then_inc(s_s, 1)

        @block.tensor
        def _(pe):
            pe.wait_ge(s_sh, 1)
            for n in range(8):
                v, w, h = n // 4, n // 2 % 2, n % 2
                src = sc2 if v == 0 else mod[:, layer, CB:CB + KD, :]
                broadcast_columns(s, pe, [src[:, 4 * h + j, w:w + 1] for j in range(4)], banks[n]).then_inc(s_bc, 1)
            pe.wait_ge(s_bcc, 8)
            pe.wait_ge(s_ld, 96)
            for t in range(NQ + 1):
                if t < NQ:
                    pe.wait_ge(s_h, t + 1)
                    if t >= 2:
                        pe.wait_ge(s_tc, 2 * (t - 1))
                    for h in range(2):
                        for j in range(4):
                            mm = pe.transpose(banks[2 * (t % 2) + h][:, j * P:(j + 1) * P],
                                              H2[:, t, (4 * h + j) * P:(4 * h + j + 1) * P], s["ident"][:])
                        mm.then_inc(s_tn, 1)
                if t >= 1:
                    pe.wait_ge(s_tc, 2 * t)
                    if t >= 3:
                        pe.wait_ge(s_s, t - 2)
                    for k in range(KD):
                        mm = pe.matmul(banks[4 + (t - 1) % 2][:, 0:EXP], HT2[(t - 1) % 2][:, k, :], rw[:, k, :],
                                       start=k == 0, stop=k == KD - 1)
                    mm.then_inc(s_lg, 1)
            pe.wait_ge(s_pc, 1)
            flat = M.rearrange("p a b -> p (a b)")
            pe.matmul(banks[6][:, 0:W], tri, flat, start=True, stop=True).then_inc(s_pp, 1)
            pe.matmul(banks[7][:, 0:W], ones, flat, start=True, stop=True).then_inc(s_pp, 1)

        @block.vector
        def _(dve):
            dve.tensor_scalar(sc2, mod[:, layer, CM:CM + KD, :], 1.0, None, ALU.add).then_inc(s_sh, 1)
            dve.wait_ge(s_root, 1)
            dve.reciprocal(rstd[:, 0:NQ], root[:, 0:NQ]).then_inc(s_r, 1)
            dve.wait_ge(s_bcc, 8)
            dve.wait_ge(s_ld, 96)
            for w in range(2):
                dve.tensor_tensor(mul[:, w], mul[:, w], n2, ALU.mult).then_inc(s_r, 1)
            dve.wait_ge(s_r, 3)
            for t in range(NQ):
                w = t // NTX
                dve.scalar_tensor_tensor(H2[:, t], X[:, t], rstd[:, t:t + 1], mul[:, w], ALU.mult,
                                         ALU.mult).then_inc(s_a, 1)
            dve.wait_ge(s_s, NQ)
            step = Count(s_c)

            def do(instruction):
                step.up(instruction)
                dve.wait_ge(s_c, step.now())

            def over(x, n):
                return x.unsqueeze(2).broadcast_to([P, x.shape[1], n])

            g4 = [SB.rearrange("p t (g e) -> p (t g) e", e=4)[:, :, i] for i in range(4)]
            hi1, lo1, hi2, lo2, top, sec, grp, oh = sm[:8]
            one = sm[8][:, 0:NQ]
            two = sm[9][:, 0:NQ]
            do(dve.tensor_tensor(SB, S, vec[:, V_RB:V_RB + EXP].unsqueeze(1).broadcast_to([P, NQ, EXP]), ALU.add))
            do(dve.tensor_tensor(hi1, g4[0], g4[1], ALU.max))
            do(dve.tensor_tensor(lo1, g4[0], g4[1], ALU.min))
            do(dve.tensor_tensor(hi2, g4[2], g4[3], ALU.max))
            do(dve.tensor_tensor(lo2, g4[2], g4[3], ALU.min))
            do(dve.tensor_tensor(top, hi1, hi2, ALU.max))
            do(dve.tensor_tensor(sec, hi1, hi2, ALU.min))
            do(dve.tensor_tensor(lo1, lo1, lo2, ALU.max))
            do(dve.tensor_tensor(sec, sec, lo1, ALU.max))
            do(dve.tensor_tensor(grp, top, sec, ALU.add))
            g3 = grp.rearrange("p (t g) -> p t g", g=4)
            o3 = oh.rearrange("p (t g) -> p t g", g=4)
            do(dve.tensor_reduce(one, g3, AX.X, ALU.max))
            do(dve.tensor_tensor(o3, g3, over(one, 4), ALU.is_equal))
            do(dve.tensor_tensor(o3, o3, desc[:, 0:4].unsqueeze(1).broadcast_to([P, NQ, 4]), ALU.mult))
            do(dve.tensor_reduce(one, o3, AX.X, ALU.max))
            do(dve.tensor_tensor(o3, o3, over(one, 4), ALU.is_equal))
            m4 = oh.unsqueeze(2).broadcast_to([P, NQ * 4, 4])
            sb4 = SB.rearrange("p t (g e) -> p (t g) e", e=4)
            do(dve.tensor_tensor(sb4, sb4, m4, ALU.mult))
            do(dve.tensor_scalar(oh, oh, -NEG, NEG, ALU.mult, ALU.add))
            do(dve.tensor_tensor(sb4, sb4, m4, ALU.add))
            for OH in (OH1, OH2):
                do(dve.tensor_reduce(one, SB, AX.X, ALU.max))
                do(dve.tensor_tensor(OH, SB, over(one, EXP), ALU.is_equal))
                do(dve.tensor_tensor(OH, OH, desc.unsqueeze(1).broadcast_to([P, NQ, EXP]), ALU.mult))
                do(dve.tensor_reduce(one, OH, AX.X, ALU.max))
                do(dve.tensor_tensor(OH, OH, over(one, EXP), ALU.is_equal))
                if OH is OH1:
                    do(dve.scalar_tensor_tensor(SB, OH, 2 * NEG, SB, ALU.mult, ALU.add))
            step.up(dve.tensor_tensor(M, OH1, OH2, ALU.add))
            dve.wait_ge(s_c, step.now())
            dve.memset(ones, 1.0).then_inc(s_pc, 1)
            for j, OH in enumerate((OH1, OH2)):
                do(dve.tensor_tensor(T1, S, OH, ALU.mult))
                do(dve.tensor_reduce((one, two)[j], T1, AX.X, ALU.add))
            do(dve.tensor_tensor(fd, one, two, ALU.add))
            do(dve.reciprocal(fd, fd))
            do(dve.tensor_tensor(s["wts"][:, 0, 0:NQ], one, fd, ALU.mult))
            do(dve.tensor_tensor(s["wts"][:, 1, 0:NQ], two, fd, ALU.mult))
            dve.wait_ge(s_pp, 2)
            do(dve.tensor_copy(RANK.rearrange("p a b -> p (a b)"), banks[6][:, 0:W]))
            do(dve.tensor_copy(TOT.rearrange("p a b -> p (a b)"), banks[7][:, 0:W]))
            do(dve.tensor_copy(cnt, TOT[:, 0]))
            for t in range(1, NQ):
                do(dve.tensor_tensor(RANK[:, t], RANK[:, t], cnt, ALU.add))
                do(dve.tensor_tensor(cnt, cnt, TOT[:, t], ALU.add))
            do(dve.tensor_tensor(cmp, over(cnt, NT), thr.unsqueeze(1).broadcast_to([P, EXP, NT]), ALU.is_gt))
            do(dve.tensor_reduce(nb, cmp, AX.X, ALU.add))
            a, b = cum, cum2
            do(dve.tensor_copy(a, nb))
            for d in (1, 2, 4, 8):
                do(dve.tensor_copy(b[:, 0:d], a[:, 0:d]))
                do(dve.tensor_tensor(b[:, d:EXP], a[:, d:EXP], a[:, 0:EXP - d], ALU.add))
                a, b = b, a
            do(dve.tensor_tensor(base, a, nb, ALU.subtract))
            do(dve.tensor_scalar(base, base, float(P), None, ALU.mult))
            do(dve.tensor_tensor(cmpb, a.unsqueeze(1).broadcast_to([P, 48, EXP]), over(blk, EXP), ALU.is_le))
            do(dve.tensor_reduce(be[:, 0:48], cmpb, AX.X, ALU.add))
            do(dve.tensor_scalar(be[:, 0:48], be[:, 0:48], float(EXP - 1), None, ALU.min))
            do(dve.tensor_copy(be[:, 48:49], a[:, EXP - 1:EXP]))
            do(dve.memset(be[:, 49:64], 0.0))
            do(dve.tensor_copy(s["block_expert"][:], be[0:1, :]))
            do(dve.tensor_tensor(RANK, RANK, base.unsqueeze(1).broadcast_to([P, NQ, EXP]), ALU.add))
            for j, OH in enumerate((OH1, OH2)):
                do(dve.tensor_tensor(T1, RANK, OH, ALU.mult))
                do(dve.tensor_reduce(fd, T1, AX.X, ALU.add))
                do(dve.tensor_copy(s["dest"][:, j, 0:NQ], fd))
                dve.sem_inc(s_idx, 1)

        @block.gpsimd
        def _(pool):
            pool.wait_ge(s_bcc, 8)
            for t in range(NQ):
                pool.wait_ge(s_a, t + 1)
                pool.tensor_tensor(H2[:, t], H2[:, t], add[:, t // NTX], ALU.add).then_inc(s_h, 1)
            pool.wait_ge(s_h, NQ)
            for j in range(2):
                pool.wait_ge(s_idx, j + 1)
                for t in range(NQ):
                    pool.indirect_dma_start(
                        out=s["slots"][0:MAX_SLOTS], out_offset=bass.IndirectOffsetOnAxis(
                            s["dest"][:, j, t:t + 1], 0),
                        in_=H2[:, t], in_offset=None).then_inc(s_sent, 16)
            pool.wait_ge(s_sent, 16 * 2 * NQ)


def experts(s, layer, last):
    nc, sem, place, banks = s["nc"], s["sem"], s["place"], s["banks"]
    MAXB = ((SEQ if last else TOK) * 2 + EXP * (P - 1)) // P
    ROUNDS = (MAXB + 1) // 2
    at = A_H
    w13 = [place(at + i * 8192, 2, KD, DE) for i in range(2)]
    at += 16384
    w2 = [place(at + i * 4096, DE // P, D) for i in range(2)]
    at += 8192
    xb = [place(at + i * D, D) for i in range(2)]
    xt = [place(at + 2 * D + i * D, KD, P) for i in range(2)]
    yb = [place(at + 4 * D + i * D, D) for i in range(2)]
    at += 6 * D
    sl = [place(at + i * DE, DE) for i in range(2)]
    gl = [place(at + 2 * DE + i * DE, DE) for i in range(2)]
    gt = [place(at + 4 * DE + i * DE, 4, P) for i in range(2)]
    be = s["block_expert"]
    ident = s["ident"]
    s_w13 = [sem("w13_loaded_even"), sem("w13_loaded_odd")]
    s_w2 = [sem("w2_loaded_even"), sem("w2_loaded_odd")]
    s_xb, s_yo = [sem("slots_loaded_even"), sem("slots_loaded_odd")], [sem("y_stored_even"), sem("y_stored_odd")]
    s_tx, s_xca, s_xcb, s_h1, s_h3, s_sl, s_g = sem("slots_turned"), sem("slots_copied_first"), sem("slots_copied_second"), sem("w1_product"), \
        sem("w3_product"), sem("silu"), sem("gated")
    s_tga, s_tgb, s_gca, s_gcb = sem("first_half_turned"), sem("second_half_turned"), sem("first_half_copied"), \
        sem("second_half_copied")
    s_done = sem("stores_done")
    s_y, s_yc0, s_yc1 = sem("w2_product"), sem("y_first_copied"), sem("y_second_copied")

    def rounds(eng, body):
        used = eng.value_load(be[0:1, 48:49], min_val=1, max_val=MAXB)
        with eng.Fori(0, ROUNDS) as r:
            with eng.If(used > r * 2):
                body(r)
        return used

    with nc.Block() as block:
        @block.sync
        def _(sp):
            s["clear_last"](sp)
            def body(r):
                for b in range(2):
                    e = sp.value_load(be[0:1, bass.ds(r * 2 + b, 1)], min_val=0, max_val=EXP - 1)
                    sp.wait_ge(s_h3, r * 2 + (b + 1))
                    sp.dma_start(w13[b], s["a"]["w13"][layer, bass.ds(e, 1)].rearrange("o p a k n -> p (o a) k n"))\
                        .then_inc(s_w13[b], 16)
                    sp.dma_start(xb[b], s["slots"][bass.ds(r * (2 * P) + b * P, P)]).then_inc(s_xb[b], 16)
                    sp.wait_ge(s_y, r * 4 + (2 * b + 2))
                    sp.dma_start(w2[b], s["a"]["w2"][layer, bass.ds(e, 1)].rearrange("o p k n -> p (o k) n"))\
                        .then_inc(s_w2[b], 16)
            rounds(sp, body)

        @block.tensor
        def _(pe):
            pe.sem_inc(s_h3, 2)
            pe.sem_inc(s_y, 4)

            def body(r):
                for b in range(2):
                    pe.wait_ge(s_xb[b], r * 16 + 16)
                    pe.wait_ge(s_xca, r * 2 + (b + 1))
                    pe.wait_ge(s_xcb, r * 2 + (b + 1))
                    for h in range(2):
                        for j in range(4):
                            mm = pe.transpose(banks[h][:, j * P:(j + 1) * P],
                                              xb[b][:, (4 * h + j) * P:(4 * h + j + 1) * P], ident[:])
                        mm.then_inc(s_tx, 1)
                    pe.wait_ge(s_xca, r * 2 + (b + 2))
                    pe.wait_ge(s_xcb, r * 2 + (b + 2))
                    pe.wait_ge(s_w13[b], r * 16 + 16)
                    pe.wait_ge(s_sl, r * 2 + (b + 1))
                    for k in range(KD):
                        mm = pe.matmul(banks[2][:], xt[b][:, k, :], w13[b][:, 0, k, :], start=k == 0,
                                       stop=k == KD - 1)
                    mm.then_inc(s_h1, 1)
                    pe.wait_ge(s_g, r * 2 + (b + 1))
                    for k in range(KD):
                        mm = pe.matmul(banks[3][:], xt[b][:, k, :], w13[b][:, 1, k, :], start=k == 0,
                                       stop=k == KD - 1)
                    mm.then_inc(s_h3, 1)
                    pe.wait_ge(s_g, r * 2 + (b + 2))
                    for h, (turned, copied) in enumerate(((s_tga, s_gca), (s_tgb, s_gcb))):
                        pe.wait_ge(copied, r * 2 + (b + 1))
                        for j in range(2):
                            mm = pe.transpose(banks[4 + h][:, j * P:(j + 1) * P],
                                              gl[b][:, (2 * h + j) * P:(2 * h + j + 1) * P], ident[:])
                        mm.then_inc(turned, 1)
                    pe.wait_ge(s_gca, r * 2 + (b + 2))
                    pe.wait_ge(s_gcb, r * 2 + (b + 2))
                    pe.wait_ge(s_w2[b], r * 16 + 16)
                    for h, copied in enumerate((s_yc0, s_yc1)):
                        pe.wait_ge(copied, r * 2 + (b + 1))
                        for k in range(4):
                            mm = pe.matmul(banks[6 + h][:], gt[b][:, k, :], w2[b][:, k, h * 512:(h + 1) * 512],
                                           start=k == 0, stop=k == 3)
                        mm.then_inc(s_y, 1)
            rounds(pe, body)

        @block.scalar
        def _(act):
            for b in range(2):
                act.sem_inc(s_yo[b], 16)
            act.sem_inc(s_xca, 1)
            act.sem_inc(s_sl, 1)
            act.sem_inc(s_gca, 1)
            act.sem_inc(s_yc0, 1)

            def body(r):
                for b in range(2):
                    act.wait_ge(s_tx, r * 4 + (2 * b + 1))
                    act.activation(xt[b][:, 0:4].rearrange("p a b -> p (a b)"), banks[0][:], ACT.Copy)\
                        .then_inc(s_xca, 1)
                    act.wait_ge(s_h1, r * 2 + (b + 1))
                    act.wait_ge(s_g, r * 2 + (b + 1))
                    act.activation(sl[b], banks[2][:], ACT.Silu).then_inc(s_sl, 1)
                    act.wait_ge(s_tga, r * 2 + (b + 1))
                    act.activation(gt[b][:, 0:2].rearrange("p a b -> p (a b)"), banks[4][:, 0:256], ACT.Copy)\
                        .then_inc(s_gca, 1)
                    act.wait_ge(s_y, r * 4 + (2 * b + 5))
                    act.wait_ge(s_yo[b], r * 16 + 16)
                    act.activation(yb[b][:, 0:512], banks[6][:], ACT.Copy).then_inc(s_yc0, 1)
                    act.wait_ge(s_yc0, r * 2 + (b + 2))
                    act.wait_ge(s_yc1, r * 2 + (b + 2))
                    act.dma_start(s["slots"][bass.ds(r * (2 * P) + b * P, P)], yb[b]).then_inc(s_yo[b], 16)
            used = rounds(act, body)
            for b in range(2):
                act.wait_ge(s_yo[b], ((used + 1) // 2) * 16 + 16)
            apart(act, s_done)

        @block.vector
        def _(dve):
            dve.sem_inc(s_xcb, 1)
            dve.sem_inc(s_g, 1)
            dve.sem_inc(s_gcb, 1)
            dve.sem_inc(s_yc1, 1)

            def body(r):
                for b in range(2):
                    dve.wait_ge(s_tx, r * 4 + (2 * b + 2))
                    dve.tensor_copy(xt[b][:, 4:8].rearrange("p a b -> p (a b)"), banks[1][:]).then_inc(s_xcb, 1)
                    dve.wait_ge(s_sl, r * 2 + (b + 2))
                    dve.wait_ge(s_h3, r * 2 + (b + 3))
                    dve.tensor_tensor(gl[b], banks[3][:], sl[b], ALU.mult).then_inc(s_g, 1)
                    dve.wait_ge(s_tgb, r * 2 + (b + 1))
                    dve.tensor_copy(gt[b][:, 2:4].rearrange("p a b -> p (a b)"), banks[5][:, 0:256])\
                        .then_inc(s_gcb, 1)
                    dve.wait_ge(s_y, r * 4 + (2 * b + 6))
                    dve.wait_ge(s_yo[b], r * 16 + 16)
                    dve.tensor_copy(yb[b][:, 512:1024], banks[7][:]).then_inc(s_yc1, 1)
            rounds(dve, body)


def combine(s, layer, last):
    nc, sem, place, mod, banks = s["nc"], s["sem"], s["place"], s["mod"], s["banks"]
    X = place(A_X, NT, D)
    NQ = NTX if last else NT
    g2 = place(A_H, 2, D)
    RING = 4
    Y = [place(A_H + 2 * D + i * 2 * D, 2, D) for i in range(RING)]
    t1 = [place(A_H + 10 * D + i * D, D) for i in range(2)]
    wts = s["wts"]
    s_y = [s["pool_dma_sem"](f"y_rows_{i}") for i in range(RING)]
    s_b, s_g, s_t1, s_t2, s_t3, s_x, s_out = sem("g2_rows"), sem("g2_copied"), sem("first_weighted"), \
        sem("both_weighted"), sem("gated_by_g2"), sem("x_done"), sem("out_stored")
    with nc.Block() as block:
        @block.tensor
        def _(pe):
            for w in range(2):
                for h in range(2):
                    cols = [mod[:, layer, 5 * KD + 4 * h + j, w:w + 1] for j in range(4)]
                    broadcast_columns(s, pe, cols, banks[2 * w + h]).then_inc(s_b, 1)

        @block.gpsimd
        def _(pool):
            def fetch(t):
                if t >= RING:
                    pool.wait_ge(s_t2, t - RING + 1)
                for j in range(2):
                    pool.indirect_dma_start(
                        out=Y[t % RING][:, j], out_offset=None, in_=s["slots"][0:MAX_SLOTS],
                        in_offset=bass.IndirectOffsetOnAxis(s["dest"][:, j, t:t + 1], 0)).then_inc(s_y[t % RING], 16)
            for t in range(RING):
                fetch(t)
            for t in range(NQ):
                if t + RING < NQ:
                    fetch(t + RING)
                pool.wait_ge(s_t3, t + 1)
                pool.tensor_tensor(X[:, t], X[:, t], t1[t % 2], ALU.add).then_inc(s_x, 1)
            pool.wait_ge(s_x, NQ)

        @block.scalar
        def _(act):
            for w in range(2):
                for h in range(2):
                    act.wait_ge(s_b, 2 * w + h + 1)
                    act.activation(g2[:, w, h * 512:(h + 1) * 512], banks[2 * w + h][:], ACT.Copy).then_inc(s_g, 1)
            for t in range(NQ):
                act.wait_ge(s_y[t % RING], 32 * (t // RING + 1))
                if t >= 2:
                    act.wait_ge(s_x, t - 1)
                act.activation(t1[t % 2], Y[t % RING][:, 0], ACT.Copy, scale=wts[:, 0, t:t + 1]).then_inc(s_t1, 1)

        @block.vector
        def _(dve):
            dve.wait_ge(s_g, 4)
            for t in range(NQ):
                dve.wait_ge(s_t1, t + 1)
                dve.wait_ge(s_y[t % RING], 32 * (t // RING + 1))
                dve.scalar_tensor_tensor(t1[t % 2], Y[t % RING][:, 1], wts[:, 1, t:t + 1], t1[t % 2], ALU.mult,
                                         ALU.add).then_inc(s_t2, 1)
                dve.wait_ge(s_t2, t + 1)
                dve.tensor_tensor(t1[t % 2], t1[t % 2], g2[:, t // NTX], ALU.mult).then_inc(s_t3, 1)

        @block.sync
        def _(sp):
            s["clear_last"](sp)
            if last:
                for t in range(NQ):
                    sp.wait_ge(s_x, t + 1)
                    sp.dma_start(s["out"][0, t * P:(t + 1) * P], X[:, t]).then_inc(s_out, 16)
                sp.wait_ge(s_out, 16 * NQ)



def _constants():
    c = np.zeros((P, C_TOTAL), np.float32)
    c[:, C_ID:C_ID + P] = np.eye(P)
    c[:, C_TRI:C_TRI + P] = np.triu(np.ones((P, P)), 1)
    col = np.arange(GRID_W)
    first = np.clip(col - WIN_C // 2, 0, GRID_W - WIN_C)
    inside = (col[None] >= first[:, None]) & (col[None] < first[:, None] + WIN_C)
    c[:, C_MASK:C_MASK + GRID_W] = np.tile(np.where(inside, 0.0, NEG), (2, 1))
    angle = 2 * np.pi * (np.outer(np.arange(64), np.arange(64)) % 64) / 64
    for i, length in enumerate((SEQ, CTX)):
        for j, m in enumerate((np.cos(angle), -np.sin(angle))):
            m = m / np.sqrt(length * 64)
            at = C_DFT + (2 * i + j) * P
            c[0:64, at:at + 64] = m
            c[64:128, at + 64:at + 128] = m
    angle = 2 * np.pi * (np.outer(np.arange(CTX), np.arange(CTX)) % CTX) / CTX
    d = np.stack([np.cos(angle), np.sin(angle)]).reshape(2, 2, P, CTX).transpose(2, 1, 0, 3)
    c[:, C_DCTX:C_DCTX + 4 * CTX] = d.reshape(P, 4 * CTX)
    c[:, C_THR:C_THR + NT] = P * np.arange(NT)
    c[:, C_BLK:C_BLK + 48] = np.arange(48)
    c[:, C_DESC:C_DESC + EXP] = 32 - np.arange(EXP)
    t = np.arange(SEQ)
    inv = np.power(np.float32(10000.0), -np.arange(HD // 4, dtype=np.float32) / np.float32(HD // 4))
    ang = np.concatenate([(t // GRID_W).astype(np.float32)[:, None] * inv,
                          (t % GRID_W).astype(np.float32)[:, None] * inv], 1).astype(np.float32)
    cos, sin = np.cos(ang), np.sin(ang)
    trig = np.stack([np.concatenate([cos, cos], 1), np.concatenate([-sin, sin], 1)])
    trig = trig.reshape(2, NTX, P, HD).transpose(2, 0, 1, 3).astype(np.float32)
    angle = 2 * np.pi * (np.outer(np.arange(SEQ), np.arange(SEQ)) % SEQ) / SEQ
    dft = np.stack([np.cos(angle), np.sin(angle)]).reshape(2, NTX, P, 2, 512).transpose(3, 0, 2, 1, 4)
    return c, trig, dft.reshape(4, P, NTX, 512).astype(np.float32)


def kernel(**inputs):
    import concourse.bacc as bacc
    from concourse.bass_utils import run_bass_kernel_spmd as run

    def arr(name):
        return np.asarray(inputs[name])

    def columns(v):
        return v.reshape(-1, P).T

    vectors = np.zeros((P, V_TOTAL), np.float32)
    vectors[:, V_C:V_C + 2 * KD:2] = columns(arr("c")[0])
    vectors[:, V_C + 1:V_C + 2 * KD:2] = columns(arr("c_ctx"))
    for layer in range(DEPTH):
        vectors[:, V_ADAB + layer * 48:V_ADAB + (layer + 1) * 48] = columns(arr("ada_b")[layer])
        vectors[:, V_N1 + layer * KD:V_N1 + (layer + 1) * KD] = columns(arr("norm1_g")[layer])
        cw = arr("conv_w")[layer].reshape(3, 2, P).transpose(2, 1, 0)
        vectors[:, V_CONV + layer * 6:V_CONV + (layer + 1) * 6] = cw.reshape(P, 6)
        for j, name in enumerate(("qn_g", "kn_g")):
            g = arr(name)[layer]
            at = V_QG + layer * 4 * HD + 2 * j * HD
            vectors[:, at:at + HD] = g
            vectors[:, at + HD:at + HD + 32] = g[32:]
            vectors[:, at + HD + 32:at + 2 * HD] = g[:32]
    vectors[:, V_RB:V_RB + EXP] = arr("router_b")
    consts, trig, dft = _constants()
    w_in = arr("w_in").reshape(DEPTH, KD, P, -1).transpose(0, 2, 1, 3)
    rows = [w_in[:, :, :, a:b].reshape(DEPTH, P, -1) for a, b in zip(KS[:5], KS[1:])]
    gates = w_in[:, :, :, KS[5]:].reshape(DEPTH, P, KD, 3, KD, P).transpose(0, 4, 1, 3, 2, 5)
    gates = gates.reshape(DEPTH, KD, P, 3 * KD, P)
    parts = [gates]
    for name, k in (("w_f", 2), ("w_na", 4), ("w_cv", 2)):
        parts.append(arr(name).reshape(DEPTH, k, P, KD, P).transpose(0, 3, 2, 1, 4))
    rpb = np.zeros((DEPTH, HEADS, RPB_R, RPB_PAD), np.float32)
    rpb[..., GRID_W - WIN_C:GRID_W + WIN_C - 1] = arr("rpb")[..., ::-1]
    w13 = np.stack([arr(n).reshape(DEPTH, EXP, KD, P, DE).transpose(0, 1, 3, 2, 4) for n in ("w1", "w3")], 3)
    data = dict(
        x=arr("x"), ctx=arr("ctx"), vectors=vectors, consts=consts, trig=trig, dft=dft,
        ada_w=arr("ada_w").reshape(DEPTH, KD, P, 12, 512).transpose(0, 3, 2, 1, 4),
        w_rows=np.concatenate(rows, 2), w_gates=np.concatenate(parts, 3), rpb=rpb,
        w_o=arr("w_o").reshape(DEPTH, KD, P, 2, 512).transpose(0, 3, 2, 1, 4),
        norm2_rows=np.repeat(arr("norm2_g")[:, None], P, 1),
        router_w=arr("router_w").reshape(KD, P, EXP).transpose(1, 0, 2),
        w13=w13, w2=arr("w2").reshape(DEPTH, EXP, DE // P, P, D).transpose(0, 1, 3, 2, 4),
    )
    nc = bacc.Bacc("TRN2", target_bir_lowering=False, num_devices=1)
    feeds, aps = {}, {}
    for name, v in data.items():
        v = np.ascontiguousarray(v)
        feeds[f"in_{name}"] = v
        aps[name] = nc.dram_tensor(f"in_{name}", v.shape, mybir.dt.from_np(v.dtype), kind="ExternalInput").ap()
    out = nc.dram_tensor("out_x", (1, SEQ, D), F32, kind="ExternalOutput").ap()
    hybrid_backbone(nc, aps, out)
    return run(nc, [feeds], core_ids=[0]).results[0]["out_x"]
```

```python
import concourse.bass as bass
from concourse import mybir
from contextlib import ExitStack
import numpy as np

F32 = mybir.dt.float32
F32R = mybir.dt.float32r
I32 = mybir.dt.int32
ALU = mybir.AluOpType
ACT = mybir.ActivationFunctionType
AX = mybir.AxisListType

P = 128
D = 1024
DEPTH = 2
SEQ = 1024
CTX = 256
GRID_W = 64
ROWS = SEQ // GRID_W
EPS = 1e-6
KD = D // P
NTX = SEQ // P
NT = (SEQ + CTX) // P
TOK = SEQ + CTX
F_WIDTH = 256
HEADS = 8
HD = 64
NAW = HEADS * HD
PAIRS = HEADS // 2
WIN_R = 8
WIN_C = 16
RPB_R = 2 * WIN_R - 1
RPB_PAD = 128
CONV = 256
KS = (0, 256, 768, 1280, 1792, 2560)
EXP = 16
GROUPS = 4
DE = 512
NEG = -1e30

V_C = 0
V_ADAB = V_C + 2 * KD
V_N1 = V_ADAB + DEPTH * 48
V_CONV = V_N1 + DEPTH * KD
V_QG = V_CONV + DEPTH * 6
V_RB = V_QG + DEPTH * 4 * HD
V_TOTAL = V_RB + EXP
C_ID = 0
C_TRI = C_ID + P
C_MASK = C_TRI + P
C_DFT = C_MASK + GRID_W
C_DCTX = C_DFT + 4 * P
C_THR = C_DCTX + 4 * CTX
C_BLK = C_THR + NT
C_DESC = C_BLK + 48
C_SEL = C_DESC + EXP
C_TOTAL = C_SEL + 2

ARENA = 52000
A_X = 0
A_H = A_X + NT * D
A_ATT = A_H + NT * D
A_FT = A_ATT + 4 * TOK
A_YC = A_FT + 2 * TOK
A_R = A_YC + 2 * TOK
A_U = ARENA - NT * F_WIDTH


class Count:

    def __init__(self, sem, base=0):
        self.sem, self.base, self.n = sem, base, 0

    def up(self, instruction, by=1):
        instruction.then_inc(self.sem, by)
        self.n += by
        return instruction

    def now(self):
        return self.base + self.n


def hybrid_backbone(nc, a, out):
    with ExitStack() as es:
        def sb(name, shape, dt=F32):
            return es.enter_context(nc.sbuf_tensor(name, shape, dt))

        banks = [es.enter_context(nc.psum_tensor(f"bank{i}", [P, 512], F32)) for i in range(8)]
        sb("arena", [P, ARENA])
        arena_base = nc.sbuf_base - 4 * ARENA
        vec = sb("vec", [P, V_TOTAL])
        mod = sb("mod", [P, DEPTH, 48, 2])
        scale1 = sb("scale1", [P, KD, 2])
        eps_col = sb("eps_col", [P, 1])
        ident = sb("ident", [P, P])
        silu = sb("silu", [P, KD, 2])
        select = sb("select", [P, 2])
        state = dict(
            nc=nc, a=a, out=out, banks=banks, vec=vec, mod=mod, scale1=scale1, ident=ident, eps=eps_col,
            silu=silu, select=select,
            slots=nc.dram_tensor("slots", [MAX_SLOTS, D], F32).ap(),
            q_rows=nc.dram_tensor("q_rows", [TOK, NAW], F32).ap(),
            k_rows=nc.dram_tensor("k_rows", [TOK, NAW], F32).ap(),
            x_rows=nc.dram_tensor("x_rows", [TOK, D], F32).ap(),
            v_rows=nc.dram_tensor("v_rows", [TOK, NAW], F32).ap(),
            dest=sb("dest", [P, 2, NT], I32), wts=sb("wts", [P, 2, NT]),
            plan=sb("plan", [1, PLAN], I32),
        )

        first_sem = min(nc.free_semaphores)
        sets = [range(first_sem + i * STAGE_SEMS, first_sem + (i + 1) * STAGE_SEMS) for i in range(2)]
        names = {"stage": 0, "used": 0, "pool": 0}

        def sem(name):
            n = names["used"]
            names["used"] += 1
            assert n < STAGE_SEMS
            return stage_semaphores.enter_context(
                nc.semaphore(f"{name}_{names['stage']}", num=sets[names["stage"] % 2][n]))

        def pool_dma_sem(name):
            names["pool"] += 1
            return es.enter_context(nc.semaphore(f"{name}_{names['stage']}", num=sets[1][-1] + names["pool"]))

        def clear_last(sp):
            if names["stage"]:
                sp.sem_clear(sets[(names["stage"] + 1) % 2])

        def shaped(flat, dims):
            if len(dims) == 1:
                return flat
            if len(dims) == 2:
                return flat.rearrange("p (a b) -> p a b", b=dims[1])
            return flat.rearrange("p (a b c) -> p a b c", b=dims[1], c=dims[2])

        placed = {}

        def place(at, *dims, dtype=F32):
            skip = at % 8
            start, n = at - skip, int(np.prod(dims)) + skip
            assert start + n <= ARENA
            if (start, n, dtype) not in placed:
                kind = "part" if dtype == F32R else "place"
                placed[start, n, dtype] = nc.alloc_sbuf_tensor_at(f"{kind}_{start}_{n}", [P, n], dtype,
                                                                  offset=arena_base + 4 * start)
            return shaped(placed[start, n, dtype][:, skip:n], dims)

        def part(at, *dims):
            return place(at, *dims, dtype=F32R)

        state["part"] = part
        state["sem"], state["place"], state["clear_last"] = sem, place, clear_last
        state["pool_dma_sem"] = pool_dma_sem
        stages = [(load_and_modulations, ())]
        for layer in range(DEPTH):
            last = layer == DEPTH - 1
            stages += [(norm_for_mixers, (layer,))]
            stages += [(f, (layer, last)) for f in (project_rows, conv_branch, fourier_branch, attention,
                                                    gates_and_merge, mixer_output, norm_and_route, experts, combine)]
        for n, (stage, args) in enumerate(stages):
            names.update(stage=n, used=0)
            with ExitStack() as stage_semaphores:
                stage(state, *args)


STAGE_SEMS = 36
ZEROS = 256
MAX_SLOTS = 42 * P
PLAN_USED = 48
PLAN_BEFORE = 49
PLAN = 80


def split_product(pe, out, left, right, first, last):
    pe.matmul(out, left[0], right[0], start=first, stop=False)
    pe.matmul(out, left[0], right[1], start=False, stop=False)
    return pe.matmul(out, left[1], right[0], start=False, stop=last)


def apart(eng, passed):
    eng.sem_inc(passed, 1)


class Modulations:

    CH = 12

    def __init__(self, s, first, count, weights, rows):
        self.s, self.first, self.count, self.weights, self.rows = s, first, count, weights, rows
        sem = s["sem"]
        self.loaded = [sem(f"ada_w_loaded_{i}") for i in range(len(weights))]
        self.product, self.copied = sem("mod_product"), sem("mod_rows_copied")
        self.turned, self.kept = sem("mod_turned"), sem("mod_kept")

    def load(self, eng, i):
        layer, chunk = divmod(self.first + i, self.CH)
        b = i % len(self.weights)
        if i >= len(self.weights):
            eng.wait_ge(self.product, i - len(self.weights) + 1)
        eng.dma_start(self.weights[b], self.s["a"]["ada_w"][layer, chunk]).then_inc(self.loaded[b], 16)

    def clear_rows(self, dve):
        dve.memset(self.rows, 0.0).then_inc(self.copied, 1)
        dve.wait_ge(self.copied, 1)

    def multiply(self, pe, i):
        b = i % len(self.weights)
        pe.wait_ge(self.loaded[b], 16 * (i // len(self.weights) + 1))
        if i:
            pe.wait_ge(self.copied, 4 * i + 1)
        for h in range(KD // 4):
            for j in range(4):
                mm = pe.matmul(self.s["banks"][6][32 * j:32 * j + 2, :], self.s["silu"][:, 4 * h + j, :],
                               self.weights[b][:, 4 * h + j, :], start=h == 0, stop=h == KD // 4 - 1)
        mm.then_inc(self.product, 1)

    def copy(self, dve, i):
        dve.wait_ge(self.product, i + 1)
        if i:
            dve.wait_ge(self.turned, i)
        for j in range(4):
            dve.tensor_copy(self.rows[32 * j:32 * j + 2], self.s["banks"][6][32 * j:32 * j + 2, :])\
                .then_inc(self.copied, 1)

    def turn(self, pe, i):
        pe.wait_ge(self.copied, 4 * i + 5)
        if i:
            pe.wait_ge(self.kept, i)
        for t in range(4):
            mm = pe.matmul(self.s["banks"][7][:, 2 * t:2 * t + 2], self.rows[:, t * P:(t + 1) * P],
                           self.s["select"][:], start=True, stop=True)
        mm.then_inc(self.turned, 1)

    def keep(self, dve, i):
        layer, chunk = divmod(self.first + i, self.CH)
        dve.wait_ge(self.turned, i + 1)
        at = V_ADAB + layer * 48 + 4 * chunk
        dve.tensor_tensor(self.s["mod"][:, layer, 4 * chunk:4 * chunk + 4, :],
                          self.s["banks"][7][:, 0:8].rearrange("p (t w) -> p t w", w=2),
                          self.s["vec"][:, at:at + 4].unsqueeze(2).broadcast_to([P, 4, 2]), ALU.add)\
            .then_inc(self.kept, 1)


FIRST_CHUNKS = 4
CONV_CHUNKS = 12
FOURIER_CHUNKS = 8


def load_and_modulations(s):
    nc, sem, place, vec, mod, banks = s["nc"], s["sem"], s["place"], s["vec"], s["mod"], s["banks"]
    X = place(A_X, NT, D)
    ada = Modulations(s, 0, FIRST_CHUNKS, [place(A_H + i * 4096, KD, 512) for i in range(FIRST_CHUNKS)],
                      place(A_R + 4096, 512))
    s_vec, s_small, s_x, s_silu, s_out = sem("vectors_loaded"), sem("small_loaded"), sem("x_loaded"), \
        sem("silu_done"), sem("eps_set")
    with nc.Block() as block:
        @block.sync
        def _(sp):
            s["clear_last"](sp)
            for i in range(FIRST_CHUNKS):
                ada.load(sp, i)

        @block.scalar
        def _(act):
            act.dma_start(vec[:], s["a"]["vectors"]).then_inc(s_vec, 16)
            act.dma_start(s["ident"][:], s["a"]["consts"][:, C_ID:C_ID + P]).then_inc(s_small, 16)
            act.dma_start(s["select"][:], s["a"]["consts"][:, C_SEL:C_SEL + 2]).then_inc(s_small, 16)
            act.dma_start(X[:, 0:NTX], s["a"]["x"][0].rearrange("(t p) d -> p t d", p=P)).then_inc(s_x, 16)
            act.dma_start(X[:, NTX:NT], s["a"]["ctx"][0].rearrange("(t p) d -> p t d", p=P)).then_inc(s_x, 16)
            act.wait_ge(s_vec, 16)
            act.activation(s["silu"][:], vec[:, V_C:V_C + 2 * KD].rearrange("p (k w) -> p k w", w=2),
                           ACT.Silu).then_inc(s_silu, 1)
            act.wait_ge(s_x, 32)
            act.wait_ge(s_small, 32)

        @block.tensor
        def _(pe):
            pe.wait_ge(s_silu, 1)
            pe.wait_ge(s_small, 32)
            for i in range(FIRST_CHUNKS):
                ada.multiply(pe, i)
                ada.turn(pe, i)

        @block.vector
        def _(dve):
            dve.memset(s["eps"][:], EPS).then_inc(s_out, 1)
            ada.clear_rows(dve)
            dve.wait_ge(s_vec, 16)
            for i in range(FIRST_CHUNKS):
                ada.copy(dve, i)
                ada.keep(dve, i)
            dve.wait_ge(ada.kept, FIRST_CHUNKS)
            dve.wait_ge(s_out, 1)


def norm_for_mixers(s, layer):
    nc, sem, place, vec, mod, banks = s["nc"], s["sem"], s["place"], s["vec"], s["mod"], s["banks"]
    X = place(A_X, NT, D)
    HT, HI, LO = place(A_X, KD, TOK), s["part"](A_H, KD, TOK), s["part"](A_X, KD, TOK)
    xn = place(A_R, NT, D)
    junk = place(A_R + NT * D, D)
    sq = place(A_ATT, NT)
    root = place(A_ATT + 16, NT)
    rstd = place(A_ATT + 32, NT)
    scale1 = s["scale1"]
    groups = [(0, 4, 0), (4, 8, 0), (8, 10, 1)]
    work = [(k, t0, t1, w) for t0, t1, w in groups for k in range(KD)]
    s_sq, s_root, s_rstd, s_sc = sem("squares"), sem("root"), sem("rstd"), sem("scale1_done")
    s_xn, s_turn, s_hi, s_raw, s_lo = sem("rows_scaled"), sem("turned"), sem("hi"), sem("turned_copied"), sem("lo")
    with nc.Block() as block:
        @block.sync
        def _(sp):
            s["clear_last"](sp)

        @block.scalar
        def _(act):
            for t in range(NT):
                if t:
                    act.wait_ge(s_sq, t)
                act.activation(junk, X[:, t], ACT.Square, accum_out=sq[:, t:t + 1]).then_inc(s_sq, 1)
            act.wait_ge(s_sq, NT)
            act.activation(root, sq, ACT.Sqrt, bias=s["eps"][:, 0:1], scale=1.0 / D).then_inc(s_root, 1)
            act.wait_ge(s_sc, 2)
            for n, (k, t0, t1, w) in enumerate(work):
                act.wait_ge(s_turn, n + 1)
                act.activation(HI[:, k, t0 * P:t1 * P], banks[n % 8][:, 0:(t1 - t0) * P], ACT.Identity,
                               bias=mod[:, layer, k, w:w + 1], scale=scale1[:, k, w:w + 1]).then_inc(s_hi, 1)
            act.wait_ge(s_hi, len(work))

        @block.vector
        def _(dve):
            gain = vec[:, V_N1 + layer * KD:V_N1 + (layer + 1) * KD]
            dve.tensor_scalar(scale1[:], mod[:, layer, KD:2 * KD, :], 1.0, None, ALU.add).then_inc(s_sc, 1)
            dve.wait_ge(s_sc, 1)
            dve.tensor_tensor(scale1[:], scale1[:], gain.unsqueeze(2).broadcast_to([P, KD, 2]),
                              ALU.mult).then_inc(s_sc, 1)
            dve.wait_ge(s_root, 1)
            dve.reciprocal(rstd, root).then_inc(s_rstd, 1)
            dve.wait_ge(s_rstd, 1)
            dve.wait_ge(s_sc, 2)
            for t in range(NT):
                dve.tensor_scalar(xn[:, t], X[:, t], rstd[:, t:t + 1], None, ALU.mult).then_inc(s_xn, 1)
            dve.wait_ge(s_xn, NT)
            for n, (k, t0, t1, w) in enumerate(work):
                dve.wait_ge(s_hi, n + 1)
                dve.tensor_scalar(HT[:, k, t0 * P:t1 * P], banks[n % 8][:, 0:(t1 - t0) * P],
                                  scale1[:, k, w:w + 1], mod[:, layer, k, w:w + 1],
                                  ALU.mult, ALU.add).then_inc(s_raw, 1)
            dve.wait_ge(s_raw, len(work))

        @block.gpsimd
        def _(pool):
            for n, (k, t0, t1, w) in enumerate(work):
                pool.wait_ge(s_hi, n + 1)
                pool.wait_ge(s_raw, n + 1)
                pool.tensor_tensor(LO[:, k, t0 * P:t1 * P], HT[:, k, t0 * P:t1 * P],
                                   HI[:, k, t0 * P:t1 * P].bitcast(F32), ALU.subtract).then_inc(s_lo, 1)
            pool.wait_ge(s_lo, len(work))

        @block.tensor
        def _(pe):
            for n, (k, t0, t1, w) in enumerate(work):
                pe.wait_ge(s_xn, t1)
                if n >= 8:
                    pe.wait_ge(s_raw, n - 7)
                for t in range(t0, t1):
                    mm = pe.transpose(banks[n % 8][:, (t - t0) * P:(t - t0 + 1) * P],
                                      xn[:, t, k * P:(k + 1) * P], s["ident"][:])
                mm.then_inc(s_turn, 1)


def project_rows(s, layer, last):
    nc, sem, place, vec, banks = s["nc"], s["sem"], s["place"], s["vec"], s["banks"]
    part = s["part"]
    HI, LO, U = part(A_H, KD, TOK), part(A_X, KD, TOK), place(A_U, NT, F_WIDTH)
    at = A_ATT
    wb = [place(at + i * 4096, KD, 512) for i in range(2)]
    wlo = [part(at + i * 4096, KD, 512) for i in range(2)]
    whi = [part(at + 8192 + i * 4096, KD, 512) for i in range(2)]
    at += 16384
    trig = place(at, 2, NTX, HD)
    tabs = place(at + 1024, 4, NTX, HD)
    gq = place(at + 3072, HD)
    at += 3136
    sqb = [place(at + i * 512, 512) for i in range(2)]
    xr = [place(at + 1024 + i * 512, 512) for i in range(2)]
    rot = [place(at + 2048 + i * 512, 512) for i in range(2)]
    res = [place(at + 3072 + i * 512, 512) for i in range(4)]
    ssum = place(at + 5120, 2, HEADS)
    root = place(at + 5136, 2, HEADS)
    rinv = place(at + 5152, 2, HEADS)
    chunks = []
    for c in range(4):
        chunks.append((c, list(range(NTX if last and c < 2 else NT))))
    work = [(c, t) for c, ts in chunks for t in ts]
    normed = [n for n, (c, t) in enumerate(work) if c in (1, 2)]
    s_w = [sem(f"w_in_{'FQKV'[c]}_loaded") for c in range(4)]
    s_trig, s_tab, s_mm = sem("trig_loaded"), sem("tables"), sem("row_product")
    s_free = sem("row_bank_free")
    s_sq, s_ss, s_rt, s_ri, s_xr = sem("q_squared"), sem("q_sums"), sem("q_root"), sem("q_rinv"), sem("q_scaled")
    s_rot, s_res, s_vc = sem("q_rot"), sem("qk_rows"), sem("v_rows")
    s_st = [sem(f"stored_{i}") for i in range(4)]
    s_sin = sem("q_sin")
    s_whi, s_wlo = sem("weights_hi"), sem("weights_lo")
    width = [256, 512, 512, 512]
    vwork = [n for n, (c, t) in enumerate(work) if c == 3]
    RQ = V_QG + layer * 4 * HD

    with nc.Block() as block:
        @block.sync
        def _(sp):
            s["clear_last"](sp)
            w = s["a"]["w_rows"]

            def load(c):
                if c >= 2:
                    sp.wait_ge(s_mm, sum(len(ts) for _, ts in chunks[:c - 1]))
                n = width[c]
                sp.dma_start(wb[c % 2][:, :, 0:n], w[layer, :, KS[c] * KD:KS[c] * KD + n * KD]
                             .rearrange("p (k n) -> p k n", k=KD)).then_inc(s_w[c], 16)

            load(0)
            sp.dma_start(trig, s["a"]["trig"]).then_inc(s_trig, 16)
            load(1)
            load(2)
            for m, n in enumerate(normed):
                if n == sum(len(ts) for _, ts in chunks[:2]):
                    load(3)
                sp.wait_ge(s_res, m + 1)
                c, t = work[n]
                sp.dma_start(s["q_rows" if c == 1 else "k_rows"][t * P:(t + 1) * P], res[m % 4])\
                    .then_inc(s_st[m % 4], 16)
            for m, n in enumerate(vwork):
                sp.wait_ge(s_vc, m + 1)
                sp.dma_start(s["v_rows"][work[n][1] * P:(work[n][1] + 1) * P], res[m % 4]).then_inc(s_st[m % 4], 16)
            for q in range(4):
                sp.wait_ge(s_st[q], 16 * (len(range(q, len(normed), 4)) + len(range(q, len(vwork), 4))))

        @block.tensor
        def _(pe):
            for n, (c, t) in enumerate(work):
                if n >= 6:
                    was = work[n - 6][0]
                    done = sum(1 for k, _ in work[:n - 5] if k == was or {k, was} == {1, 2})
                    pe.wait_ge({0: s_free, 1: s_xr, 2: s_xr, 3: s_vc}[was], done)
                w = width[c]
                for k in range(KD):
                    if t == 0:
                        pe.wait_ge(s_whi, c * KD + k + 1)
                        pe.wait_ge(s_wlo, c * KD + k + 1)
                    mm = split_product(pe, banks[n % 6][:, 0:w],
                                       (HI[:, k, t * P:(t + 1) * P], LO[:, k, t * P:(t + 1) * P]),
                                       (whi[c % 2][:, k, 0:w], wlo[c % 2][:, k, 0:w]), k == 0, k == KD - 1)
                mm.then_inc(s_mm, 1)

        @block.scalar
        def _(act):
            def round_weights(c, k):
                if k == 0:
                    act.wait_ge(s_w[c], 16)
                act.activation(whi[c % 2][:, k, 0:width[c]], wb[c % 2][:, k, 0:width[c]], ACT.Copy)\
                    .then_inc(s_whi, 1)

            for k in range(KD):
                round_weights(0, k)
            nq = nv = 0
            for n, (c, t) in enumerate(work):
                if c < 3 and t < KD:
                    round_weights(c + 1, t)
                act.wait_ge(s_mm, n + 1)
                if c == 0:
                    act.activation(U[:, t], banks[n % 6][:, 0:256], ACT.Copy).then_inc(s_free, 1)
                elif c == 3:
                    m = nv
                    act.wait_ge(s_st[m % 4], 16 * (len(range(m % 4, len(normed), 4)) + m // 4))
                    act.activation(res[m % 4], banks[n % 6][:], ACT.Copy).then_inc(s_vc, 1)
                    nv += 1
                else:
                    if nq >= 2:
                        act.wait_ge(s_ss, nq - 1)
                    act.activation(sqb[nq % 2], banks[n % 6][:], ACT.Square).then_inc(s_sq, 1)
                    act.wait_ge(s_ss, nq + 1)
                    act.activation(root[:, nq % 2], ssum[:, nq % 2], ACT.Sqrt, bias=s["eps"][:, 0:1],
                                   scale=1.0 / HD).then_inc(s_rt, 1)
                    nq += 1

        @block.vector
        def _(dve):
            def leave_weights(c, k):
                dve.wait_ge(s_whi, c * KD + k + 1)
                dve.tensor_tensor(wlo[c % 2][:, k, 0:width[c]], wb[c % 2][:, k, 0:width[c]],
                                  whi[c % 2][:, k, 0:width[c]].bitcast(F32), ALU.subtract).then_inc(s_wlo, 1)

            for k in range(KD):
                leave_weights(0, k)
            dve.wait_ge(s_trig, 16)
            dve.tensor_scalar(gq, vec[:, RQ:RQ + HD], HD ** -0.5, None, ALU.mult).then_inc(s_tab, 1)
            for j in range(4):
                g = vec[:, RQ + j * HD:RQ + (j + 1) * HD].unsqueeze(1).broadcast_to([P, NTX, HD])
                if j < 2:
                    dve.tensor_scalar(tabs[:, j], trig[:, j % 2], HD ** -0.5, None, ALU.mult).then_inc(s_tab, 1)
                    dve.wait_ge(s_tab, 2 + 2 * j)
                    dve.tensor_tensor(tabs[:, j], tabs[:, j], g, ALU.mult).then_inc(s_tab, 1)
                else:
                    dve.tensor_tensor(tabs[:, j], trig[:, j % 2], g, ALU.mult).then_inc(s_tab, 1)
            dve.wait_ge(s_tab, 7)
            for k in range(KD):
                leave_weights(1, k)
            for m, n in enumerate(normed):
                c, t = work[n]
                b = m % 2
                if t < KD:
                    leave_weights(c + 1, t)
                dve.wait_ge(s_sq, m + 1)
                if m >= 2:
                    dve.wait_ge(s_rt, m - 1)
                dve.tensor_reduce(ssum[:, b], sqb[b].rearrange("p (h d) -> p h d", d=HD), AX.X,
                                  ALU.add).then_inc(s_ss, 1)
                dve.wait_ge(s_rt, m + 1)
                dve.reciprocal(rinv[:, b], root[:, b]).then_inc(s_ri, 1)
                dve.wait_ge(s_ri, m + 1)
                if m >= 2:
                    dve.wait_ge(s_res, m - 1)
                dve.tensor_tensor(xr[b].rearrange("p (h d) -> p h d", d=HD),
                                  banks[n % 6][:].rearrange("p (h d) -> p h d", d=HD),
                                  rinv[:, b].unsqueeze(2).broadcast_to([P, HEADS, HD]), ALU.mult).then_inc(s_xr, 1)
                dve.wait_ge(s_xr, m + 1)
                if t < NTX:
                    sn = tabs[:, 2 * c - 1, t]
                    v = xr[b].rearrange("p (h f d) -> p h f d", h=HEADS, f=2)
                    o = rot[b].rearrange("p (h f d) -> p h f d", h=HEADS, f=2)
                    for f in range(2):
                        dve.tensor_tensor(o[:, :, f], v[:, :, 1 - f],
                                          sn[:, f * 32:(f + 1) * 32].unsqueeze(1).broadcast_to([P, HEADS, 32]),
                                          ALU.mult).then_inc(s_rot, 1)

        @block.gpsimd
        def _(pool):
            pool.wait_ge(s_tab, 7)
            pool.wait_ge(s_trig, 16)
            rots = 0
            for m, n in enumerate(normed):
                c, t = work[n]
                b = m % 2
                pool.wait_ge(s_xr, m + 1)
                if m >= 4:
                    pool.wait_ge(s_st[m % 4], 16 * (m // 4))
                if t < NTX:
                    g = tabs[:, 2 * c - 2, t]
                else:
                    g = gq if c == 1 else vec[:, RQ + 2 * HD:RQ + 3 * HD]
                gb = g.unsqueeze(1).broadcast_to([P, HEADS, HD])
                o = res[m % 4].rearrange("p (h d) -> p h d", d=HD)
                pool.tensor_tensor(o, xr[b].rearrange("p (h d) -> p h d", d=HD), gb, ALU.mult)\
                    .then_inc(s_sin, 1)
                pool.wait_ge(s_sin, m + 1)
                if t < NTX:
                    rots += 2
                    pool.wait_ge(s_rot, rots)
                    pool.tensor_tensor(res[m % 4], res[m % 4], rot[b], ALU.add).then_inc(s_res, 1)
                else:
                    pool.sem_inc(s_res, 1)


def conv_branch(s, layer, last):
    nc, sem, place, vec, banks = s["nc"], s["sem"], s["place"], s["vec"], s["banks"]
    part = s["part"]
    HI, LO, YC = part(A_H, KD, TOK), part(A_X, KD, TOK), place(A_YC, 2, TOK)
    W = 3 * P
    wb = place(A_R, 2, KD, W)
    wlo, whi = part(A_R, 2, KD, W), part(A_R + 2 * KD * W, 2, KD, W)
    at = A_ATT + 4096 + 512
    UW = TOK + 4
    u = place(at, UW)
    xc = [place(at + UW + i * 512, 512) for i in range(2)]
    y = place(A_R + 4 * KD * W + 4096, TOK)
    ada_at = {}
    if layer == 0:
        ada = Modulations(s, FIRST_CHUNKS, CONV_CHUNKS, [place(A_ATT, KD, 512), place(A_R + 4 * KD * W, KD, 512)],
                          place(A_ATT + 4096, 512))
        ada_at = {3 * i // 2: i for i in range(CONV_CHUNKS)}
    spans = [(0, 512, 1), (512, 512, 1)] + ([] if last else [(1024, 256, 3)])
    work = [(j, sp) for j in range(2) for sp in spans]
    segs = [(0, SEQ, 0)] + ([] if last else [(SEQ, CTX, SEQ + 2)])
    s_w = [sem(f"w_conv_loaded_{i}") for i in range(4)]
    s_whi, s_wlo, s_mm, s_zero = sem("weights_hi"), sem("weights_lo"), sem("conv_product"), sem("conv_zeros")
    s_x, s_g, s_u, s_y = sem("conv_x"), sem("conv_gate"), sem("conv_u"), sem("conv_y")
    NW = len(spans)
    with nc.Block() as block:
        @block.sync
        def _(sp):
            s["clear_last"](sp)
            for i in range(4):
                rows = slice(i % 2 * 4, i % 2 * 4 + 4)
                sp.dma_start(wb[:, i // 2, rows], s["a"]["w_conv"][layer, :, i // 2, rows]).then_inc(s_w[i], 16)
            if layer == 0:
                for i in range(CONV_CHUNKS):
                    ada.load(sp, i)

        @block.tensor
        def _(pe):
            turn = None
            for n, (j, (t0, tn, _)) in enumerate(work):
                if n >= 2:
                    pe.wait_ge(s_g, n - 1)
                    pe.wait_ge(s_u, n - 1)
                for q in range(3):
                    cols = slice(q * P, (q + 1) * P)
                    for k in range(KD):
                        if n % NW == 0 and q == 0:
                            pe.wait_ge(s_whi, j * KD + k + 1)
                            pe.wait_ge(s_wlo, j * KD + k + 1)
                        mm = split_product(pe, banks[3 * (n % 2) + q][:, 0:tn], (whi[:, j, k, cols], wlo[:, j, k, cols]),
                                           (HI[:, k, t0:t0 + tn], LO[:, k, t0:t0 + tn]), k == 0, k == KD - 1)
                    mm.then_inc(s_mm, 1)
                    if turn is not None:
                        ada.turn(pe, turn)
                        turn = None
                    if 3 * n + q in ada_at:
                        turn = ada_at[3 * n + q]
                        ada.multiply(pe, turn)

        @block.scalar
        def _(act):
            for j in range(2):
                for k in range(KD):
                    if k % 4 == 0:
                        act.wait_ge(s_w[2 * j + k // 4], 16)
                    act.activation(whi[:, j, k], wb[:, j, k], ACT.Copy).then_inc(s_whi, 1)
            for n, (j, (t0, tn, _)) in enumerate(work):
                act.wait_ge(s_mm, 3 * n + 1)
                if n >= 2:
                    act.wait_ge(s_u, n - 1)
                act.activation(xc[n % 2][:, 0:tn], banks[3 * (n % 2)][:, 0:tn], ACT.Copy).then_inc(s_x, 1)
                act.wait_ge(s_mm, 3 * n + 2)
                act.activation(YC[:, j, t0:t0 + tn], banks[3 * (n % 2) + 1][:, 0:tn], ACT.Copy).then_inc(s_g, 1)
            act.wait_ge(s_g, len(work))

        @block.vector
        def _(dve):
            for j in range(2):
                for k in range(KD):
                    dve.wait_ge(s_whi, j * KD + k + 1)
                    dve.tensor_tensor(wlo[:, j, k], wb[:, j, k], whi[:, j, k].bitcast(F32), ALU.subtract)\
                        .then_inc(s_wlo, 1)
            dve.memset(u, 0.0).then_inc(s_zero, 1)
            dve.wait_ge(s_zero, 1)
            if layer == 0:
                ada.clear_rows(dve)
            keep = None
            done = Count(s_y)
            for n, (j, (t0, tn, off)) in enumerate(work):
                for q in range(3):
                    if q == 2:
                        dve.wait_ge(s_x, n + 1)
                        dve.wait_ge(s_mm, 3 * n + 3)
                        if n == NW:
                            dve.wait_ge(s_y, done.now())
                        dve.tensor_tensor(u[:, off + t0:off + t0 + tn], banks[3 * (n % 2) + 2][:, 0:tn],
                                          xc[n % 2][:, 0:tn], ALU.mult).then_inc(s_u, 1)
                    if keep is not None:
                        ada.keep(dve, keep)
                        keep = None
                    if 3 * n + q in ada_at:
                        keep = ada_at[3 * n + q]
                        ada.copy(dve, keep)
                if n % NW < NW - 1:
                    continue
                dve.wait_ge(s_u, n + 1)
                for t0, tn, off in segs:
                    w = [vec[:, V_CONV + layer * 6 + j * 3 + i:V_CONV + layer * 6 + j * 3 + i + 1] for i in range(3)]
                    yy = y[:, t0:t0 + tn]
                    if done.n:
                        dve.wait_ge(s_y, done.now())
                    done.up(dve.tensor_scalar(yy, u[:, off:off + tn], w[0], None, ALU.mult))
                    for i in (1, 2):
                        dve.wait_ge(s_y, done.now())
                        done.up(dve.scalar_tensor_tensor(yy, u[:, off + i:off + i + tn], w[i], yy,
                                                         ALU.mult, ALU.add))
                    dve.wait_ge(s_y, done.now())
                    dve.wait_ge(s_g, n + 1)
                    done.up(dve.tensor_tensor(YC[:, j, t0:t0 + tn], yy, YC[:, j, t0:t0 + tn], ALU.mult))
            if layer == 0:
                dve.wait_ge(ada.kept, CONV_CHUNKS)
            dve.wait_ge(s_y, done.now())


def fourier_branch(s, layer, last):
    nc, sem, place, banks = s["nc"], s["sem"], s["place"], s["banks"]
    U, FT = place(A_U, NT, F_WIDTH), place(A_FT, 2, TOK)
    at = A_R
    cb = [place(at + i * 4096, NTX, 512) for i in range(2)]
    at += 8192
    small = place(at, 4, P)
    dctx = place(at + 512, 2, 2, CTX)
    ab = place(at + 1536, 4, 512)
    s_c = [sem("dft_loaded_even"), sem("dft_loaded_odd")]
    s_small, s_mm, s_ab, s_fm, s_f = sem("dft_small_loaded"), sem("dft_product"), sem("dft_copied"), \
        sem("dft_channels"), sem("ft_copied")
    spans = [(0, 0, 512), (1, 512, 512)] + ([] if last else [(2, 1024, 256)])
    modulate = layer == 0
    if modulate:
        ada = Modulations(s, FIRST_CHUNKS + CONV_CHUNKS, FOURIER_CHUNKS,
                          [place(A_ATT, KD, 512), place(A_R + 12288, KD, 512)], place(A_ATT + 4096, 512))
    with nc.Block() as block:
        @block.sync
        def _(sp):
            s["clear_last"](sp)
            sp.dma_start(small, s["a"]["consts"][:, C_DFT:C_DFT + 4 * P].rearrange("p (a b) -> p a b", b=P))\
                .then_inc(s_small, 16)
            sp.dma_start(dctx, s["a"]["consts"][:, C_DCTX:C_DCTX + 4 * CTX]
                         .rearrange("p (a b c) -> p a b c", b=2, c=CTX)).then_inc(s_small, 16)
            for n in range(4):
                if n >= 2:
                    sp.wait_ge(s_mm, 2 * (n - 1))
                sp.dma_start(cb[n % 2], s["a"]["dft"][n]).then_inc(s_c[n % 2], 16)
                if modulate:
                    for i in range(2 * n, 2 * n + 2):
                        ada.load(sp, i)

        @block.tensor
        def _(pe):
            pe.wait_ge(s_small, 32)
            for g, t0, tn in spans:
                if g:
                    pe.wait_ge(s_ab, 4 * g)
                for w in range(2):
                    n = 2 * g + w
                    if g < 2:
                        pe.wait_ge(s_c[n % 2], 16 * (n // 2 + 1))
                    tiles = range(NTX) if g < 2 else range(2)
                    for ct in range(2):
                        for t in tiles:
                            rhs = cb[n % 2][:, t, :] if g < 2 else dctx[:, t, w, :]
                            mm = pe.matmul(banks[2 * w + ct][:, 0:tn],
                                           U[:, t + (NTX if g == 2 else 0), ct * P:(ct + 1) * P], rhs,
                                           start=t == 0, stop=t == len(tiles) - 1)
                        mm.then_inc(s_mm, 1)
                        i = 4 * g + 2 * w + ct
                        if modulate and i <= FOURIER_CHUNKS:
                            if i:
                                ada.turn(pe, i - 1)
                            if i < FOURIER_CHUNKS:
                                ada.multiply(pe, i)
                pe.wait_ge(s_ab, 4 * g + 4)
                if g:
                    pe.wait_ge(s_f, 2 * g)
                for ct in range(2):
                    for w in range(2):
                        mm = pe.matmul(banks[4 + ct][:, 0:tn], small[:, (2 if g == 2 else 0) + w, :],
                                       ab[:, 2 * w + ct, 0:tn], start=w == 0, stop=w == 1)
                    mm.then_inc(s_fm, 1)

        @block.scalar
        def _(act):
            for g, t0, tn in spans:
                if g:
                    act.wait_ge(s_fm, 2 * g)
                for i in range(4):
                    act.wait_ge(s_mm, 4 * g + i + 1)
                    act.activation(ab[:, i, 0:tn], banks[i][:, 0:tn], ACT.Copy).then_inc(s_ab, 1)
            act.wait_ge(s_ab, 4 * len(spans))

        @block.vector
        def _(dve):
            if modulate:
                ada.clear_rows(dve)
            for g, t0, tn in spans:
                if modulate:
                    for i in range(4 * g, min(4 * g + 4, FOURIER_CHUNKS + 1)):
                        if i:
                            ada.keep(dve, i - 1)
                        if i < FOURIER_CHUNKS:
                            ada.copy(dve, i)
                for ct in range(2):
                    dve.wait_ge(s_fm, 2 * g + ct + 1)
                    dve.tensor_copy(FT[:, ct, t0:t0 + tn], banks[4 + ct][:, 0:tn]).then_inc(s_f, 1)
            dve.wait_ge(s_f, 2 * len(spans))
            if modulate:
                dve.wait_ge(ada.kept, FOURIER_CHUNKS)


def attention(s, layer, last):
    nc, sem, place, vec, banks = s["nc"], s["sem"], s["place"], s["vec"], s["banks"]
    ATT = place(A_ATT, PAIRS, TOK)
    at = A_R
    V = place(at, NT, NAW)
    VS = place(at + NT * NAW, NTX - 1, NAW)
    at += (2 * NT - 3) * NAW
    raw, tbl = place(at, RPB_R, GRID_W), place(at + 960, RPB_R, GRID_W)
    at += 1920
    QT, KT = place(at, TOK), place(at + TOK, TOK)
    qs, ks = place(at + 2 * TOK, NT, P), place(at + 3 * TOK, NT, P)
    at += 4 * TOK
    sc = [place(at + i * 512, 512) for i in range(2)]
    pr = [place(at + 1024 + i * 768, 768) for i in range(2)]
    pt = [place(at + 2560 + i * 768, 6, P) for i in range(2)]
    ao = [place(at + 4096 + i * HD, HD) for i in range(2)]
    at += 4096 + 2 * HD
    mask = place(at, GRID_W)
    st = place(at + GRID_W, 4, 8)
    zeros = place(ARENA - ZEROS, ZEROS)
    ident = s["ident"]
    NQ = NTX if last else NT
    NI = ROWS + (0 if last else CTX // GRID_W)
    groups = [(qs, QT, t, min(t + 4, NQ)) for t in range(0, NQ, 4)] + [(ks, KT, t, min(t + 4, NT)) for t in range(0, NT, 4)]
    G4, G5 = (len(groups) + 1) // 2, len(groups) // 2
    U4, U5 = G4 + ROWS, G5 + NI
    start = [min(max(r - WIN_R // 2, 0), ROWS - WIN_R) for r in range(ROWS)]
    s_v, s_qk, s_raw, s_mask = sem("v_loaded"), sem("qk_loaded"), sem("bias_loaded"), sem("mask_loaded")
    s_tbl, s_pe, s_dve = sem("bias_ready"), sem("tensor_passed"), sem("vector_passed")
    s_sc, s_mid, s_m, s_e, s_el = sem("scores"), sem("local_max"), sem("neg_max"), sem("probs"), sem("probs_local")
    s_t4, s_t5, s_b4, s_b5 = sem("bank4_filled"), sem("bank5_filled"), sem("bank4_copied"), sem("bank5_copied")
    s_zero, s_fill = sem("zeros"), sem("slots_filled")
    s_pv, s_o, s_tt, s_at, s_l = sem("weighted"), sem("normalised"), sem("out_turned"), sem("out_copied"), sem("inv")

    def v_tiles(n, pair):
        cols = bass.ds(pair * P, P)
        local = []
        if n < ROWS:
            src, t0 = (V, start[n] // 2) if start[n] % 2 == 0 else (VS, (start[n] - 1) // 2)
            local = [(j, src[:, t0 + j, cols]) for j in range(4)]
        return local + [(4 + j, V[:, NTX + j, cols]) for j in range(2)]

    with nc.Block() as block:
        @block.sync
        def _(sp):
            s["clear_last"](sp)
            sp.dma_start(mask, s["a"]["consts"][:, C_MASK:C_MASK + GRID_W]).then_inc(s_mask, 16)

            def load(pair):
                sp.dma_start(qs[:, 0:NQ], s["q_rows"][0:NQ * P, bass.ds(pair * P, P)]
                             .rearrange("(t p) d -> p t d", p=P)).then_inc(s_qk, 16)
                sp.dma_start(ks, s["k_rows"][:, bass.ds(pair * P, P)]
                             .rearrange("(t p) d -> p t d", p=P)).then_inc(s_qk, 16)

            def load_biases(pair):
                for h in range(2):
                    sp.dma_start(raw[h * 64:(h + 1) * 64],
                                 bass.AP(s["a"]["rpb"].tensor,
                                         pair * (2 * RPB_R * RPB_PAD) + (layer * HEADS + h) * RPB_R * RPB_PAD,
                                         [[1, GRID_W], [RPB_PAD, RPB_R], [1, GRID_W]])).then_inc(s_raw, 16)

            load(0)
            load_biases(0)
            sp.dma_start(V, s["v_rows"].rearrange("(t p) d -> p t d", p=P)).then_inc(s_v, 16)
            sp.dma_start(VS, s["v_rows"][GRID_W:SEQ - GRID_W].rearrange("(t p) d -> p t d", p=P)).then_inc(s_v, 16)
            if layer == 0:
                sp.wait_ge(s_zero, 1)
                rows = MAX_SLOTS // 3
                for r in range(3):
                    sp.dma_start(s["slots"][r * rows:(r + 1) * rows].rearrange("(p a) (b z) -> p (a b) z", p=P, z=ZEROS),
                                 zeros.unsqueeze(1).broadcast_to([P, rows * D // P // ZEROS, ZEROS]))\
                        .then_inc(s_fill, 16)
            with sp.Fori(0, PAIRS - 1) as i:
                sp.wait_ge(s_b4, i * U4 + (G4 + 1))
                sp.wait_ge(s_b5, i * U5 + (G5 + 1))
                load(i + 1)
                sp.wait_ge(s_tbl, i + 1)
                load_biases(i + 1)
            if layer == 0:
                sp.wait_ge(s_fill, 48)

        @block.gpsimd
        def _(pool):
            if layer == 0:
                pool.memset(zeros, 0.0).then_inc(s_zero, 1)
            pool.wait_ge(s_mask, 16)
            with pool.Fori(0, PAIRS) as i:
                pool.wait_ge(s_raw, i * 32 + 32)
                pool.wait_ge(s_m, i * NI + 1)
                pool.tensor_tensor(tbl, raw[:, :, ::-1], mask.unsqueeze(1).broadcast_to([P, RPB_R, GRID_W]),
                                   ALU.add).then_inc(s_tbl, 1)
            pool.wait_ge(s_tbl, PAIRS)

        @block.tensor
        def _(pe):
            pe.sem_inc(s_pv, 2)
            pe.sem_inc(s_tt, 2)
            with pe.Fori(0, PAIRS) as i:
                pe.wait_ge(s_qk, i * 32 + 32)
                for g, (src, dst, t0, t1) in enumerate(groups):
                    filled, copied, u = (s_t5, s_b5, i * U5 + g // 2) if g % 2 else (s_t4, s_b4, i * U4 + g // 2)
                    pe.wait_ge(copied, u + 1)
                    for t in range(t0, t1):
                        mm = pe.transpose(banks[4 + g % 2][:, (t - t0) * P:(t - t0 + 1) * P], src[:, t, :], ident[:])
                    mm.then_inc(filled, 1)
                pe.wait_ge(s_b4, i * U4 + (G4 + 1))
                pe.wait_ge(s_b5, i * U5 + (G5 + 1))
                for j in range(NI + 3):
                    if j < NI:
                        n = j
                        pe.wait_ge(s_e, i * NI + (n + 1))
                        q0 = n * GRID_W
                        apart(pe, s_pe)
                        for h in (0, 64):
                            if n < ROWS:
                                k0 = start[n] * GRID_W
                                pe.matmul(banks[n % 2][h:h + 64, :], QT[h:h + 64, q0:q0 + 64],
                                          KT[h:h + 64, k0:k0 + 512], start=True, stop=True)
                            mm = pe.matmul(banks[2 + n % 2][h:h + 64, 0:CTX], QT[h:h + 64, q0:q0 + 64],
                                           KT[h:h + 64, SEQ:TOK], start=True, stop=True)
                        mm.then_inc(s_sc, 1)
                    if 1 <= j <= NI:
                        n = j - 1
                        pe.wait_ge(s_e, i * NI + (n + 3))
                        if n < ROWS:
                            pe.wait_ge(s_b4, i * U4 + (G4 + n + 1))
                            for k in range(4):
                                mm = pe.transpose(banks[4][:, k * P:(k + 1) * P], pr[n % 2][:, k * P:(k + 1) * P],
                                                  ident[:])
                            mm.then_inc(s_t4, 1)
                        pe.wait_ge(s_b5, i * U5 + (G5 + n + 1))
                        for k in range(2):
                            mm = pe.transpose(banks[5][:, k * P:(k + 1) * P], pr[n % 2][:, (4 + k) * P:(5 + k) * P],
                                              ident[:])
                        mm.then_inc(s_t5, 1)
                    if 2 <= j <= NI + 1:
                        n = j - 2
                        if n == 0:
                            pe.wait_ge(s_v, 32)
                        if n < ROWS:
                            pe.wait_ge(s_b4, i * U4 + (G4 + n + 2))
                        pe.wait_ge(s_b5, i * U5 + (G5 + n + 2))
                        pe.wait_ge(s_o, i * NI + (n + 1))
                        tiles = v_tiles(n, i)
                        for m, (k, v) in enumerate(tiles):
                            mm = pe.matmul(banks[6][:, 0:P], pt[n % 2][:, k, :], v, start=m == 0,
                                           stop=m == len(tiles) - 1)
                        mm.then_inc(s_pv, 1)
                    if j >= 3:
                        n = j - 3
                        pe.wait_ge(s_o, i * NI + (n + 2))
                        pe.wait_ge(s_at, i * NI + (n + 1))
                        apart(pe, s_pe)
                        pe.transpose(banks[7][0:HD, 0:P], ao[n % 2], ident[:]).then_inc(s_tt, 1)

        @block.vector
        def _(dve):
            dve.sem_inc(s_m, 1)
            dve.sem_inc(s_b5, 1)
            dve.sem_inc(s_o, 1)
            with dve.Fori(0, PAIRS) as i:
                for g, (src, dst, t0, t1) in enumerate(groups):
                    if g % 2:
                        dve.wait_ge(s_t5, i * U5 + (g // 2 + 1))
                        dve.tensor_copy(dst[:, t0 * P:t1 * P], banks[5][:, 0:(t1 - t0) * P]).then_inc(s_b5, 1)
                dve.wait_ge(s_b5, i * U5 + (G5 + 1))
                for j in range(NI + 2):
                    if j < NI:
                        n = j
                        x = st[:, n % 4]
                        dve.wait_ge(s_sc, i * NI + (n + 1))
                        dve.wait_ge(s_e, i * NI + (n + 1))
                        if n < ROWS:
                            if n == 0:
                                dve.wait_ge(s_tbl, i + 1)
                            d0 = start[n] - n + WIN_R - 1
                            apart(dve, s_dve)
                            dve.tensor_tensor_reduce(
                                out=sc[n % 2], in0=banks[n % 2][:],
                                in1=tbl[:, d0:d0 + WIN_R, :].rearrange("p a b -> p (a b)"), scale=1.0,
                                scalar=-3e38, op0=ALU.add, op1=ALU.max, accum_out=x[:, 0:1]).then_inc(s_mid, 1)
                        dve.tensor_reduce(x[:, 1:2], banks[2 + n % 2][:, 0:CTX], AX.X, ALU.max).then_inc(s_mid, 1)
                        dve.wait_ge(s_mid, i * (ROWS + NI) + (min(n + 1, ROWS) + n + 1))
                        if n < ROWS:
                            dve.tensor_scalar(x[:, 2:3], x[:, 1:2], x[:, 0:1], -1.0, ALU.max,
                                              ALU.mult).then_inc(s_m, 1)
                        else:
                            dve.tensor_scalar(x[:, 2:3], x[:, 1:2], -1.0, None, ALU.mult).then_inc(s_m, 1)
                    if 1 <= j <= NI:
                        n = j - 1
                        dve.wait_ge(s_t5, i * U5 + (G5 + n + 1))
                        dve.wait_ge(s_pv, i * NI + (n + 1))
                        dve.tensor_copy(pt[n % 2][:, 4:6, :].rearrange("p a b -> p (a b)"),
                                        banks[5][:, 0:CTX]).then_inc(s_b5, 1)
                    if j >= 2:
                        n = j - 2
                        x = st[:, n % 4]
                        if n < ROWS:
                            dve.tensor_tensor(x[:, 5:6], x[:, 3:4], x[:, 4:5], ALU.add).then_inc(s_l, 1)
                        else:
                            dve.tensor_copy(x[:, 5:6], x[:, 4:5]).then_inc(s_l, 1)
                        dve.wait_ge(s_l, i * (2 * NI) + (2 * n + 1))
                        dve.reciprocal(x[:, 6:7], x[:, 5:6]).then_inc(s_l, 1)
                        dve.wait_ge(s_l, i * (2 * NI) + (2 * n + 2))
                        dve.wait_ge(s_pv, i * NI + (n + 3))
                        dve.wait_ge(s_tt, i * NI + (n + 1))
                        dve.tensor_scalar(ao[n % 2][0:64], banks[6][0:64, 0:HD], x[0:64, 6:7], None, ALU.mult)
                        dve.tensor_scalar(ao[n % 2][64:128], banks[6][64:128, HD:2 * HD], x[64:128, 6:7], None,
                                          ALU.mult).then_inc(s_o, 1)

        @block.scalar
        def _(act):
            act.sem_inc(s_e, 2)
            act.sem_inc(s_b4, 1)
            act.sem_inc(s_at, 1)
            with act.Fori(0, PAIRS) as i:
                for g, (src, dst, t0, t1) in enumerate(groups):
                    if g % 2 == 0:
                        act.wait_ge(s_t4, i * U4 + (g // 2 + 1))
                        act.activation(dst[:, t0 * P:t1 * P], banks[4][:, 0:(t1 - t0) * P], ACT.Copy).then_inc(s_b4, 1)
                for j in range(NI + 3):
                    if j < NI:
                        n = j
                        x = st[:, n % 4]
                        act.wait_ge(s_m, i * NI + (n + 2))
                        if n >= 2:
                            act.wait_ge(s_t5, i * U5 + (G5 + n - 1))
                        if n < ROWS:
                            act.activation(pr[n % 2][:, 0:512], sc[n % 2], ACT.Exp, bias=x[:, 2:3],
                                           accum_out=x[:, 3:4]).then_inc(s_el, 1)
                            act.wait_ge(s_el, i * ROWS + (n + 1))
                        act.activation(pr[n % 2][:, 512:768], banks[2 + n % 2][:, 0:CTX], ACT.Exp, bias=x[:, 2:3],
                                       accum_out=x[:, 4:5]).then_inc(s_e, 1)
                    if 1 <= j <= ROWS:
                        n = j - 1
                        act.wait_ge(s_t4, i * U4 + (G4 + n + 1))
                        act.wait_ge(s_pv, i * NI + (n + 1))
                        act.activation(pt[n % 2][:, 0:4, :].rearrange("p a b -> p (a b)"), banks[4][:],
                                       ACT.Copy).then_inc(s_b4, 1)
                    if j >= 3:
                        n = j - 3
                        act.wait_ge(s_tt, i * NI + (n + 3))
                        for h in range(2):
                            cp = act.activation(ATT[h * 64:(h + 1) * 64, bass.ds(i, 1), n * 64:(n + 1) * 64],
                                                banks[7][0:HD, h * 64:(h + 1) * 64].unsqueeze(1), ACT.Copy)
                        cp.then_inc(s_at, 1)
            act.wait_ge(s_at, PAIRS * NI + 1)


def gates_and_merge(s, layer, last):
    nc, sem, place, banks, part = s["nc"], s["sem"], s["place"], s["banks"], s["part"]
    ATT, FT, YC = place(A_ATT, PAIRS, TOK), place(A_FT, 2, TOK), place(A_YC, 2, TOK)
    HI, LO = part(A_H, KD, TOK), part(A_X, KD, TOK)
    MERGED = place(A_R, KD, TOK)
    branches = [(FT, 2), (ATT, 4), (YC, 2)]
    at = A_R + KD * TOK
    wb = [place(at + q * 1536, KD + branches[q][1], P) for q in range(3)]
    wlo = [part(at + q * 1536, KD, P) for q in range(3)]
    whi = [part(at + 4608 + q * 1024, KD, P) for q in range(3)]
    at += 4608 + 3072
    sg = [place(at + i * 512, 512) for i in range(2)]
    prod = [place(at + 1024 + i * 512, 512) for i in range(2)]
    spans = [(0, 512), (512, 512)] + ([] if last else [(1024, 256)])
    NS = len(spans)
    s_w = [sem(f"gate_w_loaded_{q}") for q in range(3)]
    s_whi, s_wlo = sem("weights_hi"), sem("weights_lo")
    s_gm, s_bm, s_sg, s_pr, s_mg = sem("gate_product"), sem("branch_product"), sem("gate_ready"), sem("gated"), sem("merged")
    s_pool = sem("gpsimd_passed")
    U = 3 * NS
    work = [(q, span) for q in range(3) for span in range(NS)]

    def chunks(eng, body):
        with eng.Fori(0, KD - 3, 2) as i:
            for b in range(2):
                body(i, b, False)
        for b in range(2):
            body(KD - 2, b, b == 1)

    with nc.Block() as block:
        @block.sync
        def _(sp):
            s["clear_last"](sp)
            with sp.Fori(0, KD - 1, 2) as i:
                for b in range(2):
                    at = 0
                    for q in range(3):
                        n = KD + branches[q][1]
                        sp.wait_ge(s_bm, i * U + (b * U + (q + 1) * NS))
                        sp.dma_start(wb[q], s["a"]["w_gates"][layer, bass.ds(i + b, 1), :, at:at + n]
                                     .rearrange("o p k n -> p (o k) n")).then_inc(s_w[q], 16)
                        at += n

        @block.tensor
        def _(pe):
            pe.sem_inc(s_bm, U)
            with pe.Fori(0, KD - 1, 2) as i:
                for b in range(2):
                    for n, (q, span) in enumerate(work):
                        t0, tn = spans[span]
                        src, ks = branches[q]
                        if span == 0:
                            pe.wait_ge(s_w[q], i * 16 + (b * 16 + 16))
                            pe.wait_ge(s_whi, i * 3 + (b * 3 + q + 1))
                            pe.wait_ge(s_wlo, i * 3 + (b * 3 + q + 1))
                        pe.wait_ge(s_pr, i * U + (b * U + n + 1))
                        for k in range(KD):
                            mm = split_product(pe, banks[2 * (n % 3)][:, 0:tn], (whi[q][:, k, :], wlo[q][:, k, :]),
                                               (HI[:, k, t0:t0 + tn], LO[:, k, t0:t0 + tn]), k == 0, k == KD - 1)
                        mm.then_inc(s_gm, 1)
                        for k in range(ks):
                            mm = pe.matmul(banks[2 * (n % 3) + 1][:, 0:tn], wb[q][:, KD + k, :], src[:, k, t0:t0 + tn],
                                           start=k == 0, stop=k == ks - 1)
                        mm.then_inc(s_bm, 1)

        @block.scalar
        def _(act):
            def round_weights(i, q):
                act.wait_ge(s_w[q], i * 16 + 16)
                act.activation(whi[q], wb[q][:, 0:KD], ACT.Copy).then_inc(s_whi, 1)

            def body(i, b, final):
                for n, (q, span) in enumerate(work):
                    tn, m = spans[span][1], b * U + n
                    if span == 0 and not (final and q == 2):
                        round_weights(i + (b + (q + 1) // 3), (q + 1) % 3)
                    act.wait_ge(s_gm, i * U + (m + 1))
                    act.wait_ge(s_pr, i * U + (m + 2))
                    act.activation(sg[m % 2][:, 0:tn], banks[2 * (n % 3)][:, 0:tn], ACT.Sigmoid).then_inc(s_sg, 1)

            round_weights(0, 0)
            chunks(act, body)

        @block.vector
        def _(dve):
            def leave_weights(i, q):
                dve.wait_ge(s_whi, i * 3 + (q + 1))
                dve.tensor_tensor(wlo[q], wb[q][:, 0:KD], whi[q].bitcast(F32), ALU.subtract).then_inc(s_wlo, 1)

            def body(i, b, final):
                for n, (q, span) in enumerate(work):
                    (t0, tn), m = spans[span], b * U + n
                    if span == 0 and not (final and q == 2):
                        leave_weights(i + (b + (q + 1) // 3), (q + 1) % 3)
                    dve.wait_ge(s_sg, i * U + (m + 1))
                    dve.wait_ge(s_bm, i * U + (m + U + 1))
                    if q == 0:
                        to = MERGED[:, bass.ds(i + b, 1), t0:t0 + tn].rearrange("p o n -> p (o n)")
                    else:
                        c = b * 2 * NS + n - NS
                        to = prod[c % 2][:, 0:tn]
                        dve.wait_ge(s_mg, i * (2 * NS) + (c + 1))
                    dve.tensor_tensor(to, banks[2 * (n % 3) + 1][:, 0:tn], sg[m % 2][:, 0:tn], ALU.mult)\
                        .then_inc(s_pr, 1)

            dve.sem_inc(s_pr, 3)
            leave_weights(0, 0)
            chunks(dve, body)

        @block.gpsimd
        def _(pool):
            pool.sem_inc(s_mg, 2)
            with pool.Fori(0, KD - 1, 2) as i:
                for b in range(2):
                    for n, (q, span) in enumerate(work):
                        if q == 0:
                            continue
                        t0, tn = spans[span]
                        c = b * 2 * NS + n - NS
                        pool.wait_ge(s_pr, i * U + (b * U + n + 4))
                        pool.wait_ge(s_mg, i * (2 * NS) + (c + 2))
                        to = MERGED[:, bass.ds(i + b, 1), t0:t0 + tn].rearrange("p o n -> p (o n)")
                        apart(pool, s_pool)
                        pool.tensor_tensor(to, to, prod[c % 2][:, 0:tn], ALU.add).then_inc(s_mg, 1)
            pool.wait_ge(s_mg, 2 + KD * NS * 2)


def broadcast_columns(s, pe, columns, bank):
    for j, col in enumerate(columns):
        mm = pe.matmul(bank[:, j * P:(j + 1) * P], col.broadcast_to([P, P]), s["ident"][:], start=True, stop=True)
    return mm


def mixer_output(s, layer, last):
    nc, sem, place, mod, banks, part = s["nc"], s["sem"], s["place"], s["mod"], s["banks"], s["part"]
    X = place(A_X, NT, D)
    MERGED, MLO, MHI = place(A_R, KD, TOK), part(A_R, KD, TOK), part(A_H, KD, TOK)
    wo = place(A_R + KD * TOK, 2, KD, 512)
    wlo, whi = part(A_R + KD * TOK, 2, KD, 512), part(A_ATT, 2, KD, 512)
    g1 = place(A_ATT + 8192, 2, D)
    tmp = [place(A_R + KD * TOK + 8192 + i * 512, 512) for i in range(2)]
    NQ = NTX if last else NT
    work = [(h, t) for h in range(2) for t in range(NQ)]
    s_w = [sem(f"w_o_loaded_{i}") for i in range(4)]
    s_xl = sem("x_loaded")
    s_whi, s_wlo, s_mhi, s_mlo = sem("weights_hi"), sem("weights_lo"), sem("merged_hi"), sem("merged_lo")
    s_b, s_g, s_mm, s_t, s_x = sem("g1_rows"), sem("g1_copied"), sem("out_product"), sem("gated_out"), sem("x_updated")
    with nc.Block() as block:
        @block.sync
        def _(sp):
            s["clear_last"](sp)
            for i in range(4):
                rows = slice(i % 2 * 4, i % 2 * 4 + 4)
                sp.dma_start(wo[:, i // 2, rows], s["a"]["w_o"][layer, i // 2, :, rows]).then_inc(s_w[i], 16)
                if i == 1:
                    x = s["a"]["x"][0] if layer == 0 else s["x_rows"][0:SEQ]
                    sp.dma_start(X[:, 0:NTX], x.rearrange("(t p) d -> p t d", p=P)).then_inc(s_xl, 16)
                    if not last:
                        c = s["a"]["ctx"][0] if layer == 0 else s["x_rows"][SEQ:TOK]
                        sp.dma_start(X[:, NTX:NT], c.rearrange("(t p) d -> p t d", p=P)).then_inc(s_xl, 16)

        @block.tensor
        def _(pe):
            for w in range(2):
                for h in range(2):
                    cols = [mod[:, layer, 2 * KD + 4 * h + j, w:w + 1] for j in range(4)]
                    broadcast_columns(s, pe, cols, banks[4 + 2 * w + h]).then_inc(s_b, 1)
            for n, (h, t) in enumerate(work):
                if h == 0:
                    pe.wait_ge(s_mlo, t + 1)
                if n >= 4:
                    pe.wait_ge(s_t, n - 3)
                for k in range(KD):
                    if t == 0:
                        pe.wait_ge(s_wlo, h * KD + k + 1)
                    mm = split_product(pe, banks[n % 4][:], (MHI[:, k, t * P:(t + 1) * P], MLO[:, k, t * P:(t + 1) * P]),
                                       (whi[:, h, k, :], wlo[:, h, k, :]), k == 0, k == KD - 1)
                mm.then_inc(s_mm, 1)

        @block.scalar
        def _(act):
            def round_weights(h, k):
                if k % 4 == 0:
                    act.wait_ge(s_w[2 * h + k // 4], 16)
                act.activation(whi[:, h, k], wo[:, h, k], ACT.Copy).then_inc(s_whi, 1)

            def round_merged(t):
                act.activation(MHI[:, :, t * P:(t + 1) * P], MERGED[:, :, t * P:(t + 1) * P], ACT.Copy)\
                    .then_inc(s_mhi, 1)

            round_merged(0)
            round_merged(1)
            for w in range(2):
                for h in range(2):
                    act.wait_ge(s_b, 2 * w + h + 1)
                    act.activation(g1[:, w, h * 512:(h + 1) * 512], banks[4 + 2 * w + h][:], ACT.Copy)\
                        .then_inc(s_g, 1)
            for k in range(KD):
                round_weights(0, k)
            for t in range(2, NQ):
                round_merged(t)
            for k in range(KD):
                round_weights(1, k)

        @block.vector
        def _(dve):
            def leave_weights(h, k):
                dve.wait_ge(s_whi, h * KD + k + 1)
                dve.tensor_tensor(wlo[:, h, k], wo[:, h, k], whi[:, h, k].bitcast(F32), ALU.subtract)\
                    .then_inc(s_wlo, 1)

            for k in range(KD):
                leave_weights(0, k)
            dve.wait_ge(s_g, 4)
            for n, (h, t) in enumerate(work):
                if h == 0 and t < KD:
                    leave_weights(1, t)
                dve.wait_ge(s_mm, n + 1)
                if n >= 2:
                    dve.wait_ge(s_x, n - 1)
                dve.tensor_tensor(tmp[n % 2], banks[n % 4][:], g1[:, t // NTX, h * 512:(h + 1) * 512],
                                  ALU.mult).then_inc(s_t, 1)

        @block.gpsimd
        def _(pool):
            def leave_merged(t):
                pool.wait_ge(s_mhi, t + 1)
                pool.tensor_tensor(MLO[:, :, t * P:(t + 1) * P], MERGED[:, :, t * P:(t + 1) * P],
                                   MHI[:, :, t * P:(t + 1) * P].bitcast(F32), ALU.subtract).then_inc(s_mlo, 1)

            leave_merged(0)
            leave_merged(1)
            for n, (h, t) in enumerate(work):
                if n + 2 < NQ:
                    leave_merged(n + 2)
                if n == 0:
                    pool.wait_ge(s_xl, 16 if last else 32)
                pool.wait_ge(s_t, n + 1)
                xs = X[:, t, h * 512:(h + 1) * 512]
                pool.tensor_tensor(xs, xs, tmp[n % 2], ALU.add).then_inc(s_x, 1)
            pool.wait_ge(s_x, len(work))


def norm_and_route(s, layer, last):
    nc, sem, place, vec, mod, banks = s["nc"], s["sem"], s["place"], s["vec"], s["mod"], s["banks"]
    X, H2 = place(A_X, NT, D), place(A_H, NT, D)
    NQ = NTX if last else NT
    at = A_R - 5 * TOK
    mul, add = place(at, 2, D), place(at + 2 * D, 2, D)
    n2 = place(at + 4 * D, D)
    rw = place(at + 5 * D, KD, EXP)
    at += 5 * D + KD * EXP
    junk = place(at, D)
    HT2 = [place(at + D + i * D, KD, P) for i in range(2)]
    at += 3 * D
    sq, root, rstd = place(at, NT), place(at + 16, NT), place(at + 32, NT)
    at += 48
    W = NQ * EXP
    big = [place(at + i * NT * EXP, NQ, EXP) for i in range(10)]
    S, SB, MSK, OH1, OH2, M, T1, RANK, TOT, T2 = big
    at += 10 * NT * EXP
    sm = [place(at + i * 48, NQ * 4) for i in range(10)]
    at += 480
    tri = place(at, P)
    ones = place(at + P, P)
    thr = place(at + 2 * P, NT)
    blk = place(at + 2 * P + NT, 48)
    desc = place(at + 2 * P + NT + 48, EXP)
    at += 2 * P + NT + 48 + EXP
    cnt, nb, cum, cum2, base = (place(at + i * EXP, EXP) for i in range(5))
    cmp = place(at + 5 * EXP, EXP, NT)
    cmpb = place(at + 5 * EXP + EXP * NT, 48, EXP)
    be = place(at + 5 * EXP + EXP * NT + 48 * EXP, PLAN)
    fd = place(at + 5 * EXP + EXP * NT + 48 * EXP + PLAN, NQ)
    s_ld, s_sq, s_root, s_r, s_bc, s_bcc = sem("router_loaded"), sem("squares2"), sem("root2"), sem("rstd2"), \
        sem("mod2_rows"), sem("mod2_copied")
    s_a, s_h, s_tn, s_tc, s_lg, s_s = sem("rows_scaled2"), sem("h2_ready"), sem("h2_turned"), sem("h2_turned_copied"), \
        sem("logits"), sem("router_scores")
    s_c, s_pp, s_pc, s_idx, s_sent = sem("routing_step"), sem("ranks"), sem("ones_ready"), sem("slots_known"), \
        s["pool_dma_sem"]("rows_sent")
    s_sh, s_xst = sem("mod2_scale"), sem("x_stored")
    CM, CB = 4 * KD, 3 * KD
    sc2 = place(at + 5 * EXP + EXP * NT + 48 * EXP + PLAN + NT, KD, 2)
    with nc.Block() as block:
        @block.sync
        def _(sp):
            s["clear_last"](sp)
            sp.dma_start(n2, s["a"]["norm2_rows"][layer]).then_inc(s_ld, 16)
            sp.dma_start(rw, s["a"]["router_w"]).then_inc(s_ld, 16)
            c = s["a"]["consts"]
            sp.dma_start(tri, c[:, C_TRI:C_TRI + P]).then_inc(s_ld, 16)
            sp.dma_start(thr, c[:, C_THR:C_THR + NT]).then_inc(s_ld, 16)
            sp.dma_start(blk, c[:, C_BLK:C_BLK + 48]).then_inc(s_ld, 16)
            sp.dma_start(desc, c[:, C_DESC:C_DESC + EXP]).then_inc(s_ld, 16)
            sp.dma_start(s["x_rows"][0:NQ * P].rearrange("(t p) d -> p t d", p=P), X[:, 0:NQ]).then_inc(s_xst, 16)
            sp.wait_ge(s_xst, 16)

        @block.scalar
        def _(act):
            for t in range(NQ):
                if t:
                    act.wait_ge(s_sq, t)
                act.activation(junk, X[:, t], ACT.Square, accum_out=sq[:, t:t + 1]).then_inc(s_sq, 1)
            act.wait_ge(s_sq, NQ)
            act.activation(root[:, 0:NQ], sq[:, 0:NQ], ACT.Sqrt, bias=s["eps"][:, 0:1], scale=1.0 / D)\
                .then_inc(s_root, 1)
            for n in range(8):
                v, w, h = n // 4, n // 2 % 2, n % 2
                act.wait_ge(s_bc, n + 1)
                act.activation((mul, add)[v][:, w, h * 512:(h + 1) * 512], banks[n][:], ACT.Copy).then_inc(s_bcc, 1)
            for t in range(NQ):
                for h in range(2):
                    act.wait_ge(s_tn, 2 * t + h + 1)
                    if t >= 2:
                        act.wait_ge(s_lg, t - 1)
                    act.activation(HT2[t % 2][:, 4 * h:4 * h + 4].rearrange("p a b -> p (a b)"),
                                   banks[2 * (t % 2) + h][:], ACT.Copy).then_inc(s_tc, 1)
                if t >= 1:
                    act.wait_ge(s_lg, t)
                    act.activation(S[:, t - 1], banks[4 + (t - 1) % 2][:, 0:EXP], ACT.Sigmoid).then_inc(s_s, 1)
            act.wait_ge(s_lg, NQ)
            act.activation(S[:, NQ - 1], banks[4 + (NQ - 1) % 2][:, 0:EXP], ACT.Sigmoid).then_inc(s_s, 1)

        @block.tensor
        def _(pe):
            pe.wait_ge(s_sh, 1)
            for n in range(8):
                v, w, h = n // 4, n // 2 % 2, n % 2
                src = sc2 if v == 0 else mod[:, layer, CB:CB + KD, :]
                broadcast_columns(s, pe, [src[:, 4 * h + j, w:w + 1] for j in range(4)], banks[n]).then_inc(s_bc, 1)
            pe.wait_ge(s_bcc, 8)
            pe.wait_ge(s_ld, 96)
            for t in range(NQ + 1):
                if t < NQ:
                    pe.wait_ge(s_h, t + 1)
                    if t >= 2:
                        pe.wait_ge(s_tc, 2 * (t - 1))
                    for h in range(2):
                        for j in range(4):
                            mm = pe.transpose(banks[2 * (t % 2) + h][:, j * P:(j + 1) * P],
                                              H2[:, t, (4 * h + j) * P:(4 * h + j + 1) * P], s["ident"][:])
                        mm.then_inc(s_tn, 1)
                if t >= 1:
                    pe.wait_ge(s_tc, 2 * t)
                    if t >= 3:
                        pe.wait_ge(s_s, t - 2)
                    for k in range(KD):
                        mm = pe.matmul(banks[4 + (t - 1) % 2][:, 0:EXP], HT2[(t - 1) % 2][:, k, :], rw[:, k, :],
                                       start=k == 0, stop=k == KD - 1)
                    mm.then_inc(s_lg, 1)
            pe.wait_ge(s_pc, 1)
            flat = M.rearrange("p a b -> p (a b)")
            pe.matmul(banks[6][:, 0:W], tri, flat, start=True, stop=True).then_inc(s_pp, 1)
            pe.matmul(banks[7][:, 0:W], ones, flat, start=True, stop=True).then_inc(s_pp, 1)

        @block.vector
        def _(dve):
            dve.tensor_scalar(sc2, mod[:, layer, CM:CM + KD, :], 1.0, None, ALU.add).then_inc(s_sh, 1)
            dve.wait_ge(s_root, 1)
            dve.reciprocal(rstd[:, 0:NQ], root[:, 0:NQ]).then_inc(s_r, 1)
            dve.wait_ge(s_bcc, 8)
            dve.wait_ge(s_ld, 96)
            for w in range(2):
                dve.tensor_tensor(mul[:, w], mul[:, w], n2, ALU.mult).then_inc(s_r, 1)
            dve.wait_ge(s_r, 3)
            for t in range(NQ):
                w = t // NTX
                dve.scalar_tensor_tensor(H2[:, t], X[:, t], rstd[:, t:t + 1], mul[:, w], ALU.mult,
                                         ALU.mult).then_inc(s_a, 1)
            dve.wait_ge(s_s, NQ)
            step = Count(s_c)

            def do(instruction):
                step.up(instruction)
                dve.wait_ge(s_c, step.now())

            def over(x, n):
                return x.unsqueeze(2).broadcast_to([P, x.shape[1], n])

            g4 = [SB.rearrange("p t (g e) -> p (t g) e", e=4)[:, :, i] for i in range(4)]
            hi1, lo1, hi2, lo2, top, sec, grp, oh = sm[:8]
            one = sm[8][:, 0:NQ]
            two = sm[9][:, 0:NQ]
            do(dve.tensor_tensor(SB, S, vec[:, V_RB:V_RB + EXP].unsqueeze(1).broadcast_to([P, NQ, EXP]), ALU.add))
            do(dve.tensor_tensor(hi1, g4[0], g4[1], ALU.max))
            do(dve.tensor_tensor(lo1, g4[0], g4[1], ALU.min))
            do(dve.tensor_tensor(hi2, g4[2], g4[3], ALU.max))
            do(dve.tensor_tensor(lo2, g4[2], g4[3], ALU.min))
            do(dve.tensor_tensor(top, hi1, hi2, ALU.max))
            do(dve.tensor_tensor(sec, hi1, hi2, ALU.min))
            do(dve.tensor_tensor(lo1, lo1, lo2, ALU.max))
            do(dve.tensor_tensor(sec, sec, lo1, ALU.max))
            do(dve.tensor_tensor(grp, top, sec, ALU.add))
            g3 = grp.rearrange("p (t g) -> p t g", g=4)
            o3 = oh.rearrange("p (t g) -> p t g", g=4)
            do(dve.tensor_reduce(one, g3, AX.X, ALU.max))
            do(dve.tensor_tensor(o3, g3, over(one, 4), ALU.is_equal))
            do(dve.tensor_tensor(o3, o3, desc[:, 0:4].unsqueeze(1).broadcast_to([P, NQ, 4]), ALU.mult))
            do(dve.tensor_reduce(one, o3, AX.X, ALU.max))
            do(dve.tensor_tensor(o3, o3, over(one, 4), ALU.is_equal))
            m4 = oh.unsqueeze(2).broadcast_to([P, NQ * 4, 4])
            sb4 = SB.rearrange("p t (g e) -> p (t g) e", e=4)
            do(dve.tensor_tensor(sb4, sb4, m4, ALU.mult))
            do(dve.tensor_scalar(oh, oh, -NEG, NEG, ALU.mult, ALU.add))
            do(dve.tensor_tensor(sb4, sb4, m4, ALU.add))
            for OH in (OH1, OH2):
                do(dve.tensor_reduce(one, SB, AX.X, ALU.max))
                do(dve.tensor_tensor(OH, SB, over(one, EXP), ALU.is_equal))
                do(dve.tensor_tensor(OH, OH, desc.unsqueeze(1).broadcast_to([P, NQ, EXP]), ALU.mult))
                do(dve.tensor_reduce(one, OH, AX.X, ALU.max))
                do(dve.tensor_tensor(OH, OH, over(one, EXP), ALU.is_equal))
                if OH is OH1:
                    do(dve.scalar_tensor_tensor(SB, OH, 2 * NEG, SB, ALU.mult, ALU.add))
            step.up(dve.tensor_tensor(M, OH1, OH2, ALU.add))
            dve.wait_ge(s_c, step.now())
            dve.memset(ones, 1.0).then_inc(s_pc, 1)
            for j, OH in enumerate((OH1, OH2)):
                do(dve.tensor_tensor(T1, S, OH, ALU.mult))
                do(dve.tensor_reduce((one, two)[j], T1, AX.X, ALU.add))
            do(dve.tensor_tensor(fd, one, two, ALU.add))
            do(dve.reciprocal(fd, fd))
            do(dve.tensor_tensor(s["wts"][:, 0, 0:NQ], one, fd, ALU.mult))
            do(dve.tensor_tensor(s["wts"][:, 1, 0:NQ], two, fd, ALU.mult))
            dve.wait_ge(s_pp, 2)
            do(dve.tensor_copy(RANK.rearrange("p a b -> p (a b)"), banks[6][:, 0:W]))
            do(dve.tensor_copy(TOT.rearrange("p a b -> p (a b)"), banks[7][:, 0:W]))
            do(dve.tensor_copy(cnt, TOT[:, 0]))
            for t in range(1, NQ):
                do(dve.tensor_tensor(RANK[:, t], RANK[:, t], cnt, ALU.add))
                do(dve.tensor_tensor(cnt, cnt, TOT[:, t], ALU.add))
            do(dve.tensor_tensor(cmp, over(cnt, NT), thr.unsqueeze(1).broadcast_to([P, EXP, NT]), ALU.is_gt))
            do(dve.tensor_reduce(nb, cmp, AX.X, ALU.add))
            a, b = cum, cum2
            do(dve.tensor_copy(a, nb))
            for d in (1, 2, 4, 8):
                do(dve.tensor_copy(b[:, 0:d], a[:, 0:d]))
                do(dve.tensor_tensor(b[:, d:EXP], a[:, d:EXP], a[:, 0:EXP - d], ALU.add))
                a, b = b, a
            do(dve.tensor_tensor(base, a, nb, ALU.subtract))
            do(dve.tensor_scalar(base, base, float(P), None, ALU.mult))
            do(dve.tensor_scalar(cnt, nb, 1.0, None, ALU.min))
            do(dve.tensor_tensor(cnt, cnt, blk[:, 0:EXP], ALU.mult))
            do(dve.tensor_reduce(one[:, 0:1], cnt, AX.X, ALU.max))
            do(dve.tensor_tensor(cmpb, a.unsqueeze(1).broadcast_to([P, 48, EXP]), over(blk, EXP), ALU.is_le))
            do(dve.tensor_reduce(be[:, 0:48], cmpb, AX.X, ALU.add))
            do(dve.tensor_tensor(be[:, 0:48], be[:, 0:48], one[:, 0:1].broadcast_to([P, 48]), ALU.min))
            do(dve.tensor_copy(be[:, PLAN_USED:PLAN_USED + 1], a[:, EXP - 1:EXP]))
            do(dve.memset(be[:, PLAN_BEFORE:PLAN], 0.0))
            do(dve.tensor_tensor(cnt, a, a[:, EXP - 1:EXP].broadcast_to([P, EXP]), ALU.is_equal))
            do(dve.tensor_scalar(cnt, cnt, 2.0, None, ALU.mult))
            do(dve.tensor_tensor(be[:, PLAN_BEFORE + 2:PLAN_BEFORE + EXP], a[:, 0:EXP - 2], cnt[:, 0:EXP - 2],
                                 ALU.add))
            do(dve.tensor_copy(s["plan"][:], be[0:1, :]))
            do(dve.tensor_tensor(RANK, RANK, base.unsqueeze(1).broadcast_to([P, NQ, EXP]), ALU.add))
            for j, OH in enumerate((OH1, OH2)):
                do(dve.tensor_tensor(T1, RANK, OH, ALU.mult))
                do(dve.tensor_reduce(fd, T1, AX.X, ALU.add))
                do(dve.tensor_copy(s["dest"][:, j, 0:NQ], fd))
                dve.sem_inc(s_idx, 1)

        @block.gpsimd
        def _(pool):
            pool.wait_ge(s_bcc, 8)
            for t in range(NQ):
                pool.wait_ge(s_a, t + 1)
                pool.tensor_tensor(H2[:, t], H2[:, t], add[:, t // NTX], ALU.add).then_inc(s_h, 1)
            pool.wait_ge(s_h, NQ)
            for j in range(2):
                pool.wait_ge(s_idx, j + 1)
                for t in range(NQ):
                    pool.indirect_dma_start(
                        out=s["slots"][0:MAX_SLOTS], out_offset=bass.IndirectOffsetOnAxis(
                            s["dest"][:, j, t:t + 1], 0),
                        in_=H2[:, t], in_offset=None).then_inc(s_sent, 16)
            pool.wait_ge(s_sent, 16 * 2 * NQ)


def experts(s, layer, last):
    nc, sem, place, banks, part = s["nc"], s["sem"], s["place"], s["banks"], s["part"]
    MAXB = ((SEQ if last else TOK) * 2 + EXP * (P - 1)) // P
    ROUNDS = (MAXB + 1) // 2
    w13 = place(0, 2, 2 * KD, DE)
    wlo, whi = part(0, 2, 2 * KD, DE), part(16384, 2, 2 * KD, DE)
    w2 = place(32768, 2, DE // P, D)
    at = 40960
    xb = [place(at + i * D, D) for i in range(2)]
    at += 2 * D
    xhi, xlo = [part(at + i * D, KD, P) for i in range(2)], [part(at + (2 + i) * D, KD, P) for i in range(2)]
    xraw = [place(at + (2 + i) * D, KD, P) for i in range(2)]
    at += 4 * D
    yb = [place(at + i * D, D) for i in range(2)]
    at += 2 * D
    sl, h3, gl, gt = place(at, DE), place(at + DE, DE), place(at + 2 * DE, DE), place(at + 3 * DE, 4, P)
    plan = s["plan"]
    ident = s["ident"]
    PIECES = 4
    PK = 2 * KD // PIECES
    s_w13 = [[sem(f"w13_loaded_{b}_{i}") for i in range(PIECES)] for b in range(2)]
    s_w2 = [sem("w2_loaded_even"), sem("w2_loaded_odd")]
    s_whi, s_split = sem("w13_hi"), sem("w13_split")
    s_xb, s_yo = [sem("slots_loaded_even"), sem("slots_loaded_odd")], [sem("y_stored_even"), sem("y_stored_odd")]
    s_tx, s_xh, s_xl, s_h1, s_h3, s_sl, s_g = sem("slots_turned"), sem("slots_hi"), sem("slots_lo"), \
        sem("w1_product"), sem("w3_product"), sem("silu"), sem("gated")
    s_tg, s_gc, s_3c, s_done = sem("gated_turned"), sem("gated_copied"), sem("w3_product_copied"), sem("stores_done")
    s_y, s_yc = sem("w2_product"), sem("y_copied")

    def rounds(eng, body):
        used = eng.value_load(plan[0:1, PLAN_USED:PLAN_USED + 1], min_val=1, max_val=MAXB)
        with eng.Fori(0, ROUNDS) as r:
            with eng.If(used > r * 2):
                body(r)
        return used

    with nc.Block() as block:
        @block.sync
        def _(sp):
            s["clear_last"](sp)
            for b in range(2):
                sp.sem_inc(s_w2[b], 16)
            with sp.Fori(0, EXP - 1, 2) as e:
                for b in range(2):
                    before = sp.value_load(plan[0:1, bass.ds(e + (PLAN_BEFORE + b), 1)], min_val=0, max_val=MAXB + 2)
                    for i in range(PIECES):
                        if i % (PIECES // 2) == 0:
                            sp.wait_ge((s_h1, s_h3)[2 * i // PIECES], before + 1)
                        sp.dma_start(w13[:, b, i * PK:(i + 1) * PK],
                                     s["a"]["w13"][layer, bass.ds(e + b, 1), :, i * PK:(i + 1) * PK]
                                     .rearrange("o p k n -> p (o k) n")).then_inc(s_w13[b][i], 16)
                    sp.wait_ge(s_y, before * 2 + 2)
                    sp.dma_start(w2[:, b], s["a"]["w2"][layer, bass.ds(e + b, 1)]
                                 .rearrange("o p k n -> p (o k) n")).then_inc(s_w2[b], 16)
            for b in range(2):
                for i in range(PIECES):
                    sp.wait_ge(s_w13[b][i], 16 * (EXP // 2))
                sp.wait_ge(s_w2[b], 16 * (EXP // 2 + 1))

        @block.tensor
        def _(pe):
            pe.sem_inc(s_h1, 1)
            pe.sem_inc(s_h3, 1)
            pe.sem_inc(s_y, 2)

            def turn_slots(half, b, n):
                if half == 0:
                    pe.wait_ge(s_xb[b], n // 2 * 16 + 16)
                pe.wait_ge(s_xh, n * 4 + (2 * half + 2))
                for j in range(4):
                    mm = pe.transpose(banks[half][:, j * P:(j + 1) * P],
                                      xb[b][:, (4 * half + j) * P:(4 * half + j + 1) * P], ident[:])
                mm.then_inc(s_tx, 1)

            def up(a, b, e, slot):
                for k in range(KD):
                    if k % PK == 0:
                        pe.wait_ge(s_split, e * PIECES + ((a * KD + k) // PK + 1))
                    mm = split_product(pe, banks[2 + a][:], (xhi[b][:, k, :], xlo[b][:, k, :]),
                                       [w[:, bass.ds(slot, 1), a * KD + k, :].rearrange("p o n -> p (o n)")
                                        for w in (whi, wlo)], k == 0, k == KD - 1)
                mm.then_inc((s_h1, s_h3)[a], 1)

            for n in range(2):
                turn_slots(0, n, n)
                turn_slots(1, n, n)
            first = pe.value_load(plan[0:1, 0:1], min_val=0, max_val=EXP - 1)
            slot = pe.snap(first % 2, min_val=0, max_val=1)
            pe.wait_ge(s_xl, 2)
            pe.wait_ge(s_sl, 1)
            up(0, 0, first, slot)
            pe.wait_ge(s_3c, 1)
            up(1, 0, first, slot)

            def body(r):
                experts_of = [pe.value_load(plan[0:1, bass.ds(r * 2 + b, 1)], min_val=0, max_val=EXP - 1)
                              for b in range(3)]
                slots = [pe.snap(e % 2, min_val=0, max_val=1) for e in experts_of]
                for b in range(2):
                    e = experts_of[b]
                    evens, odds = pe.snap(e // 2 * 16 + 32), pe.snap((e + 1) // 2 * 16 + 16)
                    pe.wait_ge(s_xl, r * 4 + (2 * b + 4))
                    pe.wait_ge(s_sl, r * 2 + (b + 2))
                    up(0, 1 - b, experts_of[b + 1], slots[b + 1])
                    turn_slots(0, b, r * 2 + (b + 2))
                    pe.wait_ge(s_g, r * 2 + (b + 2))
                    pe.wait_ge(s_gc, r * 2 + (b + 1))
                    for j in range(4):
                        mm = pe.transpose(banks[4][:, j * P:(j + 1) * P], gl[:, j * P:(j + 1) * P], ident[:])
                    mm.then_inc(s_tg, 1)
                    pe.wait_ge(s_3c, r * 2 + (b + 2))
                    up(1, 1 - b, experts_of[b + 1], slots[b + 1])
                    turn_slots(1, b, r * 2 + (b + 2))
                    pe.wait_ge(s_w2[0], evens)
                    pe.wait_ge(s_w2[1], odds)
                    pe.wait_ge(s_gc, r * 2 + (b + 2))
                    for h in range(2):
                        pe.wait_ge(s_yc, r * 4 + (2 * b + h + 1))
                        for k in range(4):
                            mm = pe.matmul(banks[6 + h][:], gt[:, k, :],
                                           w2[:, bass.ds(slots[b], 1), k, h * 512:(h + 1) * 512]
                                           .rearrange("p o n -> p (o n)"), start=k == 0, stop=k == 3)
                        mm.then_inc(s_y, 1)
            used = rounds(pe, body)
            pe.wait_ge(s_h1, (used + 1) // 2 * 2 + 2)
            pe.wait_ge(s_h3, (used + 1) // 2 * 2 + 2)
            pe.wait_ge(s_y, (used + 1) // 2 * 4 + 2)
            pe.sem_inc(s_h1, 1)
            pe.sem_inc(s_h3, 1)
            pe.sem_inc(s_y, 4)

        @block.scalar
        def _(act):
            for b in range(2):
                act.dma_start(xb[b], s["slots"][b * P:(b + 1) * P]).then_inc(s_xb[b], 16)
                act.sem_inc(s_yo[b], 16)
            act.sem_inc(s_sl, 1)
            act.sem_inc(s_gc, 1)
            act.sem_inc(s_3c, 1)
            act.sem_inc(s_yc, 2)
            act.sem_inc(s_xh, 4)

            def copy_turned(half, b, n):
                act.wait_ge(s_tx, n * 2 + (half + 1))
                for to in (xraw[b], xhi[b]):
                    act.activation(to[:, 4 * half:4 * half + 4].rearrange("p a b -> p (a b)"), banks[half][:], ACT.Copy)\
                        .then_inc(s_xh, 1)

            def silu(n):
                act.wait_ge(s_h1, n + 2)
                act.wait_ge(s_g, n + 1)
                act.activation(sl, banks[2][:], ACT.Silu).then_inc(s_sl, 1)

            def copy_h3(n):
                act.wait_ge(s_h3, n + 2)
                act.wait_ge(s_g, n + 1)
                act.activation(h3, banks[3][:], ACT.Copy).then_inc(s_3c, 1)

            for n in range(2):
                copy_turned(0, n, n)
                copy_turned(1, n, n)
                act.dma_start(xb[n], s["slots"][(n + 2) * P:(n + 3) * P]).then_inc(s_xb[n], 16)
            silu(0)
            copy_h3(0)

            def body(r):
                for b in range(2):
                    silu(r * 2 + (b + 1))
                    copy_turned(0, b, r * 2 + (b + 2))
                    act.wait_ge(s_tg, r * 2 + (b + 1))
                    act.activation(gt.rearrange("p a b -> p (a b)"), banks[4][:], ACT.Copy).then_inc(s_gc, 1)
                    copy_h3(r * 2 + (b + 1))
                    copy_turned(1, b, r * 2 + (b + 2))
                    act.dma_start(xb[b], s["slots"][bass.ds(r * (2 * P) + (b + 4) * P, P)]).then_inc(s_xb[b], 16)
                    act.wait_ge(s_yo[b], r * 16 + 16)
                    for h in range(2):
                        act.wait_ge(s_y, r * 4 + (2 * b + h + 3))
                        act.activation(yb[b][:, h * 512:(h + 1) * 512], banks[6 + h][:], ACT.Copy).then_inc(s_yc, 1)
                    act.wait_ge(s_yc, r * 4 + (2 * b + 4))
                    act.dma_start(s["slots"][bass.ds(r * (2 * P) + b * P, P)], yb[b]).then_inc(s_yo[b], 16)
            used = rounds(act, body)
            for b in range(2):
                act.wait_ge(s_yo[b], ((used + 1) // 2) * 16 + 16)
                act.wait_ge(s_xb[b], ((used + 1) // 2) * 16 + 32)
            apart(act, s_done)

        @block.vector
        def _(dve):
            with dve.Fori(0, EXP - 1, 2) as e:
                for b in range(2):
                    for i in range(PIECES):
                        at = slice(i * PK, (i + 1) * PK)
                        dve.wait_ge(s_w13[b][i], e * 8 + 16)
                        dve.tensor_copy(whi[:, b, at], w13[:, b, at]).then_inc(s_whi, 1)
                        dve.wait_ge(s_whi, e * PIECES + (b * PIECES + i + 1))
                        dve.tensor_tensor(wlo[:, b, at], w13[:, b, at], whi[:, b, at].bitcast(F32), ALU.subtract)\
                            .then_inc(s_split, 1)
            dve.wait_ge(s_split, EXP * PIECES)

        @block.gpsimd
        def _(pool):
            pool.sem_inc(s_g, 1)

            def leave_turned(half, b, n):
                pool.wait_ge(s_xh, n * 4 + (2 * half + 6))
                at = slice(4 * half, 4 * half + 4)
                pool.tensor_tensor(xlo[b][:, at], xraw[b][:, at], xhi[b][:, at].bitcast(F32), ALU.subtract)\
                    .then_inc(s_xl, 1)

            def gate(n):
                pool.wait_ge(s_sl, n + 2)
                pool.wait_ge(s_3c, n + 2)
                pool.tensor_tensor(gl, h3, sl, ALU.mult).then_inc(s_g, 1)

            for n in range(2):
                leave_turned(0, n, n)
                leave_turned(1, n, n)
            gate(0)

            def body(r):
                for b in range(2):
                    leave_turned(0, b, r * 2 + (b + 2))
                    gate(r * 2 + (b + 1))
                    leave_turned(1, b, r * 2 + (b + 2))
            rounds(pool, body)


def combine(s, layer, last):
    nc, sem, place, mod, banks = s["nc"], s["sem"], s["place"], s["mod"], s["banks"]
    X = place(A_X, NT, D)
    NQ = NTX if last else NT
    g2 = place(A_H, 2, D)
    RING = 4
    Y = [place(A_H + 2 * D + i * 2 * D, 2, D) for i in range(RING)]
    t1 = [place(A_H + 10 * D + i * D, D) for i in range(2)]
    wts = s["wts"]
    s_y = [s["pool_dma_sem"](f"y_rows_{i}") for i in range(RING)]
    s_xl = sem("x_loaded")
    s_b, s_g, s_t1, s_t2, s_t3, s_x, s_out = sem("g2_rows"), sem("g2_copied"), sem("first_weighted"), \
        sem("both_weighted"), sem("gated_by_g2"), sem("x_done"), sem("out_stored")
    with nc.Block() as block:
        @block.tensor
        def _(pe):
            for w in range(2):
                for h in range(2):
                    cols = [mod[:, layer, 5 * KD + 4 * h + j, w:w + 1] for j in range(4)]
                    broadcast_columns(s, pe, cols, banks[2 * w + h]).then_inc(s_b, 1)

        @block.gpsimd
        def _(pool):
            def fetch(t):
                if t >= RING:
                    pool.wait_ge(s_t2, t - RING + 1)
                for j in range(2):
                    pool.indirect_dma_start(
                        out=Y[t % RING][:, j], out_offset=None, in_=s["slots"][0:MAX_SLOTS],
                        in_offset=bass.IndirectOffsetOnAxis(s["dest"][:, j, t:t + 1], 0)).then_inc(s_y[t % RING], 16)
            for t in range(RING):
                fetch(t)
            pool.wait_ge(s_xl, 16)
            for t in range(NQ):
                if t + RING < NQ:
                    fetch(t + RING)
                pool.wait_ge(s_t3, t + 1)
                pool.tensor_tensor(X[:, t], X[:, t], t1[t % 2], ALU.add).then_inc(s_x, 1)
            pool.wait_ge(s_x, NQ)

        @block.scalar
        def _(act):
            for w in range(2):
                for h in range(2):
                    act.wait_ge(s_b, 2 * w + h + 1)
                    act.activation(g2[:, w, h * 512:(h + 1) * 512], banks[2 * w + h][:], ACT.Copy).then_inc(s_g, 1)
            for t in range(NQ):
                act.wait_ge(s_y[t % RING], 32 * (t // RING + 1))
                if t >= 2:
                    act.wait_ge(s_x, t - 1)
                act.activation(t1[t % 2], Y[t % RING][:, 0], ACT.Copy, scale=wts[:, 0, t:t + 1]).then_inc(s_t1, 1)

        @block.vector
        def _(dve):
            dve.wait_ge(s_g, 4)
            for t in range(NQ):
                dve.wait_ge(s_t1, t + 1)
                dve.wait_ge(s_y[t % RING], 32 * (t // RING + 1))
                dve.scalar_tensor_tensor(t1[t % 2], Y[t % RING][:, 1], wts[:, 1, t:t + 1], t1[t % 2], ALU.mult,
                                         ALU.add).then_inc(s_t2, 1)
                dve.wait_ge(s_t2, t + 1)
                dve.tensor_tensor(t1[t % 2], t1[t % 2], g2[:, t // NTX], ALU.mult).then_inc(s_t3, 1)

        @block.sync
        def _(sp):
            s["clear_last"](sp)
            sp.dma_start(X[:, 0:NQ], s["x_rows"][0:NQ * P].rearrange("(t p) d -> p t d", p=P)).then_inc(s_xl, 16)
            to = s["out"][0] if last else s["x_rows"]
            for t in range(NQ):
                sp.wait_ge(s_x, t + 1)
                sp.dma_start(to[t * P:(t + 1) * P], X[:, t]).then_inc(s_out, 16)
            sp.wait_ge(s_out, 16 * NQ)



def _constants():
    c = np.zeros((P, C_TOTAL), np.float32)
    c[:, C_ID:C_ID + P] = np.eye(P)
    c[:, C_TRI:C_TRI + P] = np.triu(np.ones((P, P)), 1)
    col = np.arange(GRID_W)
    first = np.clip(col - WIN_C // 2, 0, GRID_W - WIN_C)
    inside = (col[None] >= first[:, None]) & (col[None] < first[:, None] + WIN_C)
    c[:, C_MASK:C_MASK + GRID_W] = np.tile(np.where(inside, 0.0, NEG), (2, 1))
    angle = 2 * np.pi * (np.outer(np.arange(64), np.arange(64)) % 64) / 64
    for i, length in enumerate((SEQ, CTX)):
        for j, m in enumerate((np.cos(angle), -np.sin(angle))):
            m = m / np.sqrt(length * 64)
            at = C_DFT + (2 * i + j) * P
            c[0:64, at:at + 64] = m
            c[64:128, at + 64:at + 128] = m
    angle = 2 * np.pi * (np.outer(np.arange(CTX), np.arange(CTX)) % CTX) / CTX
    d = np.stack([np.cos(angle), np.sin(angle)]).reshape(2, 2, P, CTX).transpose(2, 1, 0, 3)
    c[:, C_DCTX:C_DCTX + 4 * CTX] = d.reshape(P, 4 * CTX)
    c[:, C_THR:C_THR + NT] = P * np.arange(NT)
    c[:, C_BLK:C_BLK + 48] = np.arange(48)
    c[:, C_DESC:C_DESC + EXP] = 32 - np.arange(EXP)
    c[:, C_SEL:C_SEL + 2] = np.arange(P)[:, None] % 32 == np.arange(2)
    t = np.arange(SEQ)
    inv = np.power(np.float32(10000.0), -np.arange(HD // 4, dtype=np.float32) / np.float32(HD // 4))
    ang = np.concatenate([(t // GRID_W).astype(np.float32)[:, None] * inv,
                          (t % GRID_W).astype(np.float32)[:, None] * inv], 1).astype(np.float32)
    cos, sin = np.cos(ang), np.sin(ang)
    trig = np.stack([np.concatenate([cos, cos], 1), np.concatenate([-sin, sin], 1)])
    trig = trig.reshape(2, NTX, P, HD).transpose(2, 0, 1, 3).astype(np.float32)
    angle = 2 * np.pi * (np.outer(np.arange(SEQ), np.arange(SEQ)) % SEQ) / SEQ
    dft = np.stack([np.cos(angle), np.sin(angle)]).reshape(2, NTX, P, 2, 512).transpose(3, 0, 2, 1, 4)
    return c, trig, dft.reshape(4, P, NTX, 512).astype(np.float32)


def kernel(**inputs):
    import concourse.bacc as bacc
    from concourse.bass_utils import run_bass_kernel_spmd as run

    def arr(name):
        return np.asarray(inputs[name])

    def columns(v):
        return v.reshape(-1, P).T

    vectors = np.zeros((P, V_TOTAL), np.float32)
    vectors[:, V_C:V_C + 2 * KD:2] = columns(arr("c")[0])
    vectors[:, V_C + 1:V_C + 2 * KD:2] = columns(arr("c_ctx"))
    for layer in range(DEPTH):
        vectors[:, V_ADAB + layer * 48:V_ADAB + (layer + 1) * 48] = columns(arr("ada_b")[layer])
        vectors[:, V_N1 + layer * KD:V_N1 + (layer + 1) * KD] = columns(arr("norm1_g")[layer])
        cw = arr("conv_w")[layer].reshape(3, 2, P).transpose(2, 1, 0)
        vectors[:, V_CONV + layer * 6:V_CONV + (layer + 1) * 6] = cw.reshape(P, 6)
        for j, name in enumerate(("qn_g", "kn_g")):
            g = arr(name)[layer]
            at = V_QG + layer * 4 * HD + 2 * j * HD
            vectors[:, at:at + HD] = g
            vectors[:, at + HD:at + HD + 32] = g[32:]
            vectors[:, at + HD + 32:at + 2 * HD] = g[:32]
    vectors[:, V_RB:V_RB + EXP] = arr("router_b")
    consts, trig, dft = _constants()
    w_in = arr("w_in").reshape(DEPTH, KD, P, -1).transpose(0, 2, 1, 3)
    rows = [w_in[:, :, :, a:b].reshape(DEPTH, P, -1) for a, b in zip(KS[:4], KS[1:5])]
    w_conv = w_in[:, :, :, KS[4]:KS[5]].reshape(DEPTH, P, KD, 3, 2, P).transpose(0, 1, 4, 2, 3, 5)
    gates = w_in[:, :, :, KS[5]:].reshape(DEPTH, P, KD, 3, KD, P).transpose(0, 4, 1, 3, 2, 5)
    parts = []
    for q, (name, k) in enumerate((("w_f", 2), ("w_na", 4), ("w_cv", 2))):
        parts.append(gates[:, :, :, q])
        parts.append(arr(name).reshape(DEPTH, k, P, KD, P).transpose(0, 3, 2, 1, 4))
    rpb = np.zeros((DEPTH, HEADS, RPB_R, RPB_PAD), np.float32)
    rpb[..., GRID_W - WIN_C:GRID_W + WIN_C - 1] = arr("rpb")[..., ::-1]
    w13 = np.stack([arr(n).reshape(DEPTH, EXP, KD, P, DE).transpose(0, 1, 3, 2, 4) for n in ("w1", "w3")], 3)
    data = dict(
        x=arr("x"), ctx=arr("ctx"), vectors=vectors, consts=consts, trig=trig, dft=dft,
        ada_w=arr("ada_w").reshape(DEPTH, KD, P, 12, 512).transpose(0, 3, 2, 1, 4),
        w_rows=np.concatenate(rows, 2), w_conv=w_conv.reshape(DEPTH, P, 2, KD, 3 * P),
        w_gates=np.concatenate(parts, 3), rpb=rpb,
        w_o=arr("w_o").reshape(DEPTH, KD, P, 2, 512).transpose(0, 3, 2, 1, 4),
        norm2_rows=np.repeat(arr("norm2_g")[:, None], P, 1),
        router_w=arr("router_w").reshape(KD, P, EXP).transpose(1, 0, 2),
        w13=w13.reshape(DEPTH, EXP, P, 2 * KD, DE), w2=arr("w2").reshape(DEPTH, EXP, DE // P, P, D).transpose(0, 1, 3, 2, 4),
    )
    nc = bacc.Bacc("TRN2", target_bir_lowering=False, num_devices=1)
    feeds, aps = {}, {}
    for name, v in data.items():
        v = np.ascontiguousarray(v)
        feeds[f"in_{name}"] = v
        aps[name] = nc.dram_tensor(f"in_{name}", v.shape, mybir.dt.from_np(v.dtype), kind="ExternalInput").ap()
    out = nc.dram_tensor("out_x", (1, SEQ, D), F32, kind="ExternalOutput").ap()
    hybrid_backbone(nc, aps, out)
    return run(nc, [feeds], core_ids=[0]).results[0]["out_x"]
```

```python
import concourse.bass as bass
from concourse import mybir
from contextlib import ExitStack
import numpy as np

F32 = mybir.dt.float32
F32R = mybir.dt.float32r
I32 = mybir.dt.int32
ALU = mybir.AluOpType
ACT = mybir.ActivationFunctionType
AX = mybir.AxisListType

P = 128
D = 1024
DEPTH = 2
SEQ = 1024
CTX = 256
GRID_W = 64
ROWS = SEQ // GRID_W
EPS = 1e-6
KD = D // P
NTX = SEQ // P
NT = (SEQ + CTX) // P
TOK = SEQ + CTX
F_WIDTH = 256
HEADS = 8
HD = 64
NAW = HEADS * HD
PAIRS = HEADS // 2
WIN_R = 8
WIN_C = 16
RPB_R = 2 * WIN_R - 1
RPB_PAD = 128
CONV = 256
KS = (0, 256, 768, 1280, 1792, 2560)
EXP = 16
GROUPS = 4
DE = 512
NEG = -1e30

V_C = 0
V_ADAB = V_C + 2 * KD
V_N1 = V_ADAB + DEPTH * 48
V_CONV = V_N1 + DEPTH * KD
V_QG = V_CONV + DEPTH * 6
V_RB = V_QG + DEPTH * 4 * HD
V_TOTAL = V_RB + EXP
C_ID = 0
C_TRI = C_ID + P
C_MASK = C_TRI + P
C_DFT = C_MASK + GRID_W
C_DCTX = C_DFT + 4 * P
C_THR = C_DCTX + 4 * CTX
C_BLK = C_THR + NT
C_DESC = C_BLK + 48
C_SEL = C_DESC + EXP
C_ALT = C_SEL + 2
C_TOTAL = C_ALT + 2

ARENA = 52000
A_X = 0
A_H = A_X + NT * D
A_ATT = A_H + NT * D
A_FT = A_ATT + 4 * TOK
A_YC = A_FT + 2 * TOK
A_R = A_YC + 2 * TOK
A_U = ARENA - NT * F_WIDTH


class Count:

    def __init__(self, sem, base=0):
        self.sem, self.base, self.n = sem, base, 0

    def up(self, instruction, by=1):
        instruction.then_inc(self.sem, by)
        self.n += by
        return instruction

    def now(self):
        return self.base + self.n


def hybrid_backbone(nc, a, out):
    with ExitStack() as es:
        def sb(name, shape, dt=F32):
            return es.enter_context(nc.sbuf_tensor(name, shape, dt))

        banks = [es.enter_context(nc.psum_tensor(f"bank{i}", [P, 512], F32)) for i in range(8)]
        sb("arena", [P, ARENA])
        arena_base = nc.sbuf_base - 4 * ARENA
        vec = sb("vec", [P, V_TOTAL])
        mod = sb("mod", [P, DEPTH, 48, 2])
        scale1 = sb("scale1", [P, KD, 2])
        eps_col = sb("eps_col", [P, 1])
        ident = sb("ident", [P, P])
        silu = sb("silu", [P, KD, 2])
        select = sb("select", [P, 2])
        squares = sb("squares", [P, NT])
        state = dict(
            nc=nc, a=a, out=out, banks=banks, vec=vec, mod=mod, scale1=scale1, ident=ident, eps=eps_col,
            silu=silu, select=select, squares=squares,
            slots=nc.dram_tensor("slots", [MAX_SLOTS, D], F32).ap(),
            q_rows=nc.dram_tensor("q_rows", [TOK, NAW], F32).ap(),
            k_rows=nc.dram_tensor("k_rows", [TOK, NAW], F32).ap(),
            x_rows=nc.dram_tensor("x_rows", [TOK, D], F32).ap(),
            v_rows=nc.dram_tensor("v_rows", [TOK, NAW], F32).ap(),
            dest=sb("dest", [P, 2, NT], I32), wts=sb("wts", [P, 2, NT]),
            plan=sb("plan", [1, PLAN], I32),
        )

        first_sem = min(nc.free_semaphores)
        sets = [range(first_sem + i * STAGE_SEMS, first_sem + (i + 1) * STAGE_SEMS) for i in range(2)]
        names = {"stage": 0, "used": 0, "pool": 0}

        def sem(name):
            n = names["used"]
            names["used"] += 1
            assert n < STAGE_SEMS
            return stage_semaphores.enter_context(
                nc.semaphore(f"{name}_{names['stage']}", num=sets[names["stage"] % 2][n]))

        def pool_dma_sem(name):
            names["pool"] += 1
            return es.enter_context(nc.semaphore(f"{name}_{names['stage']}", num=sets[1][-1] + names["pool"]))

        def clear_last(sp):
            if names["stage"]:
                sp.sem_clear(sets[(names["stage"] + 1) % 2])

        def shaped(flat, dims):
            if len(dims) == 1:
                return flat
            if len(dims) == 2:
                return flat.rearrange("p (a b) -> p a b", b=dims[1])
            return flat.rearrange("p (a b c) -> p a b c", b=dims[1], c=dims[2])

        placed = {}

        def place(at, *dims, dtype=F32):
            skip = at % 8
            start, n = at - skip, int(np.prod(dims)) + skip
            assert start + n <= ARENA
            if (start, n, dtype) not in placed:
                kind = "part" if dtype == F32R else "place"
                placed[start, n, dtype] = nc.alloc_sbuf_tensor_at(f"{kind}_{start}_{n}", [P, n], dtype,
                                                                  offset=arena_base + 4 * start)
            return shaped(placed[start, n, dtype][:, skip:n], dims)

        def part(at, *dims):
            return place(at, *dims, dtype=F32R)

        state["part"] = part
        state["sem"], state["place"], state["clear_last"] = sem, place, clear_last
        state["pool_dma_sem"] = pool_dma_sem
        stages = [(load_and_modulations, ())]
        for layer in range(DEPTH):
            last = layer == DEPTH - 1
            stages += [(norm_for_mixers, (layer,))]
            stages += [(f, (layer, last)) for f in (project_rows, conv_branch, fourier_branch, attention,
                                                    gates_and_merge, mixer_output, norm_and_route, experts, combine)]
        for n, (stage, args) in enumerate(stages):
            names.update(stage=n, used=0)
            with ExitStack() as stage_semaphores:
                stage(state, *args)


STAGE_SEMS = 36
ZEROS = 256
MAX_SLOTS = 42 * P
PLAN_USED = 48
PLAN_BEFORE = 49
PLAN = 80


def split_product(pe, out, left, right, first, last):
    pe.matmul(out, left[0], right[0], start=first, stop=False)
    pe.matmul(out, left[0], right[1], start=False, stop=False)
    return pe.matmul(out, left[1], right[0], start=False, stop=last)


def apart(eng, passed):
    eng.sem_inc(passed, 1)


class Modulations:

    CH = 12

    def __init__(self, s, first, count, weights, rows):
        self.s, self.first, self.count, self.weights, self.rows = s, first, count, weights, rows
        sem = s["sem"]
        self.loaded = [sem(f"ada_w_loaded_{i}") for i in range(len(weights))]
        self.product, self.copied = sem("mod_product"), sem("mod_rows_copied")
        self.turned, self.kept = sem("mod_turned"), sem("mod_kept")

    def load(self, eng, i):
        layer, chunk = divmod(self.first + i, self.CH)
        b = i % len(self.weights)
        if i >= len(self.weights):
            eng.wait_ge(self.product, i - len(self.weights) + 1)
        eng.dma_start(self.weights[b], self.s["a"]["ada_w"][layer, chunk]).then_inc(self.loaded[b], 16)

    def clear_rows(self, dve):
        dve.memset(self.rows, 0.0).then_inc(self.copied, 1)
        dve.wait_ge(self.copied, 1)

    def multiply(self, pe, i):
        b = i % len(self.weights)
        pe.wait_ge(self.loaded[b], 16 * (i // len(self.weights) + 1))
        if i:
            pe.wait_ge(self.copied, 4 * i + 1)
        for h in range(KD // 4):
            for j in range(4):
                mm = pe.matmul(self.s["banks"][6][32 * j:32 * j + 2, :], self.s["silu"][:, 4 * h + j, :],
                               self.weights[b][:, 4 * h + j, :], start=h == 0, stop=h == KD // 4 - 1)
        mm.then_inc(self.product, 1)

    def copy(self, dve, i):
        dve.wait_ge(self.product, i + 1)
        if i:
            dve.wait_ge(self.turned, i)
        for j in range(4):
            dve.tensor_copy(self.rows[32 * j:32 * j + 2], self.s["banks"][6][32 * j:32 * j + 2, :])\
                .then_inc(self.copied, 1)

    def turn(self, pe, i):
        pe.wait_ge(self.copied, 4 * i + 5)
        if i:
            pe.wait_ge(self.kept, i)
        for t in range(4):
            mm = pe.matmul(self.s["banks"][7][:, 2 * t:2 * t + 2], self.rows[:, t * P:(t + 1) * P],
                           self.s["select"][:], start=True, stop=True)
        mm.then_inc(self.turned, 1)

    def keep(self, dve, i):
        layer, chunk = divmod(self.first + i, self.CH)
        dve.wait_ge(self.turned, i + 1)
        at = V_ADAB + layer * 48 + 4 * chunk
        dve.tensor_tensor(self.s["mod"][:, layer, 4 * chunk:4 * chunk + 4, :],
                          self.s["banks"][7][:, 0:8].rearrange("p (t w) -> p t w", w=2),
                          self.s["vec"][:, at:at + 4].unsqueeze(2).broadcast_to([P, 4, 2]), ALU.add)\
            .then_inc(self.kept, 1)


FIRST_CHUNKS = 4
CONV_CHUNKS = 16
FOURIER_CHUNKS = 2 * Modulations.CH - FIRST_CHUNKS - CONV_CHUNKS


def load_and_modulations(s):
    nc, sem, place, vec = s["nc"], s["sem"], s["place"], s["vec"]
    X = place(A_X, NT, D)
    ada = Modulations(s, 0, FIRST_CHUNKS, [place(A_H + i * 4096, KD, 512) for i in range(FIRST_CHUNKS)],
                      place(A_R + 4096, 512))
    junk = place(A_R + 8192, D)
    s_sq = sem("squares")
    s_vec, s_small, s_x, s_silu, s_eps = sem("vectors_loaded"), sem("small_loaded"), sem("x_loaded"), \
        sem("silu_done"), sem("eps_set")
    with nc.Block() as block:
        @block.sync
        def _(sp):
            s["clear_last"](sp)
            for i in range(FIRST_CHUNKS):
                ada.load(sp, i)

        @block.scalar
        def _(act):
            act.dma_start(vec[:], s["a"]["vectors"]).then_inc(s_vec, 16)
            act.dma_start(s["ident"][:], s["a"]["consts"][:, C_ID:C_ID + P]).then_inc(s_small, 16)
            act.dma_start(s["select"][:], s["a"]["consts"][:, C_SEL:C_SEL + 2]).then_inc(s_small, 16)
            act.dma_start(X[:, 0:NTX], s["a"]["x"][0].rearrange("(t p) d -> p t d", p=P)).then_inc(s_x, 16)
            act.dma_start(X[:, NTX:NT], s["a"]["ctx"][0].rearrange("(t p) d -> p t d", p=P)).then_inc(s_x, 16)
            act.wait_ge(s_vec, 16)
            act.activation(s["silu"][:], vec[:, V_C:V_C + 2 * KD].rearrange("p (k w) -> p k w", w=2),
                           ACT.Silu).then_inc(s_silu, 1)
            act.wait_ge(s_x, 32)
            for t in range(NT):
                if t:
                    act.wait_ge(s_sq, t)
                act.activation(junk, X[:, t], ACT.Square, accum_out=s["squares"][:, t:t + 1]).then_inc(s_sq, 1)
            act.wait_ge(s_sq, NT)
            act.wait_ge(s_small, 32)

        @block.tensor
        def _(pe):
            pe.wait_ge(s_silu, 1)
            pe.wait_ge(s_small, 32)
            for i in range(FIRST_CHUNKS):
                ada.multiply(pe, i)
                ada.turn(pe, i)

        @block.vector
        def _(dve):
            dve.memset(s["eps"][:], EPS).then_inc(s_eps, 1)
            ada.clear_rows(dve)
            dve.wait_ge(s_vec, 16)
            for i in range(FIRST_CHUNKS):
                ada.copy(dve, i)
                ada.keep(dve, i)
            dve.wait_ge(ada.kept, FIRST_CHUNKS)
            dve.wait_ge(s_eps, 1)


def norm_for_mixers(s, layer):
    nc, sem, place, vec, mod, banks = s["nc"], s["sem"], s["place"], s["vec"], s["mod"], s["banks"]
    X = place(A_X, NT, D)
    HT, HI, LO = place(A_X, KD, TOK), s["part"](A_H, KD, TOK), s["part"](A_X, KD, TOK)
    xn = place(A_R, NT, D)
    sq = s["squares"]
    root = place(A_ATT + 16, NT)
    rstd = place(A_ATT + 32, NT)
    scale1 = s["scale1"]
    groups = [(0, 4, 0), (4, 8, 0), (8, 10, 1)]
    work = [(k, t0, t1, w) for t0, t1, w in groups for k in range(KD)]
    s_root, s_rstd, s_sc = sem("root"), sem("rstd"), sem("scale1_done")
    s_xn, s_turn, s_hi, s_raw = sem("rows_scaled"), sem("turned"), sem("hi"), sem("turned_copied")
    s_lo, s_lo_odd = sem("lo"), sem("lo_odd")
    with nc.Block() as block:
        @block.sync
        def _(sp):
            s["clear_last"](sp)

        @block.scalar
        def _(act):
            act.activation(root, sq[:], ACT.Sqrt, bias=s["eps"][:, 0:1], scale=1.0 / D).then_inc(s_root, 1)
            act.wait_ge(s_sc, 2)
            for n, (k, t0, t1, w) in enumerate(work):
                act.wait_ge(s_turn, n + 1)
                act.activation(HI[:, k, t0 * P:t1 * P], banks[n % 8][:, 0:(t1 - t0) * P], ACT.Identity,
                               bias=mod[:, layer, k, w:w + 1], scale=scale1[:, k, w:w + 1]).then_inc(s_hi, 1)
            act.wait_ge(s_hi, len(work))

        @block.vector
        def _(dve):
            gain = vec[:, V_N1 + layer * KD:V_N1 + (layer + 1) * KD]
            dve.tensor_scalar(scale1[:], mod[:, layer, KD:2 * KD, :], 1.0, None, ALU.add).then_inc(s_sc, 1)
            dve.wait_ge(s_sc, 1)
            dve.tensor_tensor(scale1[:], scale1[:], gain.unsqueeze(2).broadcast_to([P, KD, 2]),
                              ALU.mult).then_inc(s_sc, 1)
            dve.wait_ge(s_root, 1)
            dve.reciprocal(rstd, root).then_inc(s_rstd, 1)
            dve.wait_ge(s_rstd, 1)
            dve.wait_ge(s_sc, 2)
            for t in range(NT):
                dve.tensor_scalar(xn[:, t], X[:, t], rstd[:, t:t + 1], None, ALU.mult).then_inc(s_xn, 1)
            dve.wait_ge(s_xn, NT)
            def leave(n):
                k, t0, t1, _ = work[n]
                dve.wait_ge(s_raw, n + 1)
                dve.tensor_tensor(LO[:, k, t0 * P:t1 * P], HT[:, k, t0 * P:t1 * P],
                                  HI[:, k, t0 * P:t1 * P].bitcast(F32), ALU.subtract).then_inc(s_lo_odd, 1)

            for n, (k, t0, t1, w) in enumerate(work):
                dve.wait_ge(s_hi, n + 1)
                dve.tensor_scalar(HT[:, k, t0 * P:t1 * P], banks[n % 8][:, 0:(t1 - t0) * P],
                                  scale1[:, k, w:w + 1], mod[:, layer, k, w:w + 1],
                                  ALU.mult, ALU.add).then_inc(s_raw, 1)
                if n and n % 2 == 0:
                    leave(n - 1)
            leave(len(work) - 1)
            dve.wait_ge(s_lo_odd, len(work) // 2)

        @block.gpsimd
        def _(pool):
            for n, (k, t0, t1, w) in list(enumerate(work))[::2]:
                pool.wait_ge(s_hi, n + 1)
                pool.wait_ge(s_raw, n + 1)
                pool.tensor_tensor(LO[:, k, t0 * P:t1 * P], HT[:, k, t0 * P:t1 * P],
                                   HI[:, k, t0 * P:t1 * P].bitcast(F32), ALU.subtract).then_inc(s_lo, 1)
            pool.wait_ge(s_lo, len(work) // 2)

        @block.tensor
        def _(pe):
            for n, (k, t0, t1, w) in enumerate(work):
                pe.wait_ge(s_xn, t1)
                if n >= 8:
                    pe.wait_ge(s_raw, n - 7)
                for t in range(t0, t1):
                    mm = pe.transpose(banks[n % 8][:, (t - t0) * P:(t - t0 + 1) * P],
                                      xn[:, t, k * P:(k + 1) * P], s["ident"][:])
                mm.then_inc(s_turn, 1)


def project_rows(s, layer, last):
    nc, sem, place, vec, banks = s["nc"], s["sem"], s["place"], s["vec"], s["banks"]
    part = s["part"]
    HI, LO, U = part(A_H, KD, TOK), part(A_X, KD, TOK), place(A_U, NT, F_WIDTH)
    at = A_ATT
    wb = [place(at + i * 4096, KD, 512) for i in range(2)]
    wlo = [part(at + i * 4096, KD, 512) for i in range(2)]
    whi = [part(at + 8192 + i * 4096, KD, 512) for i in range(2)]
    at += 16384
    trig = place(at, 2, NTX, HD)
    tabs = place(at + 1024, 4, NTX, HD)
    gq = place(at + 3072, HD)
    at += 3136
    sqb = [place(at + i * 512, 512) for i in range(2)]
    xr = [place(at + 1024 + i * 512, 512) for i in range(2)]
    rot = [place(at + 2048 + i * 512, 512) for i in range(2)]
    res = [place(at + 3072 + i * 512, 512) for i in range(4)]
    ssum = place(at + 5120, 2, HEADS)
    root = place(at + 5136, 2, HEADS)
    rinv = place(at + 5152, 2, HEADS)
    chunks = []
    for c in range(4):
        chunks.append((c, list(range(NTX if last and c < 2 else NT))))
    work = [(c, t) for c, ts in chunks for t in ts]
    normed = [n for n, (c, t) in enumerate(work) if c in (1, 2)]
    s_w = [sem(f"w_in_{'FQKV'[c]}_loaded") for c in range(4)]
    s_trig, s_tab, s_mm = sem("trig_loaded"), sem("tables"), sem("row_product")
    s_free = sem("row_bank_free")
    s_sq, s_ss, s_rt, s_ri, s_xr = sem("q_squared"), sem("q_sums"), sem("q_root"), sem("q_rinv"), sem("q_scaled")
    s_rot, s_res, s_vc = sem("q_rot"), sem("qk_rows"), sem("v_rows")
    s_st = [sem(f"stored_{i}") for i in range(4)]
    s_sin = sem("q_sin")
    s_whi, s_wlo = sem("weights_hi"), sem("weights_lo")
    width = [256, 512, 512, 512]
    vwork = [n for n, (c, t) in enumerate(work) if c == 3]
    RQ = V_QG + layer * 4 * HD

    with nc.Block() as block:
        @block.sync
        def _(sp):
            s["clear_last"](sp)
            w = s["a"]["w_rows"]

            def load(c):
                if c >= 2:
                    sp.wait_ge(s_mm, sum(len(ts) for _, ts in chunks[:c - 1]))
                n = width[c]
                sp.dma_start(wb[c % 2][:, :, 0:n], w[layer, :, KS[c] * KD:KS[c] * KD + n * KD]
                             .rearrange("p (k n) -> p k n", k=KD)).then_inc(s_w[c], 16)

            load(0)
            sp.dma_start(trig, s["a"]["trig"]).then_inc(s_trig, 16)
            load(1)
            load(2)
            for m, n in enumerate(normed):
                if n == sum(len(ts) for _, ts in chunks[:2]):
                    load(3)
                sp.wait_ge(s_res, m + 1)
                c, t = work[n]
                sp.dma_start(s["q_rows" if c == 1 else "k_rows"][t * P:(t + 1) * P], res[m % 4])\
                    .then_inc(s_st[m % 4], 16)
            for m, n in enumerate(vwork):
                sp.wait_ge(s_vc, m + 1)
                sp.dma_start(s["v_rows"][work[n][1] * P:(work[n][1] + 1) * P], res[m % 4]).then_inc(s_st[m % 4], 16)
            for q in range(4):
                sp.wait_ge(s_st[q], 16 * (len(range(q, len(normed), 4)) + len(range(q, len(vwork), 4))))

        @block.tensor
        def _(pe):
            for n, (c, t) in enumerate(work):
                if n >= 6:
                    was = work[n - 6][0]
                    done = sum(1 for k, _ in work[:n - 5] if k == was or {k, was} == {1, 2})
                    pe.wait_ge({0: s_free, 1: s_xr, 2: s_xr, 3: s_vc}[was], done)
                w = width[c]
                for k in range(KD):
                    if t == 0:
                        pe.wait_ge(s_whi, c * KD + k + 1)
                        pe.wait_ge(s_wlo, c * KD + k + 1)
                    mm = split_product(pe, banks[n % 6][:, 0:w],
                                       (HI[:, k, t * P:(t + 1) * P], LO[:, k, t * P:(t + 1) * P]),
                                       (whi[c % 2][:, k, 0:w], wlo[c % 2][:, k, 0:w]), k == 0, k == KD - 1)
                mm.then_inc(s_mm, 1)

        @block.scalar
        def _(act):
            def round_weights(c, k):
                if k == 0:
                    act.wait_ge(s_w[c], 16)
                act.activation(whi[c % 2][:, k, 0:width[c]], wb[c % 2][:, k, 0:width[c]], ACT.Copy)\
                    .then_inc(s_whi, 1)

            for k in range(KD):
                round_weights(0, k)
            nq = nv = 0
            for n, (c, t) in enumerate(work):
                if c < 3 and t < KD:
                    round_weights(c + 1, t)
                act.wait_ge(s_mm, n + 1)
                if c == 0:
                    act.activation(U[:, t], banks[n % 6][:, 0:256], ACT.Copy).then_inc(s_free, 1)
                elif c == 3:
                    m = nv
                    act.wait_ge(s_st[m % 4], 16 * (len(range(m % 4, len(normed), 4)) + m // 4))
                    act.activation(res[m % 4], banks[n % 6][:], ACT.Copy).then_inc(s_vc, 1)
                    nv += 1
                else:
                    if nq >= 2:
                        act.wait_ge(s_ss, nq - 1)
                    act.activation(sqb[nq % 2], banks[n % 6][:], ACT.Square).then_inc(s_sq, 1)
                    act.wait_ge(s_ss, nq + 1)
                    act.activation(root[:, nq % 2], ssum[:, nq % 2], ACT.Sqrt, bias=s["eps"][:, 0:1],
                                   scale=1.0 / HD).then_inc(s_rt, 1)
                    nq += 1

        @block.vector
        def _(dve):
            def leave_weights(c, k):
                dve.wait_ge(s_whi, c * KD + k + 1)
                dve.tensor_tensor(wlo[c % 2][:, k, 0:width[c]], wb[c % 2][:, k, 0:width[c]],
                                  whi[c % 2][:, k, 0:width[c]].bitcast(F32), ALU.subtract).then_inc(s_wlo, 1)

            for k in range(KD):
                leave_weights(0, k)
            dve.wait_ge(s_trig, 16)
            dve.tensor_scalar(gq, vec[:, RQ:RQ + HD], HD ** -0.5, None, ALU.mult).then_inc(s_tab, 1)
            for j in range(4):
                g = vec[:, RQ + j * HD:RQ + (j + 1) * HD].unsqueeze(1).broadcast_to([P, NTX, HD])
                if j < 2:
                    dve.tensor_scalar(tabs[:, j], trig[:, j % 2], HD ** -0.5, None, ALU.mult).then_inc(s_tab, 1)
                    dve.wait_ge(s_tab, 2 + 2 * j)
                    dve.tensor_tensor(tabs[:, j], tabs[:, j], g, ALU.mult).then_inc(s_tab, 1)
                else:
                    dve.tensor_tensor(tabs[:, j], trig[:, j % 2], g, ALU.mult).then_inc(s_tab, 1)
            dve.wait_ge(s_tab, 7)
            for k in range(KD):
                leave_weights(1, k)
            for m, n in enumerate(normed):
                c, t = work[n]
                b = m % 2
                if t < KD:
                    leave_weights(c + 1, t)
                dve.wait_ge(s_sq, m + 1)
                if m >= 2:
                    dve.wait_ge(s_rt, m - 1)
                dve.tensor_reduce(ssum[:, b], sqb[b].rearrange("p (h d) -> p h d", d=HD), AX.X,
                                  ALU.add).then_inc(s_ss, 1)
                dve.wait_ge(s_rt, m + 1)
                dve.reciprocal(rinv[:, b], root[:, b]).then_inc(s_ri, 1)
                dve.wait_ge(s_ri, m + 1)
                if m >= 2:
                    dve.wait_ge(s_res, m - 1)
                dve.tensor_tensor(xr[b].rearrange("p (h d) -> p h d", d=HD),
                                  banks[n % 6][:].rearrange("p (h d) -> p h d", d=HD),
                                  rinv[:, b].unsqueeze(2).broadcast_to([P, HEADS, HD]), ALU.mult).then_inc(s_xr, 1)
                dve.wait_ge(s_xr, m + 1)
                if t < NTX:
                    sn = tabs[:, 2 * c - 1, t]
                    v = xr[b].rearrange("p (h f d) -> p h f d", h=HEADS, f=2)
                    o = rot[b].rearrange("p (h f d) -> p h f d", h=HEADS, f=2)
                    for f in range(2):
                        dve.tensor_tensor(o[:, :, f], v[:, :, 1 - f],
                                          sn[:, f * 32:(f + 1) * 32].unsqueeze(1).broadcast_to([P, HEADS, 32]),
                                          ALU.mult).then_inc(s_rot, 1)

        @block.gpsimd
        def _(pool):
            pool.wait_ge(s_tab, 7)
            pool.wait_ge(s_trig, 16)
            rots = 0
            for m, n in enumerate(normed):
                c, t = work[n]
                b = m % 2
                pool.wait_ge(s_xr, m + 1)
                if m >= 4:
                    pool.wait_ge(s_st[m % 4], 16 * (m // 4))
                if t < NTX:
                    g = tabs[:, 2 * c - 2, t]
                else:
                    g = gq if c == 1 else vec[:, RQ + 2 * HD:RQ + 3 * HD]
                gb = g.unsqueeze(1).broadcast_to([P, HEADS, HD])
                o = res[m % 4].rearrange("p (h d) -> p h d", d=HD)
                pool.tensor_tensor(o, xr[b].rearrange("p (h d) -> p h d", d=HD), gb, ALU.mult)\
                    .then_inc(s_sin, 1)
                pool.wait_ge(s_sin, m + 1)
                if t < NTX:
                    rots += 2
                    pool.wait_ge(s_rot, rots)
                    pool.tensor_tensor(res[m % 4], res[m % 4], rot[b], ALU.add).then_inc(s_res, 1)
                else:
                    pool.sem_inc(s_res, 1)


def conv_branch(s, layer, last):
    nc, sem, place, vec, banks = s["nc"], s["sem"], s["place"], s["vec"], s["banks"]
    part = s["part"]
    HI, LO, YC = part(A_H, KD, TOK), part(A_X, KD, TOK), place(A_YC, 2, TOK)
    W = 3 * P
    wb = place(A_R, 2, KD, W)
    wlo, whi = part(A_R, 2, KD, W), part(A_R + 2 * KD * W, 2, KD, W)
    at = A_ATT + 4096 + 512
    UW = TOK + 4
    u = place(at, UW)
    xc = [place(at + UW + i * 512, 512) for i in range(2)]
    y = place(A_R + 4 * KD * W + 4096, TOK)
    spans = [(0, 512, 1), (512, 512, 1)] + ([] if last else [(1024, 256, 3)])
    work = [(j, sp) for j in range(2) for sp in spans]
    ada_at = {}
    if layer == 0:
        ada = Modulations(s, FIRST_CHUNKS, CONV_CHUNKS, [place(A_ATT, KD, 512), place(A_R + 4 * KD * W, KD, 512)],
                          place(A_ATT + 4096, 512))
        ada_at = {i * 3 * len(work) // CONV_CHUNKS: i for i in range(CONV_CHUNKS)}
    segs = [(0, SEQ, 0)] + ([] if last else [(SEQ, CTX, SEQ + 2)])
    s_w = [sem(f"w_conv_loaded_{i}") for i in range(4)]
    s_whi, s_wlo, s_mm, s_zero = sem("weights_hi"), sem("weights_lo"), sem("conv_product"), sem("conv_zeros")
    s_x, s_g, s_u, s_y = sem("conv_x"), sem("conv_gate"), sem("conv_u"), sem("conv_y")
    NW = len(spans)
    with nc.Block() as block:
        @block.sync
        def _(sp):
            s["clear_last"](sp)
            for i in range(4):
                rows = slice(i % 2 * 4, i % 2 * 4 + 4)
                sp.dma_start(wb[:, i // 2, rows], s["a"]["w_conv"][layer, :, i // 2, rows]).then_inc(s_w[i], 16)
            if layer == 0:
                for i in range(CONV_CHUNKS):
                    ada.load(sp, i)

        @block.tensor
        def _(pe):
            turn = None
            for n, (j, (t0, tn, _)) in enumerate(work):
                if n >= 2:
                    pe.wait_ge(s_g, n - 1)
                    pe.wait_ge(s_u, n - 1)
                for q in range(3):
                    cols = slice(q * P, (q + 1) * P)
                    for k in range(KD):
                        if n % NW == 0 and q == 0:
                            pe.wait_ge(s_whi, j * KD + k + 1)
                            pe.wait_ge(s_wlo, j * KD + k + 1)
                        mm = split_product(pe, banks[3 * (n % 2) + q][:, 0:tn], (whi[:, j, k, cols], wlo[:, j, k, cols]),
                                           (HI[:, k, t0:t0 + tn], LO[:, k, t0:t0 + tn]), k == 0, k == KD - 1)
                    mm.then_inc(s_mm, 1)
                    if turn is not None:
                        ada.turn(pe, turn)
                        turn = None
                    if 3 * n + q in ada_at:
                        turn = ada_at[3 * n + q]
                        ada.multiply(pe, turn)

        @block.scalar
        def _(act):
            for j in range(2):
                for k in range(KD):
                    if k % 4 == 0:
                        act.wait_ge(s_w[2 * j + k // 4], 16)
                    act.activation(whi[:, j, k], wb[:, j, k], ACT.Copy).then_inc(s_whi, 1)
            for n, (j, (t0, tn, _)) in enumerate(work):
                act.wait_ge(s_mm, 3 * n + 1)
                if n >= 2:
                    act.wait_ge(s_u, n - 1)
                act.activation(xc[n % 2][:, 0:tn], banks[3 * (n % 2)][:, 0:tn], ACT.Copy).then_inc(s_x, 1)
                act.wait_ge(s_mm, 3 * n + 2)
                act.activation(YC[:, j, t0:t0 + tn], banks[3 * (n % 2) + 1][:, 0:tn], ACT.Copy).then_inc(s_g, 1)
            act.wait_ge(s_g, len(work))

        @block.vector
        def _(dve):
            for j in range(2):
                for k in range(KD):
                    dve.wait_ge(s_whi, j * KD + k + 1)
                    dve.tensor_tensor(wlo[:, j, k], wb[:, j, k], whi[:, j, k].bitcast(F32), ALU.subtract)\
                        .then_inc(s_wlo, 1)
            dve.memset(u, 0.0).then_inc(s_zero, 1)
            dve.wait_ge(s_zero, 1)
            if layer == 0:
                ada.clear_rows(dve)
            keep = None
            done = Count(s_y)
            for n, (j, (t0, tn, off)) in enumerate(work):
                for q in range(3):
                    if q == 2:
                        dve.wait_ge(s_x, n + 1)
                        dve.wait_ge(s_mm, 3 * n + 3)
                        if n == NW:
                            dve.wait_ge(s_y, done.now())
                        dve.tensor_tensor(u[:, off + t0:off + t0 + tn], banks[3 * (n % 2) + 2][:, 0:tn],
                                          xc[n % 2][:, 0:tn], ALU.mult).then_inc(s_u, 1)
                    if keep is not None:
                        ada.keep(dve, keep)
                        keep = None
                    if 3 * n + q in ada_at:
                        keep = ada_at[3 * n + q]
                        ada.copy(dve, keep)
                if n % NW < NW - 1:
                    continue
                dve.wait_ge(s_u, n + 1)
                for t0, tn, off in segs:
                    w = [vec[:, V_CONV + layer * 6 + j * 3 + i:V_CONV + layer * 6 + j * 3 + i + 1] for i in range(3)]
                    yy = y[:, t0:t0 + tn]
                    if done.n:
                        dve.wait_ge(s_y, done.now())
                    done.up(dve.tensor_scalar(yy, u[:, off:off + tn], w[0], None, ALU.mult))
                    for i in (1, 2):
                        dve.wait_ge(s_y, done.now())
                        done.up(dve.scalar_tensor_tensor(yy, u[:, off + i:off + i + tn], w[i], yy,
                                                         ALU.mult, ALU.add))
                    dve.wait_ge(s_y, done.now())
                    dve.wait_ge(s_g, n + 1)
                    done.up(dve.tensor_tensor(YC[:, j, t0:t0 + tn], yy, YC[:, j, t0:t0 + tn], ALU.mult))
            if layer == 0:
                dve.wait_ge(ada.kept, CONV_CHUNKS)
            dve.wait_ge(s_y, done.now())


def fourier_branch(s, layer, last):
    nc, sem, place, banks = s["nc"], s["sem"], s["place"], s["banks"]
    U, FT = place(A_U, NT, F_WIDTH), place(A_FT, 2, TOK)
    H = SEQ // 2
    at = A_R
    cb = [place(at + i * 4096, NTX, H) for i in range(2)]
    at += 8192
    small = place(at, 4, P)
    dctx = place(at + 512, 2, 2, CTX)
    ab = place(at + 1536, 4, 512)
    ada_weights = [place(A_ATT, KD, 512), place(A_R + 12288, KD, 512)]
    at = A_R + 16384
    odd = [place(at + i * H, H) for i in range(2)]
    mid = place(at + 2 * H, 2)
    alt = place(at + 2 * H + 8, 2)
    s_c = [sem("cosines_loaded"), sem("sines_loaded")]
    s_small, s_mm, s_ab, s_fm, s_f, s_odd = sem("dft_small_loaded"), sem("dft_product"), sem("dft_copied"), \
        sem("dft_channels"), sem("ft_written"), sem("odd_copied")
    modulate = layer == 0
    if modulate:
        ada = Modulations(s, FIRST_CHUNKS + CONV_CHUNKS, FOURIER_CHUNKS, ada_weights, place(A_ATT + 4096, 512))
    with nc.Block() as block:
        @block.sync
        def _(sp):
            s["clear_last"](sp)
            sp.dma_start(cb[0], s["a"]["dft"][0]).then_inc(s_c[0], 16)
            consts = s["a"]["consts"]
            sp.dma_start(small, consts[:, C_DFT:C_DFT + 4 * P].rearrange("p (a b) -> p a b", b=P)).then_inc(s_small, 16)
            sp.dma_start(alt, consts[:, C_ALT:C_ALT + 2]).then_inc(s_small, 16)
            sp.dma_start(dctx, consts[:, C_DCTX:C_DCTX + 4 * CTX].rearrange("p (a b c) -> p a b c", b=2, c=CTX))\
                .then_inc(s_small, 16)
            if modulate:
                ada.load(sp, 0)
            sp.dma_start(cb[1], s["a"]["dft"][1]).then_inc(s_c[1], 16)
            if modulate:
                for i in range(1, FOURIER_CHUNKS):
                    ada.load(sp, i)

        @block.tensor
        def _(pe):
            def modulations(i):
                if modulate and 0 < i <= FOURIER_CHUNKS:
                    ada.turn(pe, i - 1)
                if modulate and i < FOURIER_CHUNKS:
                    ada.multiply(pe, i)

            def over_tokens(bank, n, ct, tiles, rhs):
                for m, t in enumerate(tiles):
                    mm = pe.matmul(banks[bank][:, 0:n], U[:, t, ct * P:(ct + 1) * P], rhs(m), start=m == 0,
                                   stop=m == len(tiles) - 1)
                mm.then_inc(s_mm, 1)

            for w in range(2):
                pe.wait_ge(s_c[w], 16)
                for ct in range(2):
                    over_tokens(2 * w + ct, H, ct, range(NTX), lambda m: cb[w][:, m, :])
                    modulations(2 * w + ct)
            pe.wait_ge(s_small, 48)
            pe.wait_ge(s_ab, 2)
            for ct in range(2):
                over_tokens(ct, 1, ct, range(NTX), lambda m: alt[:, 0:1])
            pe.wait_ge(s_ab, 4)
            for ct in range(2):
                if ct:
                    pe.wait_ge(s_f, 2)
                    pe.wait_ge(s_odd, 1)
                for w in range(2):
                    mm = pe.matmul(banks[4 + w][:, 0:H], small[:, w, :], ab[:, 2 * w + ct, :], start=True, stop=True)
                mm.then_inc(s_fm, 1)
            modulations(4)
            pe.wait_ge(s_f, 4)
            pe.wait_ge(s_ab, 6)
            pe.matmul(banks[4][:, 0:2], small[:, 0, :], mid, start=True, stop=True).then_inc(s_fm, 1)
            if not last:
                for w in range(2):
                    for ct in range(2):
                        over_tokens(2 * w + ct, CTX, ct, range(NTX, NT), lambda m: dctx[:, m, w, :])
                        modulations(5 + 2 * w + ct)
                pe.wait_ge(s_ab, 10)
                pe.wait_ge(s_f, 5)
                pe.wait_ge(s_odd, 2)
                for ct in range(2):
                    for w in range(2):
                        mm = pe.matmul(banks[4 + ct][:, 0:CTX], small[:, 2 + w, :], ab[:, 2 * w + ct, 0:CTX],
                                       start=w == 0, stop=w == 1)
                    mm.then_inc(s_fm, 1)

        @block.scalar
        def _(act):
            for i in range(4):
                act.wait_ge(s_mm, i + 1)
                act.activation(ab[:, i, :], banks[i][:, 0:H], ACT.Copy).then_inc(s_ab, 1)
            for ct in range(2):
                act.wait_ge(s_mm, 5 + ct)
                act.activation(mid[:, ct:ct + 1], banks[ct][:, 0:1], ACT.Copy).then_inc(s_ab, 1)
            for ct in range(2):
                act.wait_ge(s_fm, ct + 1)
                act.activation(odd[ct], banks[5][:, 0:H], ACT.Copy).then_inc(s_odd, 1)
            if not last:
                for i in range(4):
                    act.wait_ge(s_mm, 7 + i)
                    act.activation(ab[:, i, 0:CTX], banks[i][:, 0:CTX], ACT.Copy).then_inc(s_ab, 1)
                act.wait_ge(s_ab, 10)

        @block.vector
        def _(dve):
            def modulations(i):
                if modulate and i:
                    ada.keep(dve, i - 1)
                if modulate and i < FOURIER_CHUNKS:
                    ada.copy(dve, i)

            if modulate:
                ada.clear_rows(dve)
            for i in range(4):
                modulations(i)
            for ct in range(2):
                dve.wait_ge(s_fm, ct + 1)
                dve.wait_ge(s_odd, ct + 1)
                dve.tensor_tensor(FT[:, ct, 0:H], banks[4][:, 0:H], odd[ct], ALU.add).then_inc(s_f, 1)
                dve.tensor_tensor(FT[:, ct, H + 1:SEQ], banks[4][:, H - 1:0:-1], odd[ct][:, H - 1:0:-1],
                                  ALU.subtract).then_inc(s_f, 1)
            modulations(4)
            dve.wait_ge(s_fm, 3)
            dve.tensor_copy(FT[:, :, H:H + 1], banks[4][:, 0:2].unsqueeze(2)).then_inc(s_f, 1)
            if not last:
                for i in range(5, FOURIER_CHUNKS + 1):
                    modulations(i)
                for ct in range(2):
                    dve.wait_ge(s_fm, 4 + ct)
                    dve.tensor_copy(FT[:, ct, SEQ:TOK], banks[4 + ct][:, 0:CTX]).then_inc(s_f, 1)
            dve.wait_ge(s_f, 5 if last else 7)
            if modulate:
                dve.wait_ge(ada.kept, FOURIER_CHUNKS)


def attention(s, layer, last):
    nc, sem, place, vec, banks = s["nc"], s["sem"], s["place"], s["vec"], s["banks"]
    ATT = place(A_ATT, PAIRS, TOK)
    at = A_R
    V = place(at, NT, NAW)
    VS = place(at + NT * NAW, NTX - 1, NAW)
    at += (2 * NT - 3) * NAW
    raw, tbl = place(at, RPB_R, GRID_W), place(at + 960, RPB_R, GRID_W)
    at += 1920
    QT, KT = place(at, TOK), place(at + TOK, TOK)
    qs, ks = place(at + 2 * TOK, NT, P), place(at + 3 * TOK, NT, P)
    at += 4 * TOK
    sc = [place(at + i * 512, 512) for i in range(2)]
    pr = [place(at + 1024 + i * 768, 768) for i in range(2)]
    pt = [place(at + 2560 + i * 768, 6, P) for i in range(2)]
    ao = [place(at + 4096 + i * HD, HD) for i in range(2)]
    at += 4096 + 2 * HD
    mask = place(at, GRID_W)
    st = place(at + GRID_W, 4, 8)
    zeros = place(ARENA - ZEROS, ZEROS)
    ident = s["ident"]
    NQ = NTX if last else NT
    NI = ROWS + (0 if last else CTX // GRID_W)
    groups = [(qs, QT, t, min(t + 4, NQ)) for t in range(0, NQ, 4)] + [(ks, KT, t, min(t + 4, NT)) for t in range(0, NT, 4)]
    G4, G5 = (len(groups) + 1) // 2, len(groups) // 2
    U4, U5 = G4 + ROWS, G5 + NI
    start = [min(max(r - WIN_R // 2, 0), ROWS - WIN_R) for r in range(ROWS)]
    s_v, s_qk, s_raw, s_mask = sem("v_loaded"), sem("qk_loaded"), sem("bias_loaded"), sem("mask_loaded")
    s_tbl, s_pe, s_dve = sem("bias_ready"), sem("tensor_passed"), sem("vector_passed")
    s_sc, s_mid, s_m, s_e, s_el = sem("scores"), sem("local_max"), sem("neg_max"), sem("probs"), sem("probs_local")
    s_t4, s_t5, s_b4, s_b5 = sem("bank4_filled"), sem("bank5_filled"), sem("bank4_copied"), sem("bank5_copied")
    s_zero, s_fill = sem("zeros"), sem("slots_filled")
    s_pv, s_o, s_tt, s_at, s_l = sem("weighted"), sem("normalised"), sem("out_turned"), sem("out_copied"), sem("inv")

    def v_tiles(n, pair):
        cols = bass.ds(pair * P, P)
        local = []
        if n < ROWS:
            src, t0 = (V, start[n] // 2) if start[n] % 2 == 0 else (VS, (start[n] - 1) // 2)
            local = [(j, src[:, t0 + j, cols]) for j in range(4)]
        return local + [(4 + j, V[:, NTX + j, cols]) for j in range(2)]

    with nc.Block() as block:
        @block.sync
        def _(sp):
            s["clear_last"](sp)
            sp.dma_start(mask, s["a"]["consts"][:, C_MASK:C_MASK + GRID_W]).then_inc(s_mask, 16)

            def load(pair):
                sp.dma_start(qs[:, 0:NQ], s["q_rows"][0:NQ * P, bass.ds(pair * P, P)]
                             .rearrange("(t p) d -> p t d", p=P)).then_inc(s_qk, 16)
                sp.dma_start(ks, s["k_rows"][:, bass.ds(pair * P, P)]
                             .rearrange("(t p) d -> p t d", p=P)).then_inc(s_qk, 16)

            def load_biases(pair):
                for h in range(2):
                    sp.dma_start(raw[h * 64:(h + 1) * 64],
                                 bass.AP(s["a"]["rpb"].tensor,
                                         pair * (2 * RPB_R * RPB_PAD) + (layer * HEADS + h) * RPB_R * RPB_PAD,
                                         [[1, GRID_W], [RPB_PAD, RPB_R], [1, GRID_W]])).then_inc(s_raw, 16)

            load(0)
            load_biases(0)
            sp.dma_start(V, s["v_rows"].rearrange("(t p) d -> p t d", p=P)).then_inc(s_v, 16)
            sp.dma_start(VS, s["v_rows"][GRID_W:SEQ - GRID_W].rearrange("(t p) d -> p t d", p=P)).then_inc(s_v, 16)
            if layer == 0:
                sp.wait_ge(s_zero, 1)
                rows = MAX_SLOTS // 3
                for r in range(3):
                    sp.dma_start(s["slots"][r * rows:(r + 1) * rows].rearrange("(p a) (b z) -> p (a b) z", p=P, z=ZEROS),
                                 zeros.unsqueeze(1).broadcast_to([P, rows * D // P // ZEROS, ZEROS]))\
                        .then_inc(s_fill, 16)
            with sp.Fori(0, PAIRS - 1) as i:
                sp.wait_ge(s_b4, i * U4 + (G4 + 1))
                sp.wait_ge(s_b5, i * U5 + (G5 + 1))
                load(i + 1)
                sp.wait_ge(s_tbl, i + 1)
                load_biases(i + 1)
            if layer == 0:
                sp.wait_ge(s_fill, 48)

        @block.gpsimd
        def _(pool):
            if layer == 0:
                pool.memset(zeros, 0.0).then_inc(s_zero, 1)
            pool.wait_ge(s_mask, 16)
            with pool.Fori(0, PAIRS) as i:
                pool.wait_ge(s_raw, i * 32 + 32)
                pool.wait_ge(s_m, i * NI + 1)
                pool.tensor_tensor(tbl, raw[:, :, ::-1], mask.unsqueeze(1).broadcast_to([P, RPB_R, GRID_W]),
                                   ALU.add).then_inc(s_tbl, 1)
            pool.wait_ge(s_tbl, PAIRS)

        @block.tensor
        def _(pe):
            pe.sem_inc(s_pv, 2)
            pe.sem_inc(s_tt, 2)
            with pe.Fori(0, PAIRS) as i:
                pe.wait_ge(s_qk, i * 32 + 32)
                for g, (src, dst, t0, t1) in enumerate(groups):
                    filled, copied, u = (s_t5, s_b5, i * U5 + g // 2) if g % 2 else (s_t4, s_b4, i * U4 + g // 2)
                    pe.wait_ge(copied, u + 1)
                    for t in range(t0, t1):
                        mm = pe.transpose(banks[4 + g % 2][:, (t - t0) * P:(t - t0 + 1) * P], src[:, t, :], ident[:])
                    mm.then_inc(filled, 1)
                pe.wait_ge(s_b4, i * U4 + (G4 + 1))
                pe.wait_ge(s_b5, i * U5 + (G5 + 1))
                for j in range(NI + 3):
                    if j < NI:
                        n = j
                        pe.wait_ge(s_e, i * NI + (n + 1))
                        q0 = n * GRID_W
                        apart(pe, s_pe)
                        for h in (0, 64):
                            if n < ROWS:
                                k0 = start[n] * GRID_W
                                pe.matmul(banks[n % 2][h:h + 64, :], QT[h:h + 64, q0:q0 + 64],
                                          KT[h:h + 64, k0:k0 + 512], start=True, stop=True)
                            mm = pe.matmul(banks[2 + n % 2][h:h + 64, 0:CTX], QT[h:h + 64, q0:q0 + 64],
                                           KT[h:h + 64, SEQ:TOK], start=True, stop=True)
                        mm.then_inc(s_sc, 1)
                    if 1 <= j <= NI:
                        n = j - 1
                        pe.wait_ge(s_e, i * NI + (n + 3))
                        if n < ROWS:
                            pe.wait_ge(s_b4, i * U4 + (G4 + n + 1))
                            for k in range(4):
                                mm = pe.transpose(banks[4][:, k * P:(k + 1) * P], pr[n % 2][:, k * P:(k + 1) * P],
                                                  ident[:])
                            mm.then_inc(s_t4, 1)
                        pe.wait_ge(s_b5, i * U5 + (G5 + n + 1))
                        for k in range(2):
                            mm = pe.transpose(banks[5][:, k * P:(k + 1) * P], pr[n % 2][:, (4 + k) * P:(5 + k) * P],
                                              ident[:])
                        mm.then_inc(s_t5, 1)
                    if 2 <= j <= NI + 1:
                        n = j - 2
                        if n == 0:
                            pe.wait_ge(s_v, 32)
                        if n < ROWS:
                            pe.wait_ge(s_b4, i * U4 + (G4 + n + 2))
                        pe.wait_ge(s_b5, i * U5 + (G5 + n + 2))
                        pe.wait_ge(s_o, i * NI + (n + 1))
                        tiles = v_tiles(n, i)
                        for m, (k, v) in enumerate(tiles):
                            mm = pe.matmul(banks[6][:, 0:P], pt[n % 2][:, k, :], v, start=m == 0,
                                           stop=m == len(tiles) - 1)
                        mm.then_inc(s_pv, 1)
                    if j >= 3:
                        n = j - 3
                        pe.wait_ge(s_o, i * NI + (n + 2))
                        pe.wait_ge(s_at, i * NI + (n + 1))
                        apart(pe, s_pe)
                        pe.transpose(banks[7][0:HD, 0:P], ao[n % 2], ident[:]).then_inc(s_tt, 1)

        @block.vector
        def _(dve):
            dve.sem_inc(s_m, 1)
            dve.sem_inc(s_b5, 1)
            dve.sem_inc(s_o, 1)
            with dve.Fori(0, PAIRS) as i:
                for g, (src, dst, t0, t1) in enumerate(groups):
                    if g % 2:
                        dve.wait_ge(s_t5, i * U5 + (g // 2 + 1))
                        dve.tensor_copy(dst[:, t0 * P:t1 * P], banks[5][:, 0:(t1 - t0) * P]).then_inc(s_b5, 1)
                dve.wait_ge(s_b5, i * U5 + (G5 + 1))
                for j in range(NI + 2):
                    if j < NI:
                        n = j
                        x = st[:, n % 4]
                        dve.wait_ge(s_sc, i * NI + (n + 1))
                        dve.wait_ge(s_e, i * NI + (n + 1))
                        if n < ROWS:
                            if n == 0:
                                dve.wait_ge(s_tbl, i + 1)
                            d0 = start[n] - n + WIN_R - 1
                            apart(dve, s_dve)
                            dve.tensor_tensor_reduce(
                                out=sc[n % 2], in0=banks[n % 2][:],
                                in1=tbl[:, d0:d0 + WIN_R, :].rearrange("p a b -> p (a b)"), scale=1.0,
                                scalar=-3e38, op0=ALU.add, op1=ALU.max, accum_out=x[:, 0:1]).then_inc(s_mid, 1)
                        dve.tensor_reduce(x[:, 1:2], banks[2 + n % 2][:, 0:CTX], AX.X, ALU.max).then_inc(s_mid, 1)
                        dve.wait_ge(s_mid, i * (ROWS + NI) + (min(n + 1, ROWS) + n + 1))
                        if n < ROWS:
                            dve.tensor_scalar(x[:, 2:3], x[:, 1:2], x[:, 0:1], -1.0, ALU.max,
                                              ALU.mult).then_inc(s_m, 1)
                        else:
                            dve.tensor_scalar(x[:, 2:3], x[:, 1:2], -1.0, None, ALU.mult).then_inc(s_m, 1)
                    if 1 <= j <= NI:
                        n = j - 1
                        dve.wait_ge(s_t5, i * U5 + (G5 + n + 1))
                        dve.wait_ge(s_pv, i * NI + (n + 1))
                        dve.tensor_copy(pt[n % 2][:, 4:6, :].rearrange("p a b -> p (a b)"),
                                        banks[5][:, 0:CTX]).then_inc(s_b5, 1)
                    if j >= 2:
                        n = j - 2
                        x = st[:, n % 4]
                        if n < ROWS:
                            dve.tensor_tensor(x[:, 5:6], x[:, 3:4], x[:, 4:5], ALU.add).then_inc(s_l, 1)
                        else:
                            dve.tensor_copy(x[:, 5:6], x[:, 4:5]).then_inc(s_l, 1)
                        dve.wait_ge(s_l, i * (2 * NI) + (2 * n + 1))
                        dve.reciprocal(x[:, 6:7], x[:, 5:6]).then_inc(s_l, 1)
                        dve.wait_ge(s_l, i * (2 * NI) + (2 * n + 2))
                        dve.wait_ge(s_pv, i * NI + (n + 3))
                        dve.wait_ge(s_tt, i * NI + (n + 1))
                        dve.tensor_scalar(ao[n % 2][0:64], banks[6][0:64, 0:HD], x[0:64, 6:7], None, ALU.mult)
                        dve.tensor_scalar(ao[n % 2][64:128], banks[6][64:128, HD:2 * HD], x[64:128, 6:7], None,
                                          ALU.mult).then_inc(s_o, 1)

        @block.scalar
        def _(act):
            act.sem_inc(s_e, 2)
            act.sem_inc(s_b4, 1)
            act.sem_inc(s_at, 1)
            with act.Fori(0, PAIRS) as i:
                for g, (src, dst, t0, t1) in enumerate(groups):
                    if g % 2 == 0:
                        act.wait_ge(s_t4, i * U4 + (g // 2 + 1))
                        act.activation(dst[:, t0 * P:t1 * P], banks[4][:, 0:(t1 - t0) * P], ACT.Copy).then_inc(s_b4, 1)
                for j in range(NI + 3):
                    if j < NI:
                        n = j
                        x = st[:, n % 4]
                        act.wait_ge(s_m, i * NI + (n + 2))
                        if n >= 2:
                            act.wait_ge(s_t5, i * U5 + (G5 + n - 1))
                        if n < ROWS:
                            act.activation(pr[n % 2][:, 0:512], sc[n % 2], ACT.Exp, bias=x[:, 2:3],
                                           accum_out=x[:, 3:4]).then_inc(s_el, 1)
                            act.wait_ge(s_el, i * ROWS + (n + 1))
                        act.activation(pr[n % 2][:, 512:768], banks[2 + n % 2][:, 0:CTX], ACT.Exp, bias=x[:, 2:3],
                                       accum_out=x[:, 4:5]).then_inc(s_e, 1)
                    if 1 <= j <= ROWS:
                        n = j - 1
                        act.wait_ge(s_t4, i * U4 + (G4 + n + 1))
                        act.wait_ge(s_pv, i * NI + (n + 1))
                        act.activation(pt[n % 2][:, 0:4, :].rearrange("p a b -> p (a b)"), banks[4][:],
                                       ACT.Copy).then_inc(s_b4, 1)
                    if j >= 3:
                        n = j - 3
                        act.wait_ge(s_tt, i * NI + (n + 3))
                        for h in range(2):
                            cp = act.activation(ATT[h * 64:(h + 1) * 64, bass.ds(i, 1), n * 64:(n + 1) * 64],
                                                banks[7][0:HD, h * 64:(h + 1) * 64].unsqueeze(1), ACT.Copy)
                        cp.then_inc(s_at, 1)
            act.wait_ge(s_at, PAIRS * NI + 1)


def gates_and_merge(s, layer, last):
    nc, sem, place, banks, part = s["nc"], s["sem"], s["place"], s["banks"], s["part"]
    ATT, FT, YC = place(A_ATT, PAIRS, TOK), place(A_FT, 2, TOK), place(A_YC, 2, TOK)
    HI, LO = part(A_H, KD, TOK), part(A_X, KD, TOK)
    MERGED = place(A_R, KD, TOK)
    branches = [(FT, 2), (ATT, 4), (YC, 2)]
    at = A_R + KD * TOK
    wb = [place(at + q * 1536, KD + branches[q][1], P) for q in range(3)]
    wlo = [part(at + q * 1536, KD, P) for q in range(3)]
    whi = [part(at + 4608 + q * 1024, KD, P) for q in range(3)]
    at += 4608 + 3072
    sg = [place(at + i * 512, 512) for i in range(2)]
    prod = [place(at + 1024 + i * 512, 512) for i in range(2)]
    spans = [(0, 512), (512, 512)] + ([] if last else [(1024, 256)])
    NS = len(spans)
    s_w = [sem(f"gate_w_loaded_{q}") for q in range(3)]
    s_whi, s_wlo = sem("weights_hi"), sem("weights_lo")
    s_gm, s_bm, s_sg, s_pr, s_mg = sem("gate_product"), sem("branch_product"), sem("gate_ready"), sem("gated"), sem("merged")
    s_pool = sem("gpsimd_passed")
    U = 3 * NS
    work = [(q, span) for q in range(3) for span in range(NS)]

    def chunks(eng, body):
        with eng.Fori(0, KD - 3, 2) as i:
            for b in range(2):
                body(i, b, False)
        for b in range(2):
            body(KD - 2, b, b == 1)

    with nc.Block() as block:
        @block.sync
        def _(sp):
            s["clear_last"](sp)
            with sp.Fori(0, KD - 1, 2) as i:
                for b in range(2):
                    at = 0
                    for q in range(3):
                        n = KD + branches[q][1]
                        sp.wait_ge(s_bm, i * U + (b * U + (q + 1) * NS))
                        sp.dma_start(wb[q], s["a"]["w_gates"][layer, bass.ds(i + b, 1), :, at:at + n]
                                     .rearrange("o p k n -> p (o k) n")).then_inc(s_w[q], 16)
                        at += n

        @block.tensor
        def _(pe):
            pe.sem_inc(s_bm, U)
            with pe.Fori(0, KD - 1, 2) as i:
                for b in range(2):
                    for n, (q, span) in enumerate(work):
                        t0, tn = spans[span]
                        src, ks = branches[q]
                        if span == 0:
                            pe.wait_ge(s_w[q], i * 16 + (b * 16 + 16))
                            pe.wait_ge(s_whi, i * 3 + (b * 3 + q + 1))
                            pe.wait_ge(s_wlo, i * 3 + (b * 3 + q + 1))
                        pe.wait_ge(s_pr, i * U + (b * U + n + 1))
                        for k in range(KD):
                            mm = split_product(pe, banks[2 * (n % 3)][:, 0:tn], (whi[q][:, k, :], wlo[q][:, k, :]),
                                               (HI[:, k, t0:t0 + tn], LO[:, k, t0:t0 + tn]), k == 0, k == KD - 1)
                        mm.then_inc(s_gm, 1)
                        for k in range(ks):
                            mm = pe.matmul(banks[2 * (n % 3) + 1][:, 0:tn], wb[q][:, KD + k, :], src[:, k, t0:t0 + tn],
                                           start=k == 0, stop=k == ks - 1)
                        mm.then_inc(s_bm, 1)

        @block.scalar
        def _(act):
            def round_weights(i, q):
                act.wait_ge(s_w[q], i * 16 + 16)
                act.activation(whi[q], wb[q][:, 0:KD], ACT.Copy).then_inc(s_whi, 1)

            def body(i, b, final):
                for n, (q, span) in enumerate(work):
                    tn, m = spans[span][1], b * U + n
                    if span == 0 and not (final and q == 2):
                        round_weights(i + (b + (q + 1) // 3), (q + 1) % 3)
                    act.wait_ge(s_gm, i * U + (m + 1))
                    act.wait_ge(s_pr, i * U + (m + 2))
                    act.activation(sg[m % 2][:, 0:tn], banks[2 * (n % 3)][:, 0:tn], ACT.Sigmoid).then_inc(s_sg, 1)

            round_weights(0, 0)
            chunks(act, body)

        @block.vector
        def _(dve):
            def leave_weights(i, q):
                dve.wait_ge(s_whi, i * 3 + (q + 1))
                dve.tensor_tensor(wlo[q], wb[q][:, 0:KD], whi[q].bitcast(F32), ALU.subtract).then_inc(s_wlo, 1)

            def body(i, b, final):
                for n, (q, span) in enumerate(work):
                    (t0, tn), m = spans[span], b * U + n
                    if span == 0 and not (final and q == 2):
                        leave_weights(i + (b + (q + 1) // 3), (q + 1) % 3)
                    dve.wait_ge(s_sg, i * U + (m + 1))
                    dve.wait_ge(s_bm, i * U + (m + U + 1))
                    if q == 0:
                        to = MERGED[:, bass.ds(i + b, 1), t0:t0 + tn].rearrange("p o n -> p (o n)")
                    else:
                        c = b * 2 * NS + n - NS
                        to = prod[c % 2][:, 0:tn]
                        dve.wait_ge(s_mg, i * (2 * NS) + (c + 1))
                    dve.tensor_tensor(to, banks[2 * (n % 3) + 1][:, 0:tn], sg[m % 2][:, 0:tn], ALU.mult)\
                        .then_inc(s_pr, 1)

            dve.sem_inc(s_pr, 3)
            leave_weights(0, 0)
            chunks(dve, body)

        @block.gpsimd
        def _(pool):
            pool.sem_inc(s_mg, 2)
            with pool.Fori(0, KD - 1, 2) as i:
                for b in range(2):
                    for n, (q, span) in enumerate(work):
                        if q == 0:
                            continue
                        t0, tn = spans[span]
                        c = b * 2 * NS + n - NS
                        pool.wait_ge(s_pr, i * U + (b * U + n + 4))
                        pool.wait_ge(s_mg, i * (2 * NS) + (c + 2))
                        to = MERGED[:, bass.ds(i + b, 1), t0:t0 + tn].rearrange("p o n -> p (o n)")
                        apart(pool, s_pool)
                        pool.tensor_tensor(to, to, prod[c % 2][:, 0:tn], ALU.add).then_inc(s_mg, 1)
            pool.wait_ge(s_mg, 2 + KD * NS * 2)


def broadcast_columns(s, pe, columns, bank):
    for j, col in enumerate(columns):
        mm = pe.matmul(bank[:, j * P:(j + 1) * P], col.broadcast_to([P, P]), s["ident"][:], start=True, stop=True)
    return mm


def mixer_output(s, layer, last):
    nc, sem, place, mod, banks, part = s["nc"], s["sem"], s["place"], s["mod"], s["banks"], s["part"]
    X = place(A_X, NT, D)
    MERGED, MLO, MHI = place(A_R, KD, TOK), part(A_R, KD, TOK), part(A_H, KD, TOK)
    wo = place(A_R + KD * TOK, 2, KD, 512)
    wlo, whi = part(A_R + KD * TOK, 2, KD, 512), part(A_ATT, 2, KD, 512)
    g1 = place(A_ATT + 8192, 2, D)
    tmp = [place(A_R + KD * TOK + 8192 + i * 512, 512) for i in range(2)]
    junk = place(A_R + KD * TOK + 8192 + 1024, D)
    NQ = NTX if last else NT
    work = [(h, t) for h in range(2) for t in range(NQ)]
    s_w = [sem(f"w_o_loaded_{i}") for i in range(4)]
    s_xl, s_sq = sem("x_loaded"), sem("squares")
    s_whi, s_wlo, s_mhi, s_mlo = sem("weights_hi"), sem("weights_lo"), sem("merged_hi"), sem("merged_lo")
    s_b, s_g, s_mm, s_t, s_x = sem("g1_rows"), sem("g1_copied"), sem("out_product"), sem("gated_out"), sem("x_updated")
    with nc.Block() as block:
        @block.sync
        def _(sp):
            s["clear_last"](sp)
            for i in range(4):
                rows = slice(i % 2 * 4, i % 2 * 4 + 4)
                sp.dma_start(wo[:, i // 2, rows], s["a"]["w_o"][layer, i // 2, :, rows]).then_inc(s_w[i], 16)
                if i == 1:
                    x = s["a"]["x"][0] if layer == 0 else s["x_rows"][0:SEQ]
                    sp.dma_start(X[:, 0:NTX], x.rearrange("(t p) d -> p t d", p=P)).then_inc(s_xl, 16)
                    if not last:
                        c = s["a"]["ctx"][0] if layer == 0 else s["x_rows"][SEQ:TOK]
                        sp.dma_start(X[:, NTX:NT], c.rearrange("(t p) d -> p t d", p=P)).then_inc(s_xl, 16)

        @block.tensor
        def _(pe):
            for w in range(2):
                for h in range(2):
                    cols = [mod[:, layer, 2 * KD + 4 * h + j, w:w + 1] for j in range(4)]
                    broadcast_columns(s, pe, cols, banks[4 + 2 * w + h]).then_inc(s_b, 1)
            for n, (h, t) in enumerate(work):
                if h == 0:
                    pe.wait_ge(s_mlo, t + 1)
                if n >= 4:
                    pe.wait_ge(s_t, n - 3)
                for k in range(KD):
                    if t == 0:
                        pe.wait_ge(s_wlo, h * KD + k + 1)
                    mm = split_product(pe, banks[n % 4][:], (MHI[:, k, t * P:(t + 1) * P], MLO[:, k, t * P:(t + 1) * P]),
                                       (whi[:, h, k, :], wlo[:, h, k, :]), k == 0, k == KD - 1)
                mm.then_inc(s_mm, 1)

        @block.scalar
        def _(act):
            def round_weights(h, k):
                if k % 4 == 0:
                    act.wait_ge(s_w[2 * h + k // 4], 16)
                act.activation(whi[:, h, k], wo[:, h, k], ACT.Copy).then_inc(s_whi, 1)

            def round_merged(t):
                act.activation(MHI[:, :, t * P:(t + 1) * P], MERGED[:, :, t * P:(t + 1) * P], ACT.Copy)\
                    .then_inc(s_mhi, 1)

            round_merged(0)
            round_merged(1)
            for w in range(2):
                for h in range(2):
                    act.wait_ge(s_b, 2 * w + h + 1)
                    act.activation(g1[:, w, h * 512:(h + 1) * 512], banks[4 + 2 * w + h][:], ACT.Copy)\
                        .then_inc(s_g, 1)
            for k in range(KD):
                round_weights(0, k)
            for t in range(2, NQ):
                round_merged(t)
            for k in range(KD):
                round_weights(1, k)
            for t in range(NQ):
                act.wait_ge(s_x, NQ + t + 1)
                if t:
                    act.wait_ge(s_sq, t)
                act.activation(junk, X[:, t], ACT.Square, accum_out=s["squares"][:, t:t + 1]).then_inc(s_sq, 1)
            act.wait_ge(s_sq, NQ)

        @block.vector
        def _(dve):
            def leave_weights(h, k):
                dve.wait_ge(s_whi, h * KD + k + 1)
                dve.tensor_tensor(wlo[:, h, k], wo[:, h, k], whi[:, h, k].bitcast(F32), ALU.subtract)\
                    .then_inc(s_wlo, 1)

            for k in range(KD):
                leave_weights(0, k)
            dve.wait_ge(s_g, 4)
            for n, (h, t) in enumerate(work):
                if h == 0 and t < KD:
                    leave_weights(1, t)
                dve.wait_ge(s_mm, n + 1)
                if n >= 2:
                    dve.wait_ge(s_x, n - 1)
                dve.tensor_tensor(tmp[n % 2], banks[n % 4][:], g1[:, t // NTX, h * 512:(h + 1) * 512],
                                  ALU.mult).then_inc(s_t, 1)

        @block.gpsimd
        def _(pool):
            def leave_merged(t):
                pool.wait_ge(s_mhi, t + 1)
                pool.tensor_tensor(MLO[:, :, t * P:(t + 1) * P], MERGED[:, :, t * P:(t + 1) * P],
                                   MHI[:, :, t * P:(t + 1) * P].bitcast(F32), ALU.subtract).then_inc(s_mlo, 1)

            leave_merged(0)
            leave_merged(1)
            for n, (h, t) in enumerate(work):
                if n + 2 < NQ:
                    leave_merged(n + 2)
                if n == 0:
                    pool.wait_ge(s_xl, 16 if last else 32)
                pool.wait_ge(s_t, n + 1)
                xs = X[:, t, h * 512:(h + 1) * 512]
                pool.tensor_tensor(xs, xs, tmp[n % 2], ALU.add).then_inc(s_x, 1)
            pool.wait_ge(s_x, len(work))


def norm_and_route(s, layer, last):
    nc, sem, place, vec, mod, banks = s["nc"], s["sem"], s["place"], s["vec"], s["mod"], s["banks"]
    X, H2 = place(A_X, NT, D), place(A_H, NT, D)
    NQ = NTX if last else NT
    at = A_R - 5 * TOK
    mul, add = place(at, 2, D), place(at + 2 * D, 2, D)
    n2 = place(at + 4 * D, D)
    rw = place(at + 5 * D, KD, EXP)
    at += 5 * D + KD * EXP
    HT2 = [place(ARENA - 4096 * (i + 1), KD, 512) for i in range(2)]
    ST = [place(ARENA - 8192 - 512 * (i + 1), 512) for i in range(2)]
    root, rstd = place(at + 16, NT), place(at + 32, NT)
    at += 48
    W = NQ * EXP
    big = [place(at + i * NT * EXP, NQ, EXP) for i in range(8)]
    S, SB, OH1, OH2, M, T1, RANK, TOT = big
    at += 10 * NT * EXP
    sm = [place(at + i * 48, NQ * 4) for i in range(10)]
    at += 480
    tri = place(at, P)
    ones = place(at + P, P)
    thr = place(at + 2 * P, NT)
    blk = place(at + 2 * P + NT, 48)
    desc = place(at + 2 * P + NT + 48, EXP)
    at += 2 * P + NT + 48 + EXP
    cnt, nb, cum, cum2, base = (place(at + i * EXP, EXP) for i in range(5))
    cmp = place(at + 5 * EXP, EXP, NT)
    cmpb = place(at + 5 * EXP + EXP * NT, 48, EXP)
    be = place(at + 5 * EXP + EXP * NT + 48 * EXP, PLAN)
    fd = place(at + 5 * EXP + EXP * NT + 48 * EXP + PLAN, NQ)
    s_ld, s_root, s_r, s_bc, s_bcc = sem("router_loaded"), sem("root2"), sem("rstd2"), \
        sem("mod2_rows"), sem("mod2_copied")
    s_a, s_h, s_tn, s_tc, s_lg, s_s = sem("rows_scaled2"), sem("h2_ready"), sem("h2_turned"), sem("h2_turned_copied"), \
        sem("logits"), sem("router_scores")
    s_hd, s_st, s_sb = sem("h2_ready_odd"), sem("scores_by_expert"), sem("scores_turned")
    groups = [range(t, min(t + 4, NQ)) for t in range(0, NQ, 4)]
    broadcasts = [(v, w, h) for w in range(2) for v in range(2) for h in range(2)]
    s_c, s_pp, s_pc, s_idx, s_sent = sem("routing_step"), sem("ranks"), sem("ones_ready"), sem("slots_known"), \
        s["pool_dma_sem"]("rows_sent")
    s_sh, s_xst = sem("mod2_scale"), sem("x_stored")
    CM, CB = 4 * KD, 3 * KD
    sc2 = place(at + 5 * EXP + EXP * NT + 48 * EXP + PLAN + NT, KD, 2)
    with nc.Block() as block:
        @block.sync
        def _(sp):
            s["clear_last"](sp)
            sp.dma_start(n2, s["a"]["norm2_rows"][layer]).then_inc(s_ld, 16)
            sp.dma_start(rw, s["a"]["router_w"]).then_inc(s_ld, 16)
            c = s["a"]["consts"]
            sp.dma_start(tri, c[:, C_TRI:C_TRI + P]).then_inc(s_ld, 16)
            sp.dma_start(thr, c[:, C_THR:C_THR + NT]).then_inc(s_ld, 16)
            sp.dma_start(blk, c[:, C_BLK:C_BLK + 48]).then_inc(s_ld, 16)
            sp.dma_start(desc, c[:, C_DESC:C_DESC + EXP]).then_inc(s_ld, 16)
            sp.dma_start(s["x_rows"][0:NQ * P].rearrange("(t p) d -> p t d", p=P), X[:, 0:NQ]).then_inc(s_xst, 16)
            sp.wait_ge(s_xst, 16)

        @block.scalar
        def _(act):
            act.activation(root[:, 0:NQ], s["squares"][:, 0:NQ], ACT.Sqrt, bias=s["eps"][:, 0:1], scale=1.0 / D)\
                .then_inc(s_root, 1)
            for n, (v, w, h) in enumerate(broadcasts):
                act.wait_ge(s_bc, n + 1)
                act.activation((mul, add)[v][:, w, h * 512:(h + 1) * 512], banks[n][:], ACT.Copy).then_inc(s_bcc, 1)
            for g, tiles in enumerate(groups):
                n = len(tiles) * P
                for t in tiles:
                    for h in range(2):
                        act.wait_ge(s_tn, 2 * t + h + 1)
                        if g >= 2:
                            act.wait_ge(s_lg, g - 1)
                        act.activation(HT2[g % 2][:, 4 * h:4 * h + 4, t % 4 * P:(t % 4 + 1) * P],
                                       banks[2 * (t % 2) + h][:].rearrange("p (a b) -> p a b", b=P),
                                       ACT.Copy).then_inc(s_tc, 1)
                act.wait_ge(s_lg, g + 1)
                if g >= 2:
                    act.wait_ge(s_sb, g - 1)
                act.activation(ST[g % 2][0:EXP, 0:n], banks[4 + g % 2][0:EXP, 0:n], ACT.Sigmoid).then_inc(s_st, 1)

        @block.tensor
        def _(pe):
            pe.wait_ge(s_sh, 1)
            for n, (v, w, h) in enumerate(broadcasts):
                src = sc2 if v == 0 else mod[:, layer, CB:CB + KD, :]
                broadcast_columns(s, pe, [src[:, 4 * h + j, w:w + 1] for j in range(4)], banks[n]).then_inc(s_bc, 1)
            pe.wait_ge(s_bcc, 8)
            pe.wait_ge(s_ld, 96)

            def logits(g):
                n = len(groups[g]) * P
                pe.wait_ge(s_tc, 2 * (groups[g][-1] + 1))
                if g >= 2:
                    pe.wait_ge(s_st, g - 1)
                for k in range(KD):
                    mm = pe.matmul(banks[4 + g % 2][0:EXP, 0:n], rw[:, k, :], HT2[g % 2][:, k, 0:n],
                                   start=k == 0, stop=k == KD - 1)
                mm.then_inc(s_lg, 1)

            def turn_scores(g):
                pe.wait_ge(s_st, g + 1)
                for j, t in enumerate(groups[g]):
                    mm = pe.matmul(banks[6][:, t * EXP:(t + 1) * EXP], ST[g % 2][0:EXP, j * P:(j + 1) * P],
                                   s["ident"][0:EXP, 0:EXP], start=True, stop=True)
                mm.then_inc(s_sb, 1)

            for t in range(NQ):
                if t % 2 == 0:
                    pe.wait_ge(s_h, t // 2 + 1)
                else:
                    pe.wait_ge(s_hd, t // 2 + 1)
                if t >= 2:
                    pe.wait_ge(s_tc, 2 * (t - 1))
                for h in range(2):
                    for j in range(4):
                        mm = pe.transpose(banks[2 * (t % 2) + h][:, j * P:(j + 1) * P],
                                          H2[:, t, (4 * h + j) * P:(4 * h + j + 1) * P], s["ident"][:])
                    mm.then_inc(s_tn, 1)
                if t % 4 == 0 and t:
                    logits(t // 4 - 1)
                if t % 4 == 1 and t > 1:
                    turn_scores(t // 4 - 1)
            logits(len(groups) - 1)
            turn_scores(len(groups) - 1)
            pe.wait_ge(s_pc, 1)
            pe.wait_ge(s_s, 1)
            flat = M.rearrange("p a b -> p (a b)")
            pe.matmul(banks[6][:, 0:W], tri, flat, start=True, stop=True).then_inc(s_pp, 1)
            pe.matmul(banks[7][:, 0:W], ones, flat, start=True, stop=True).then_inc(s_pp, 1)

        @block.vector
        def _(dve):
            dve.tensor_scalar(sc2, mod[:, layer, CM:CM + KD, :], 1.0, None, ALU.add).then_inc(s_sh, 1)
            dve.wait_ge(s_root, 1)
            dve.reciprocal(rstd[:, 0:NQ], root[:, 0:NQ]).then_inc(s_r, 1)
            dve.wait_ge(s_ld, 96)
            for t in range(NQ):
                w = t // NTX
                if t % NTX == 0:
                    dve.wait_ge(s_bcc, 4 * w + 2)
                    dve.tensor_tensor(mul[:, w], mul[:, w], n2, ALU.mult).then_inc(s_r, 1)
                    dve.wait_ge(s_r, 2 + w)
                dve.scalar_tensor_tensor(H2[:, t], X[:, t], rstd[:, t:t + 1], mul[:, w], ALU.mult,
                                         ALU.mult).then_inc(s_a, 1)
                if t % 2:
                    dve.wait_ge(s_a, t + 1)
                    dve.wait_ge(s_bcc, 4 * w + 4)
                    dve.tensor_tensor(H2[:, t], H2[:, t], add[:, w], ALU.add).then_inc(s_hd, 1)
            dve.wait_ge(s_sb, len(groups))
            dve.tensor_copy(S.rearrange("p a b -> p (a b)"), banks[6][:, 0:W]).then_inc(s_s, 1)
            dve.wait_ge(s_s, 1)
            step = Count(s_c)

            def do(instruction):
                step.up(instruction)
                dve.wait_ge(s_c, step.now())

            def over(x, n):
                return x.unsqueeze(2).broadcast_to([P, x.shape[1], n])

            g4 = [SB.rearrange("p t (g e) -> p (t g) e", e=4)[:, :, i] for i in range(4)]
            hi1, lo1, hi2, lo2, top, sec, grp, oh = sm[:8]
            one = sm[8][:, 0:NQ]
            two = sm[9][:, 0:NQ]
            do(dve.tensor_tensor(SB, S, vec[:, V_RB:V_RB + EXP].unsqueeze(1).broadcast_to([P, NQ, EXP]), ALU.add))
            do(dve.tensor_tensor(hi1, g4[0], g4[1], ALU.max))
            do(dve.tensor_tensor(lo1, g4[0], g4[1], ALU.min))
            do(dve.tensor_tensor(hi2, g4[2], g4[3], ALU.max))
            do(dve.tensor_tensor(lo2, g4[2], g4[3], ALU.min))
            do(dve.tensor_tensor(top, hi1, hi2, ALU.max))
            do(dve.tensor_tensor(sec, hi1, hi2, ALU.min))
            do(dve.tensor_tensor(lo1, lo1, lo2, ALU.max))
            do(dve.tensor_tensor(sec, sec, lo1, ALU.max))
            do(dve.tensor_tensor(grp, top, sec, ALU.add))
            g3 = grp.rearrange("p (t g) -> p t g", g=4)
            o3 = oh.rearrange("p (t g) -> p t g", g=4)
            do(dve.tensor_reduce(one, g3, AX.X, ALU.max))
            do(dve.tensor_tensor(o3, g3, over(one, 4), ALU.is_equal))
            do(dve.tensor_tensor(o3, o3, desc[:, 0:4].unsqueeze(1).broadcast_to([P, NQ, 4]), ALU.mult))
            do(dve.tensor_reduce(one, o3, AX.X, ALU.max))
            do(dve.tensor_tensor(o3, o3, over(one, 4), ALU.is_equal))
            m4 = oh.unsqueeze(2).broadcast_to([P, NQ * 4, 4])
            sb4 = SB.rearrange("p t (g e) -> p (t g) e", e=4)
            do(dve.tensor_tensor(sb4, sb4, m4, ALU.mult))
            do(dve.tensor_scalar(oh, oh, -NEG, NEG, ALU.mult, ALU.add))
            do(dve.tensor_tensor(sb4, sb4, m4, ALU.add))
            for OH in (OH1, OH2):
                do(dve.tensor_reduce(one, SB, AX.X, ALU.max))
                do(dve.tensor_tensor(OH, SB, over(one, EXP), ALU.is_equal))
                do(dve.tensor_tensor(OH, OH, desc.unsqueeze(1).broadcast_to([P, NQ, EXP]), ALU.mult))
                do(dve.tensor_reduce(one, OH, AX.X, ALU.max))
                do(dve.tensor_tensor(OH, OH, over(one, EXP), ALU.is_equal))
                if OH is OH1:
                    do(dve.scalar_tensor_tensor(SB, OH, 2 * NEG, SB, ALU.mult, ALU.add))
            step.up(dve.tensor_tensor(M, OH1, OH2, ALU.add))
            dve.wait_ge(s_c, step.now())
            dve.memset(ones, 1.0).then_inc(s_pc, 1)
            for j, OH in enumerate((OH1, OH2)):
                do(dve.tensor_tensor(T1, S, OH, ALU.mult))
                do(dve.tensor_reduce((one, two)[j], T1, AX.X, ALU.add))
            do(dve.tensor_tensor(fd, one, two, ALU.add))
            do(dve.reciprocal(fd, fd))
            do(dve.tensor_tensor(s["wts"][:, 0, 0:NQ], one, fd, ALU.mult))
            do(dve.tensor_tensor(s["wts"][:, 1, 0:NQ], two, fd, ALU.mult))
            dve.wait_ge(s_pp, 2)
            do(dve.tensor_copy(RANK.rearrange("p a b -> p (a b)"), banks[6][:, 0:W]))
            do(dve.tensor_copy(TOT.rearrange("p a b -> p (a b)"), banks[7][:, 0:W]))
            do(dve.tensor_copy(cnt, TOT[:, 0]))
            for t in range(1, NQ):
                do(dve.tensor_tensor(RANK[:, t], RANK[:, t], cnt, ALU.add))
                do(dve.tensor_tensor(cnt, cnt, TOT[:, t], ALU.add))
            do(dve.tensor_tensor(cmp, over(cnt, NT), thr.unsqueeze(1).broadcast_to([P, EXP, NT]), ALU.is_gt))
            do(dve.tensor_reduce(nb, cmp, AX.X, ALU.add))
            a, b = cum, cum2
            do(dve.tensor_copy(a, nb))
            for d in (1, 2, 4, 8):
                do(dve.tensor_copy(b[:, 0:d], a[:, 0:d]))
                do(dve.tensor_tensor(b[:, d:EXP], a[:, d:EXP], a[:, 0:EXP - d], ALU.add))
                a, b = b, a
            do(dve.tensor_tensor(base, a, nb, ALU.subtract))
            do(dve.tensor_scalar(base, base, float(P), None, ALU.mult))
            do(dve.tensor_scalar(cnt, nb, 1.0, None, ALU.min))
            do(dve.tensor_tensor(cnt, cnt, blk[:, 0:EXP], ALU.mult))
            do(dve.tensor_reduce(one[:, 0:1], cnt, AX.X, ALU.max))
            do(dve.tensor_tensor(cmpb, a.unsqueeze(1).broadcast_to([P, 48, EXP]), over(blk, EXP), ALU.is_le))
            do(dve.tensor_reduce(be[:, 0:48], cmpb, AX.X, ALU.add))
            do(dve.tensor_tensor(be[:, 0:48], be[:, 0:48], one[:, 0:1].broadcast_to([P, 48]), ALU.min))
            do(dve.tensor_copy(be[:, PLAN_USED:PLAN_USED + 1], a[:, EXP - 1:EXP]))
            do(dve.memset(be[:, PLAN_BEFORE:PLAN], 0.0))
            do(dve.tensor_tensor(cnt, a, a[:, EXP - 1:EXP].broadcast_to([P, EXP]), ALU.is_equal))
            do(dve.tensor_scalar(cnt, cnt, 2.0, None, ALU.mult))
            do(dve.tensor_tensor(be[:, PLAN_BEFORE + 2:PLAN_BEFORE + EXP], a[:, 0:EXP - 2], cnt[:, 0:EXP - 2],
                                 ALU.add))
            do(dve.tensor_copy(s["plan"][:], be[0:1, :]))
            do(dve.tensor_tensor(RANK, RANK, base.unsqueeze(1).broadcast_to([P, NQ, EXP]), ALU.add))
            for j, OH in enumerate((OH1, OH2)):
                do(dve.tensor_tensor(T1, RANK, OH, ALU.mult))
                do(dve.tensor_reduce(fd, T1, AX.X, ALU.add))
                do(dve.tensor_copy(s["dest"][:, j, 0:NQ], fd))
                dve.sem_inc(s_idx, 1)

        @block.gpsimd
        def _(pool):
            for t in range(0, NQ, 2):
                pool.wait_ge(s_bcc, 4 * (t // NTX) + 4)
                pool.wait_ge(s_a, t + 1)
                pool.tensor_tensor(H2[:, t], H2[:, t], add[:, t // NTX], ALU.add).then_inc(s_h, 1)
            pool.wait_ge(s_h, NQ // 2)
            pool.wait_ge(s_hd, NQ // 2)
            for j in range(2):
                pool.wait_ge(s_idx, j + 1)
                for t in range(NQ):
                    pool.indirect_dma_start(
                        out=s["slots"][0:MAX_SLOTS], out_offset=bass.IndirectOffsetOnAxis(
                            s["dest"][:, j, t:t + 1], 0),
                        in_=H2[:, t], in_offset=None).then_inc(s_sent, 16)
            pool.wait_ge(s_sent, 16 * 2 * NQ)


def experts(s, layer, last):
    nc, sem, place, banks, part = s["nc"], s["sem"], s["place"], s["banks"], s["part"]
    MAXB = ((SEQ if last else TOK) * 2 + EXP * (P - 1)) // P
    ROUNDS = (MAXB + 1) // 2
    w13 = place(0, 2, 2 * KD, DE)
    wlo, whi = part(0, 2, 2 * KD, DE), part(16384, 2, 2 * KD, DE)
    w2 = place(32768, 2, DE // P, D)
    at = 40960
    xb = [place(at + i * D, D) for i in range(2)]
    at += 2 * D
    xhi, xlo = [part(at + i * D, KD, P) for i in range(2)], [part(at + (2 + i) * D, KD, P) for i in range(2)]
    xraw = [place(at + (2 + i) * D, KD, P) for i in range(2)]
    at += 4 * D
    yb = [place(at + i * D, D) for i in range(2)]
    at += 2 * D
    sl, h3, gl, gt = place(at, DE), place(at + DE, DE), place(at + 2 * DE, DE), place(at + 3 * DE, 4, P)
    plan = s["plan"]
    ident = s["ident"]
    PIECES = 4
    PK = 2 * KD // PIECES
    s_w13 = [[sem(f"w13_loaded_{b}_{i}") for i in range(PIECES)] for b in range(2)]
    s_w2 = [sem("w2_loaded_even"), sem("w2_loaded_odd")]
    s_whi, s_split = sem("w13_hi"), sem("w13_split")
    s_xb, s_yo = [sem("slots_loaded_even"), sem("slots_loaded_odd")], [sem("y_stored_even"), sem("y_stored_odd")]
    s_tx, s_xh, s_xl, s_h1, s_h3, s_sl, s_g = sem("slots_turned"), sem("slots_hi"), sem("slots_lo"), \
        sem("w1_product"), sem("w3_product"), sem("silu"), sem("gated")
    s_tg, s_gc, s_3c, s_done = sem("gated_turned"), sem("gated_copied"), sem("w3_product_copied"), sem("stores_done")
    s_y, s_yc, s_sp = sem("w2_product"), sem("y_copied"), sem("loads_passed")

    def rounds(eng, body):
        used = eng.value_load(plan[0:1, PLAN_USED:PLAN_USED + 1], min_val=1, max_val=MAXB)
        with eng.Fori(0, ROUNDS) as r:
            with eng.If(used > r * 2):
                body(r)
        return used

    with nc.Block() as block:
        @block.sync
        def _(sp):
            s["clear_last"](sp)
            for b in range(2):
                sp.sem_inc(s_w2[b], 16)
            with sp.Fori(0, EXP - 1, 2) as e:
                for b in range(2):
                    before = sp.value_load(plan[0:1, bass.ds(e + (PLAN_BEFORE + b), 1)], min_val=0, max_val=MAXB + 2)
                    for i in range(PIECES):
                        sp.wait_ge(s_split, e * PIECES + (b * PIECES + i + 1))
                        apart(sp, s_sp)
                        if i % (PIECES // 2) == 0:
                            sp.wait_ge((s_h1, s_h3)[2 * i // PIECES], before + 1)
                            apart(sp, s_sp)
                        sp.dma_start(w13[:, b, i * PK:(i + 1) * PK],
                                     s["a"]["w13"][layer, bass.ds(e + b, 1), :, i * PK:(i + 1) * PK]
                                     .rearrange("o p k n -> p (o k) n")).then_inc(s_w13[b][i], 16)
                    sp.wait_ge(s_w2[b], e * 8 + 16)
                    sp.wait_ge(s_y, before * 2 + 2)
                    sp.dma_start(w2[:, b], s["a"]["w2"][layer, bass.ds(e + b, 1)]
                                 .rearrange("o p k n -> p (o k) n")).then_inc(s_w2[b], 16)
            for b in range(2):
                for i in range(PIECES):
                    sp.wait_ge(s_w13[b][i], 16 * (EXP // 2))
                sp.wait_ge(s_w2[b], 16 * (EXP // 2 + 1))

        @block.tensor
        def _(pe):
            pe.sem_inc(s_h1, 1)
            pe.sem_inc(s_h3, 1)
            pe.sem_inc(s_y, 2)

            def turn_slots(half, b, n):
                if half == 0:
                    pe.wait_ge(s_xb[b], n // 2 * 16 + 16)
                pe.wait_ge(s_xh, n * 4 + (2 * half + 2))
                for j in range(4):
                    mm = pe.transpose(banks[half][:, j * P:(j + 1) * P],
                                      xb[b][:, (4 * half + j) * P:(4 * half + j + 1) * P], ident[:])
                mm.then_inc(s_tx, 1)

            def up(a, b, e, slot):
                for k in range(KD):
                    if k % PK == 0:
                        pe.wait_ge(s_split, e * PIECES + ((a * KD + k) // PK + 2 * PIECES + 1))
                    mm = split_product(pe, banks[2 + a][:], (xhi[b][:, k, :], xlo[b][:, k, :]),
                                       [w[:, bass.ds(slot, 1), a * KD + k, :].rearrange("p o n -> p (o n)")
                                        for w in (whi, wlo)], k == 0, k == KD - 1)
                mm.then_inc((s_h1, s_h3)[a], 1)

            for n in range(2):
                turn_slots(0, n, n)
                turn_slots(1, n, n)
            first = pe.value_load(plan[0:1, 0:1], min_val=0, max_val=EXP - 1)
            slot = pe.snap(first % 2, min_val=0, max_val=1)
            pe.wait_ge(s_xl, 2)
            pe.wait_ge(s_sl, 1)
            up(0, 0, first, slot)
            pe.wait_ge(s_3c, 1)
            up(1, 0, first, slot)

            def body(r):
                experts_of = [pe.value_load(plan[0:1, bass.ds(r * 2 + b, 1)], min_val=0, max_val=EXP - 1)
                              for b in range(3)]
                slots = [pe.snap(e % 2, min_val=0, max_val=1) for e in experts_of]
                for b in range(2):
                    e = experts_of[b]
                    evens, odds = pe.snap(e // 2 * 16 + 32), pe.snap((e + 1) // 2 * 16 + 16)
                    pe.wait_ge(s_xl, r * 4 + (2 * b + 4))
                    pe.wait_ge(s_sl, r * 2 + (b + 2))
                    up(0, 1 - b, experts_of[b + 1], slots[b + 1])
                    turn_slots(0, b, r * 2 + (b + 2))
                    pe.wait_ge(s_g, r * 2 + (b + 2))
                    pe.wait_ge(s_gc, r * 2 + (b + 1))
                    for j in range(4):
                        mm = pe.transpose(banks[4][:, j * P:(j + 1) * P], gl[:, j * P:(j + 1) * P], ident[:])
                    mm.then_inc(s_tg, 1)
                    pe.wait_ge(s_3c, r * 2 + (b + 2))
                    up(1, 1 - b, experts_of[b + 1], slots[b + 1])
                    turn_slots(1, b, r * 2 + (b + 2))
                    pe.wait_ge(s_w2[0], evens)
                    pe.wait_ge(s_w2[1], odds)
                    pe.wait_ge(s_gc, r * 2 + (b + 2))
                    for h in range(2):
                        pe.wait_ge(s_yc, r * 4 + (2 * b + h + 1))
                        for k in range(4):
                            mm = pe.matmul(banks[6 + h][:], gt[:, k, :],
                                           w2[:, bass.ds(slots[b], 1), k, h * 512:(h + 1) * 512]
                                           .rearrange("p o n -> p (o n)"), start=k == 0, stop=k == 3)
                        mm.then_inc(s_y, 1)
            used = rounds(pe, body)
            pe.wait_ge(s_h1, (used + 1) // 2 * 2 + 2)
            pe.wait_ge(s_h3, (used + 1) // 2 * 2 + 2)
            pe.wait_ge(s_y, (used + 1) // 2 * 4 + 2)
            pe.sem_inc(s_h1, 1)
            pe.sem_inc(s_h3, 1)
            pe.sem_inc(s_y, 4)

        @block.scalar
        def _(act):
            for b in range(2):
                act.dma_start(xb[b], s["slots"][b * P:(b + 1) * P]).then_inc(s_xb[b], 16)
                act.sem_inc(s_yo[b], 16)
            act.sem_inc(s_sl, 1)
            act.sem_inc(s_gc, 1)
            act.sem_inc(s_3c, 1)
            act.sem_inc(s_yc, 2)
            act.sem_inc(s_xh, 4)

            def copy_turned(half, b, n):
                act.wait_ge(s_tx, n * 2 + (half + 1))
                for to in (xraw[b], xhi[b]):
                    act.activation(to[:, 4 * half:4 * half + 4].rearrange("p a b -> p (a b)"), banks[half][:], ACT.Copy)\
                        .then_inc(s_xh, 1)

            def silu(n):
                act.wait_ge(s_h1, n + 2)
                act.wait_ge(s_g, n + 1)
                act.activation(sl, banks[2][:], ACT.Silu).then_inc(s_sl, 1)

            def copy_h3(n):
                act.wait_ge(s_h3, n + 2)
                act.wait_ge(s_g, n + 1)
                act.activation(h3, banks[3][:], ACT.Copy).then_inc(s_3c, 1)

            for n in range(2):
                copy_turned(0, n, n)
                copy_turned(1, n, n)
                act.dma_start(xb[n], s["slots"][(n + 2) * P:(n + 3) * P]).then_inc(s_xb[n], 16)
            silu(0)
            copy_h3(0)

            def body(r):
                for b in range(2):
                    silu(r * 2 + (b + 1))
                    copy_turned(0, b, r * 2 + (b + 2))
                    act.wait_ge(s_tg, r * 2 + (b + 1))
                    act.activation(gt.rearrange("p a b -> p (a b)"), banks[4][:], ACT.Copy).then_inc(s_gc, 1)
                    copy_h3(r * 2 + (b + 1))
                    copy_turned(1, b, r * 2 + (b + 2))
                    act.dma_start(xb[b], s["slots"][bass.ds(r * (2 * P) + (b + 4) * P, P)]).then_inc(s_xb[b], 16)
                    act.wait_ge(s_yo[b], r * 16 + 16)
                    for h in range(2):
                        act.wait_ge(s_y, r * 4 + (2 * b + h + 3))
                        act.activation(yb[b][:, h * 512:(h + 1) * 512], banks[6 + h][:], ACT.Copy).then_inc(s_yc, 1)
                    act.wait_ge(s_yc, r * 4 + (2 * b + 4))
                    act.dma_start(s["slots"][bass.ds(r * (2 * P) + b * P, P)], yb[b]).then_inc(s_yo[b], 16)
            used = rounds(act, body)
            for b in range(2):
                act.wait_ge(s_yo[b], ((used + 1) // 2) * 16 + 16)
                act.wait_ge(s_xb[b], ((used + 1) // 2) * 16 + 32)
            apart(act, s_done)

        @block.vector
        def _(dve):
            dve.sem_inc(s_split, 2 * PIECES)
            with dve.Fori(0, EXP - 1, 2) as e:
                for b in range(2):
                    for i in range(PIECES):
                        at = slice(i * PK, (i + 1) * PK)
                        dve.wait_ge(s_w13[b][i], e * 8 + 16)
                        dve.tensor_copy(whi[:, b, at], w13[:, b, at]).then_inc(s_whi, 1)
                        dve.wait_ge(s_whi, e * PIECES + (b * PIECES + i + 1))
                        dve.tensor_tensor(wlo[:, b, at], w13[:, b, at], whi[:, b, at].bitcast(F32), ALU.subtract)\
                            .then_inc(s_split, 1)
            dve.wait_ge(s_split, (EXP + 2) * PIECES)

        @block.gpsimd
        def _(pool):
            pool.sem_inc(s_g, 1)

            def leave_turned(half, b, n):
                pool.wait_ge(s_xh, n * 4 + (2 * half + 6))
                at = slice(4 * half, 4 * half + 4)
                pool.tensor_tensor(xlo[b][:, at], xraw[b][:, at], xhi[b][:, at].bitcast(F32), ALU.subtract)\
                    .then_inc(s_xl, 1)

            def gate(n):
                pool.wait_ge(s_sl, n + 2)
                pool.wait_ge(s_3c, n + 2)
                pool.tensor_tensor(gl, h3, sl, ALU.mult).then_inc(s_g, 1)

            for n in range(2):
                leave_turned(0, n, n)
                leave_turned(1, n, n)
            gate(0)

            def body(r):
                for b in range(2):
                    leave_turned(0, b, r * 2 + (b + 2))
                    gate(r * 2 + (b + 1))
                    leave_turned(1, b, r * 2 + (b + 2))
            rounds(pool, body)


def combine(s, layer, last):
    nc, sem, place, mod, banks = s["nc"], s["sem"], s["place"], s["mod"], s["banks"]
    X = place(A_X, NT, D)
    NQ = NTX if last else NT
    Y = [place(A_H + t * 2 * D, 2, D) for t in range(NQ)]
    at = A_H + NT * 2 * D
    g2 = place(at, 2, D)
    t1 = [place(at + (2 + i) * D, D) for i in range(3)]
    junk = place(at + 5 * D, D)
    wts = s["wts"]
    s_y = [s["pool_dma_sem"](f"y_rows_{i}") for i in range(NQ)]
    s_xl = sem("x_loaded")
    s_b, s_g, s_t1, s_t2, s_t3, s_x, s_out, s_sq = sem("g2_rows"), sem("g2_copied"), sem("first_weighted"), \
        sem("both_weighted"), sem("gated_by_g2"), sem("x_done"), sem("x_rows_stored"), sem("squares")
    with nc.Block() as block:
        @block.tensor
        def _(pe):
            for w in range(2):
                for h in range(2):
                    cols = [mod[:, layer, 5 * KD + 4 * h + j, w:w + 1] for j in range(4)]
                    broadcast_columns(s, pe, cols, banks[2 * w + h]).then_inc(s_b, 1)

        @block.gpsimd
        def _(pool):
            for t in range(NQ):
                for j in range(2):
                    pool.indirect_dma_start(
                        out=Y[t][:, j], out_offset=None, in_=s["slots"][0:MAX_SLOTS],
                        in_offset=bass.IndirectOffsetOnAxis(s["dest"][:, j, t:t + 1], 0)).then_inc(s_y[t], 16)
            for t in range(NQ):
                pool.wait_ge(s_y[t], 32)

        @block.scalar
        def _(act):
            for w in range(2):
                for h in range(2):
                    act.wait_ge(s_b, 2 * w + h + 1)
                    act.activation(g2[:, w, h * 512:(h + 1) * 512], banks[2 * w + h][:], ACT.Copy).then_inc(s_g, 1)

            def square(t):
                act.wait_ge(s_x, t + 1)
                if t:
                    act.wait_ge(s_sq, t)
                act.activation(junk, X[:, t], ACT.Square, accum_out=s["squares"][:, t:t + 1]).then_inc(s_sq, 1)

            for t in range(NQ):
                act.wait_ge(s_y[t], 32)
                if t >= 3:
                    act.wait_ge(s_x, t - 2)
                act.activation(t1[t % 3], Y[t][:, 0], ACT.Copy, scale=wts[:, 0, t:t + 1]).then_inc(s_t1, 1)
                if t >= 3 and not last:
                    square(t - 3)
            if not last:
                for t in range(NQ - 3, NQ):
                    square(t)
                act.wait_ge(s_sq, NQ)

        @block.vector
        def _(dve):
            dve.wait_ge(s_g, 4)
            dve.wait_ge(s_xl, 16)
            for t in range(NQ):
                dve.wait_ge(s_t1, t + 1)
                dve.wait_ge(s_y[t], 32)
                dve.scalar_tensor_tensor(t1[t % 3], Y[t][:, 1], wts[:, 1, t:t + 1], t1[t % 3], ALU.mult,
                                         ALU.add).then_inc(s_t2, 1)
                dve.wait_ge(s_t2, t + 1)
                dve.tensor_tensor(t1[t % 3], t1[t % 3], g2[:, t // NTX], ALU.mult).then_inc(s_t3, 1)
                dve.wait_ge(s_t3, t + 1)
                dve.tensor_tensor(X[:, t], X[:, t], t1[t % 3], ALU.add).then_inc(s_x, 1)

        @block.sync
        def _(sp):
            s["clear_last"](sp)
            sp.dma_start(X[:, 0:NQ], s["x_rows"][0:NQ * P].rearrange("(t p) d -> p t d", p=P)).then_inc(s_xl, 16)
            to = s["out"][0] if last else s["x_rows"]
            for t in range(NQ):
                sp.wait_ge(s_x, t + 1)
                sp.dma_start(to[t * P:(t + 1) * P], X[:, t]).then_inc(s_out, 16)
            sp.wait_ge(s_out, 16 * NQ)



def _constants():
    c = np.zeros((P, C_TOTAL), np.float32)
    c[:, C_ID:C_ID + P] = np.eye(P)
    c[:, C_TRI:C_TRI + P] = np.triu(np.ones((P, P)), 1)
    col = np.arange(GRID_W)
    first = np.clip(col - WIN_C // 2, 0, GRID_W - WIN_C)
    inside = (col[None] >= first[:, None]) & (col[None] < first[:, None] + WIN_C)
    c[:, C_MASK:C_MASK + GRID_W] = np.tile(np.where(inside, 0.0, NEG), (2, 1))
    angle = 2 * np.pi * (np.outer(np.arange(64), np.arange(64)) % 64) / 64
    for i, length in enumerate((SEQ, CTX)):
        for j, m in enumerate((np.cos(angle), -np.sin(angle))):
            m = m / np.sqrt(length * 64)
            at = C_DFT + (2 * i + j) * P
            c[0:64, at:at + 64] = m
            c[64:128, at + 64:at + 128] = m
    angle = 2 * np.pi * (np.outer(np.arange(CTX), np.arange(CTX)) % CTX) / CTX
    d = np.stack([np.cos(angle), np.sin(angle)]).reshape(2, 2, P, CTX).transpose(2, 1, 0, 3)
    c[:, C_DCTX:C_DCTX + 4 * CTX] = d.reshape(P, 4 * CTX)
    c[:, C_THR:C_THR + NT] = P * np.arange(NT)
    c[:, C_BLK:C_BLK + 48] = np.arange(48)
    c[:, C_DESC:C_DESC + EXP] = 32 - np.arange(EXP)
    c[:, C_SEL:C_SEL + 2] = np.arange(P)[:, None] % 32 == np.arange(2)
    c[:, C_ALT:C_ALT + 2] = 1 - 2 * (np.arange(P)[:, None] % 2)
    t = np.arange(SEQ)
    inv = np.power(np.float32(10000.0), -np.arange(HD // 4, dtype=np.float32) / np.float32(HD // 4))
    ang = np.concatenate([(t // GRID_W).astype(np.float32)[:, None] * inv,
                          (t % GRID_W).astype(np.float32)[:, None] * inv], 1).astype(np.float32)
    cos, sin = np.cos(ang), np.sin(ang)
    trig = np.stack([np.concatenate([cos, cos], 1), np.concatenate([-sin, sin], 1)])
    trig = trig.reshape(2, NTX, P, HD).transpose(2, 0, 1, 3).astype(np.float32)
    angle = 2 * np.pi * (np.outer(np.arange(SEQ), np.arange(SEQ // 2)) % SEQ) / SEQ
    dft = np.stack([np.cos(angle), np.sin(angle)]).reshape(2, NTX, P, SEQ // 2).transpose(0, 2, 1, 3)
    return c, trig, dft.astype(np.float32)


def kernel(**inputs):
    import concourse.bacc as bacc
    from concourse.bass_utils import run_bass_kernel_spmd as run

    def arr(name):
        return np.asarray(inputs[name])

    def columns(v):
        return v.reshape(-1, P).T

    vectors = np.zeros((P, V_TOTAL), np.float32)
    vectors[:, V_C:V_C + 2 * KD:2] = columns(arr("c")[0])
    vectors[:, V_C + 1:V_C + 2 * KD:2] = columns(arr("c_ctx"))
    for layer in range(DEPTH):
        vectors[:, V_ADAB + layer * 48:V_ADAB + (layer + 1) * 48] = columns(arr("ada_b")[layer])
        vectors[:, V_N1 + layer * KD:V_N1 + (layer + 1) * KD] = columns(arr("norm1_g")[layer])
        cw = arr("conv_w")[layer].reshape(3, 2, P).transpose(2, 1, 0)
        vectors[:, V_CONV + layer * 6:V_CONV + (layer + 1) * 6] = cw.reshape(P, 6)
        for j, name in enumerate(("qn_g", "kn_g")):
            g = arr(name)[layer]
            at = V_QG + layer * 4 * HD + 2 * j * HD
            vectors[:, at:at + HD] = g
            vectors[:, at + HD:at + HD + 32] = g[32:]
            vectors[:, at + HD + 32:at + 2 * HD] = g[:32]
    vectors[:, V_RB:V_RB + EXP] = arr("router_b")
    consts, trig, dft = _constants()
    w_in = arr("w_in").reshape(DEPTH, KD, P, -1).transpose(0, 2, 1, 3)
    rows = [w_in[:, :, :, a:b].reshape(DEPTH, P, -1) for a, b in zip(KS[:4], KS[1:5])]
    w_conv = w_in[:, :, :, KS[4]:KS[5]].reshape(DEPTH, P, KD, 3, 2, P).transpose(0, 1, 4, 2, 3, 5)
    gates = w_in[:, :, :, KS[5]:].reshape(DEPTH, P, KD, 3, KD, P).transpose(0, 4, 1, 3, 2, 5)
    parts = []
    for q, (name, k) in enumerate((("w_f", 2), ("w_na", 4), ("w_cv", 2))):
        parts.append(gates[:, :, :, q])
        parts.append(arr(name).reshape(DEPTH, k, P, KD, P).transpose(0, 3, 2, 1, 4))
    rpb = np.zeros((DEPTH, HEADS, RPB_R, RPB_PAD), np.float32)
    rpb[..., GRID_W - WIN_C:GRID_W + WIN_C - 1] = arr("rpb")[..., ::-1]
    w13 = np.stack([arr(n).reshape(DEPTH, EXP, KD, P, DE).transpose(0, 1, 3, 2, 4) for n in ("w1", "w3")], 3)
    data = dict(
        x=arr("x"), ctx=arr("ctx"), vectors=vectors, consts=consts, trig=trig, dft=dft,
        ada_w=arr("ada_w").reshape(DEPTH, KD, P, 12, 512).transpose(0, 3, 2, 1, 4),
        w_rows=np.concatenate(rows, 2), w_conv=w_conv.reshape(DEPTH, P, 2, KD, 3 * P),
        w_gates=np.concatenate(parts, 3), rpb=rpb,
        w_o=arr("w_o").reshape(DEPTH, KD, P, 2, 512).transpose(0, 3, 2, 1, 4),
        norm2_rows=np.repeat(arr("norm2_g")[:, None], P, 1),
        router_w=arr("router_w").reshape(KD, P, EXP).transpose(1, 0, 2),
        w13=w13.reshape(DEPTH, EXP, P, 2 * KD, DE), w2=arr("w2").reshape(DEPTH, EXP, DE // P, P, D).transpose(0, 1, 3, 2, 4),
    )
    nc = bacc.Bacc("TRN2", target_bir_lowering=False, num_devices=1)
    feeds, aps = {}, {}
    for name, v in data.items():
        v = np.ascontiguousarray(v)
        feeds[f"in_{name}"] = v
        aps[name] = nc.dram_tensor(f"in_{name}", v.shape, mybir.dt.from_np(v.dtype), kind="ExternalInput").ap()
    out = nc.dram_tensor("out_x", (1, SEQ, D), F32, kind="ExternalOutput").ap()
    hybrid_backbone(nc, aps, out)
    return run(nc, [feeds], core_ids=[0]).results[0]["out_x"]
```
